# Optimizing a Trainium2 kernel written in Bass

```python
import jax, jax.numpy as jnp
from jax import lax
import numpy as np

D_MODEL = 1024
BATCH = 1
SEQ = 512
DEPTH = 1

D_CONV = D_MODEL // 2
CONV_W = 3
D_RWKV = D_MODEL // 2
HEAD_SIZE = 64
N_HEADS = D_RWKV // HEAD_SIZE
DECAY_LORA = 64
ICLR_LORA = 64
GATE_LORA = 128
GN_EPS = 64e-5
D_FF = 2816
RMS_EPS = 1e-6

COLS_A = 3 * D_CONV
COLS_B = 3 * D_RWKV + DECAY_LORA + ICLR_LORA + GATE_LORA
COLS_G = 2 * D_MODEL
COLS_IN = COLS_A + COLS_B + COLS_G
SPLIT_B = [D_RWKV, 2 * D_RWKV, 3 * D_RWKV, 3 * D_RWKV + DECAY_LORA, 3 * D_RWKV + DECAY_LORA + ICLR_LORA]


def rms_norm(x, g):
    xf = x.astype(jnp.float32)
    y = xf * lax.rsqrt(jnp.mean(xf * xf, axis=-1, keepdims=True) + RMS_EPS)
    return (y * g.astype(jnp.float32)).astype(x.dtype)

def swiglu(x, w_gate, w_up, w_down):
    return (jax.nn.silu(x @ w_gate) * (x @ w_up)) @ w_down

def token_shift(p):
    return jnp.pad(p, ((0, 0), (1, 0), (0, 0)))[:, :-1]

def causal_dwconv(u, w):
    return lax.conv_general_dilated(
        u, w[:, None, :].astype(u.dtype), window_strides=(1,),
        padding=[(CONV_W - 1, 0)], dimension_numbers=("NWC", "WIO", "NWC"),
        feature_group_count=u.shape[-1])

def wkv7_scan(r, w, k, v, a, b):
    bsz, _, h, n = r.shape

    def step(S, inp):
        r_t, w_t, k_t, v_t, a_t, b_t = inp
        sa = jnp.einsum("bhvk,bhk->bhv", S, a_t)
        S = S * w_t[:, :, None, :] + sa[..., None] * b_t[:, :, None, :] + v_t[..., None] * k_t[:, :, None, :]
        y = jnp.einsum("bhvk,bhk->bhv", S, r_t)
        return S, y

    xs = tuple(jnp.moveaxis(t, 1, 0) for t in (r, w, k, v, a, b))
    S0 = jnp.zeros((bsz, h, n, n), jnp.float32)
    _, ys = lax.scan(step, S0, xs)
    return jnp.moveaxis(ys, 0, 1)

def first_inputs(seed: int = 0) -> dict:
    key = jax.random.key(seed)
    ks = iter(jax.random.split(key, 40))
    f32 = jnp.float32

    def nrm(shape, scale):
        return jax.random.normal(next(ks), shape, f32) * scale

    def gain(shape):
        return 1.0 + 0.01 * jax.random.normal(next(ks), shape, f32)

    L = DEPTH
    return {
        "x": jax.random.normal(next(ks), (BATCH, SEQ, D_MODEL), f32),
        "ffn1_norm": gain((L, D_MODEL)),
        "ffn1_w_gate": nrm((L, D_MODEL, D_FF), D_MODEL ** -0.5),
        "ffn1_w_up": nrm((L, D_MODEL, D_FF), D_MODEL ** -0.5),
        "ffn1_w_down": nrm((L, D_FF, D_MODEL), D_FF ** -0.5),
        "mix_norm": gain((L, D_MODEL)),
        "w_in": nrm((L, D_MODEL, COLS_IN), D_MODEL ** -0.5),
        "conv_w": nrm((L, CONV_W, D_CONV), CONV_W ** -0.5),
        "w_out_a": nrm((L, D_CONV, D_MODEL), D_CONV ** -0.5),
        "mu_b": jax.random.uniform(next(ks), (L, COLS_B), f32),
        "w0": nrm((L, D_RWKV), 0.5) - 0.5,
        "w_decay_up": nrm((L, DECAY_LORA, D_RWKV), 0.5 * DECAY_LORA ** -0.5),
        "a0": nrm((L, D_RWKV), 0.1),
        "w_iclr_up": nrm((L, ICLR_LORA, D_RWKV), ICLR_LORA ** -0.5),
        "w_gate_up": nrm((L, GATE_LORA, D_RWKV), GATE_LORA ** -0.5),
        "k_k": 0.85 + nrm((L, D_RWKV), 0.05),
        "k_a": 1.0 + nrm((L, D_RWKV), 0.05),
        "r_k": nrm((L, N_HEADS, HEAD_SIZE), 0.1),
        "ln_x_w": gain((L, D_RWKV)),
        "ln_x_b": nrm((L, D_RWKV), 0.01),
        "w_out_b": nrm((L, D_RWKV, D_MODEL), D_RWKV ** -0.5),
        "w_o": nrm((L, D_MODEL, D_MODEL), D_MODEL ** -0.5),
        "ffn2_norm": gain((L, D_MODEL)),
        "ffn2_w_gate": nrm((L, D_MODEL, D_FF), D_MODEL ** -0.5),
        "ffn2_w_up": nrm((L, D_MODEL, D_FF), D_MODEL ** -0.5),
        "ffn2_w_down": nrm((L, D_FF, D_MODEL), D_FF ** -0.5),
        "final_norm": gain((D_MODEL,)),
    }

def token_mixer(h, w_in, conv_w, w_out_a, mu_b, w0, w_decay_up, a0, w_iclr_up,
                w_gate_up, k_k, k_a, r_k, ln_x_w, ln_x_b, w_out_b, w_o):
    bsz, t, _ = h.shape
    f32 = jnp.float32
    p = h @ w_in
    pa, pb, pg = jnp.split(p, [COLS_A, COLS_A + COLS_B], axis=-1)

    b_gate, c_gate, u = jnp.split(pa, 3, axis=-1)
    y_a = (b_gate * causal_dwconv(c_gate * u, conv_w)) @ w_out_a

    pb = pb + (token_shift(pb) - pb) * mu_b
    r, k, v, xw, xa, xg = jnp.split(pb, SPLIT_B, axis=-1)
    w_log = -jax.nn.softplus(-(w0 + jnp.tanh(xw) @ w_decay_up)) - 0.5
    decay = jnp.exp(-jnp.exp(w_log.astype(f32)))
    iclr = jax.nn.sigmoid(a0 + xa @ w_iclr_up)
    g = jax.nn.sigmoid(xg) @ w_gate_up

    def heads(z):
        return z.astype(f32).reshape(bsz, t, N_HEADS, HEAD_SIZE)

    kk = heads(k * k_k)
    kk = kk / jnp.maximum(jnp.sqrt(jnp.sum(kk * kk, axis=-1, keepdims=True)), 1e-12)
    k = k * (1.0 + (iclr - 1.0) * k_a)
    rh, kh, vh, ah = heads(r), heads(k), heads(v), heads(iclr)
    y = wkv7_scan(rh, heads(decay), kh, vh, -kk, kk * ah)

    mu = jnp.mean(y, axis=-1, keepdims=True)
    var = jnp.mean(jnp.square(y - mu), axis=-1, keepdims=True)
    y = (y - mu) * lax.rsqrt(var + GN_EPS)
    y = (y * ln_x_w.astype(f32).reshape(N_HEADS, HEAD_SIZE)
         + ln_x_b.astype(f32).reshape(N_HEADS, HEAD_SIZE))
    y = y + jnp.sum(rh * kh * r_k.astype(f32), axis=-1, keepdims=True) * vh
    y = y.reshape(bsz, t, D_RWKV).astype(h.dtype)
    y_b = (y * g) @ w_out_b

    g_a, g_b = jnp.split(pg, 2, axis=-1)
    merged = jax.nn.sigmoid(g_a) * y_a + jax.nn.sigmoid(g_b) * y_b
    return merged @ w_o

def first_block(x, ffn1_norm, ffn1_w_gate, ffn1_w_up, ffn1_w_down, mix_norm, w_in,
              conv_w, w_out_a, mu_b, w0, w_decay_up, a0, w_iclr_up, w_gate_up,
              k_k, k_a, r_k, ln_x_w, ln_x_b, w_out_b, w_o, ffn2_norm,
              ffn2_w_gate, ffn2_w_up, ffn2_w_down, final_norm):
    for l in range(DEPTH):
        x = x + 0.5 * swiglu(rms_norm(x, ffn1_norm[l]), ffn1_w_gate[l], ffn1_w_up[l], ffn1_w_down[l])
        x = x + token_mixer(rms_norm(x, mix_norm[l]), w_in[l], conv_w[l], w_out_a[l], mu_b[l],
                            w0[l], w_decay_up[l], a0[l], w_iclr_up[l], w_gate_up[l],
                            k_k[l], k_a[l], r_k[l], ln_x_w[l], ln_x_b[l], w_out_b[l], w_o[l])
        x = x + 0.5 * swiglu(rms_norm(x, ffn2_norm[l]), ffn2_w_gate[l], ffn2_w_up[l], ffn2_w_down[l])
    return rms_norm(x, final_norm)


_first_inputs = first_inputs


def first_inputs(seed=0):
    import zlib

    import numpy as np

    out = dict(_first_inputs(seed))
    spreads = {}
    factors = {'ffn1_norm': 8.0,
     'mix_norm': 5.644,
     'w_decay_up': 27.656,
     'a0': 5.055,
     'k_k': 64.0,
     'k_a': 3.816,
     'ln_x_w': 64.0,
     'ln_x_b': 64.0,
     'ffn2_norm': 64.0,
     'final_norm': 31.304,
     'w0': 8.0}
    for name, (base, spread) in spreads.items():
        noise = np.random.default_rng([zlib.crc32(name.encode()), seed]).standard_normal(out[name].shape)
        drawn = base * np.exp(spread * noise) if base else spread * noise
        out[name] = __import__('jax').numpy.asarray(drawn.astype(out[name].dtype))
    for name, factor in factors.items():
        out[name] = (out[name] * factor).astype(out[name].dtype)
    return out


_narrow_inputs = first_inputs


def first_inputs(seed=0):

    out = dict(_narrow_inputs(seed))
    wider = {'k_k': 12.0, 'ln_x_w': 12.0, 'ln_x_b': 12.0, 'ffn2_norm': 4.5, 'final_norm': 6.3}
    for name, times in wider.items():
        mean = out[name].mean()
        out[name] = (mean + times * (out[name] - mean)).astype(out[name].dtype)
    return out


DEPTH_2 = 2

GRID_W = 64
MIX_WIDTH = 2 * D_MODEL
FOURIER_WIDTH = MIX_WIDTH // 2
N_FOURIER_GROUPS = 4
FOURIER_GROUP = FOURIER_WIDTH // N_FOURIER_GROUPS
ATTN_WIDTH = MIX_WIDTH - FOURIER_WIDTH
HEAD_DIM = 128
N_Q_HEADS = ATTN_WIDTH // HEAD_DIM
N_KV_HEADS = 2
Q_PER_KV = N_Q_HEADS // N_KV_HEADS
KV_WIDTH = N_KV_HEADS * HEAD_DIM
Q_BLOCK = 128
ROPE_THETA = 10000.0
ROPE_AXIS_DIM = HEAD_DIM // 2
RNN_WIDTH = MIX_WIDTH
N_RNN_BLOCKS = 16
RNN_BLOCK = RNN_WIDTH // N_RNN_BLOCKS
CONV_WIDTH = 4
CONV_LEFT = 2
RG_LRU_C = 8.0
NORM_EPS = 1e-6
EVEN_IN_WIDTH = 2 * FOURIER_WIDTH + ATTN_WIDTH + 2 * KV_WIDTH + ATTN_WIDTH
EVEN_SPLITS = (FOURIER_WIDTH,
               2 * FOURIER_WIDTH,
               2 * FOURIER_WIDTH + ATTN_WIDTH,
               2 * FOURIER_WIDTH + ATTN_WIDTH + KV_WIDTH,
               2 * FOURIER_WIDTH + ATTN_WIDTH + 2 * KV_WIDTH)


def rms_norm_2(x, g):
    xf = x.astype(jnp.float32)
    y = xf * lax.rsqrt(jnp.mean(xf * xf, axis=-1, keepdims=True) + NORM_EPS)
    return (y * g.astype(jnp.float32)).astype(x.dtype)

def axial_rope_tables(seq_len):
    rows = seq_len // GRID_W
    row = jnp.broadcast_to(jnp.arange(rows)[:, None], (rows, GRID_W)).reshape(-1).astype(jnp.float32)
    col = jnp.broadcast_to(jnp.arange(GRID_W)[None, :], (rows, GRID_W)).reshape(-1).astype(jnp.float32)
    inv_freq = ROPE_THETA ** (-jnp.arange(0, ROPE_AXIS_DIM, 2, dtype=jnp.float32) / ROPE_AXIS_DIM)
    ang_r = row[:, None] * inv_freq[None, :]
    ang_c = col[:, None] * inv_freq[None, :]
    return (jnp.cos(ang_r), jnp.sin(ang_r), jnp.cos(ang_c), jnp.sin(ang_c))

def rope_half(x, cos, sin):
    x1, x2 = jnp.split(x, 2, axis=-1)
    c = cos[:, None, :]
    s = sin[:, None, :]
    return jnp.concatenate([x1 * c - x2 * s, x1 * s + x2 * c], axis=-1)

def axial_rope(x, tables):
    cos_r, sin_r, cos_c, sin_c = tables
    xf = x.astype(jnp.float32)
    x_row, x_col = jnp.split(xf, 2, axis=-1)
    out = jnp.concatenate([rope_half(x_row, cos_r, sin_r), rope_half(x_col, cos_c, sin_c)], axis=-1)
    return out.astype(x.dtype)

def blocked_attention(q, k, v):
    b, s = q.shape[0], q.shape[1]
    n_blocks = s // Q_BLOCK
    qb = q.reshape(b, n_blocks, Q_BLOCK, N_KV_HEADS, Q_PER_KV, HEAD_DIM).transpose(1, 0, 2, 3, 4, 5)
    scale = HEAD_DIM ** -0.5

    def one_block(q_blk):
        scores = jnp.einsum('bqhgd,bkhd->bhgqk', q_blk, k,
                            preferred_element_type=jnp.float32) * scale
        probs = jax.nn.softmax(scores, axis=-1).astype(v.dtype)
        return jnp.einsum('bhgqk,bkhd->bqhgd', probs, v)

    out = lax.map(one_block, qb)
    return out.transpose(1, 0, 2, 3, 4, 5).reshape(b, s, N_Q_HEADS * HEAD_DIM)

def fourier_attention_layer(x, norm_g, w_in, fourier_w, q_gain, k_gain, w_out, rope):
    b, s, _ = x.shape
    h = rms_norm_2(x, norm_g)
    proj = h @ w_in
    f_in, f_gate, q, k, v, a_gate = jnp.split(proj, EVEN_SPLITS, axis=-1)
    fg = f_in.astype(jnp.float32).reshape(b, s, N_FOURIER_GROUPS, FOURIER_GROUP)
    fmix = jnp.fft.fftn(fg, axes=(1, 3), norm="ortho").real.astype(x.dtype)
    fmix = jnp.einsum('bsgc,gce->bsge', fmix, fourier_w).reshape(b, s, FOURIER_WIDTH)
    f_out = fmix * jax.nn.silu(f_gate)
    q = rms_norm_2(q.reshape(b, s, N_Q_HEADS, HEAD_DIM), q_gain)
    k = rms_norm_2(k.reshape(b, s, N_KV_HEADS, HEAD_DIM), k_gain)
    v = v.reshape(b, s, N_KV_HEADS, HEAD_DIM)
    q = axial_rope(q, rope)
    k = axial_rope(k, rope)
    a_out = blocked_attention(q, k, v) * jax.nn.silu(a_gate)
    return x + jnp.concatenate([f_out, a_out], axis=-1) @ w_out

def rglru_scan(xc, w_a, b_a, w_x, b_x, lam, reverse):
    b, s, _ = xc.shape
    xb = xc.astype(jnp.float32).reshape(b, s, N_RNN_BLOCKS, RNN_BLOCK)
    r = jax.nn.sigmoid(jnp.einsum('bshc,hce->bshe', xb, w_a.astype(jnp.float32)) + b_a).reshape(b, s, RNN_WIDTH)
    i = jax.nn.sigmoid(jnp.einsum('bshc,hce->bshe', xb, w_x.astype(jnp.float32)) + b_x).reshape(b, s, RNN_WIDTH)
    log_a = -RG_LRU_C * r * jax.nn.softplus(-lam.astype(jnp.float32))
    a = jnp.exp(log_a)
    u = jnp.sqrt(-jnp.expm1(2.0 * log_a)) * (i * xb.reshape(b, s, RNN_WIDTH))

    def combine(left, right):
        a1, h1 = left
        a2, h2 = right
        return a1 * a2, a2 * h1 + h2

    _, hseq = lax.associative_scan(combine, (a, u), reverse=reverse, axis=1)
    return hseq

def rglru_layer(x, norm_g, w_in, conv_w, conv_b, w_a, b_a, w_x, b_x, lam, w_out):
    s = x.shape[1]
    h = rms_norm_2(x, norm_g)
    xr, gate = jnp.split(h @ w_in, 2, axis=-1)
    xp = jnp.pad(xr, ((0, 0), (CONV_LEFT, CONV_WIDTH - 1 - CONV_LEFT), (0, 0)))
    xc = conv_b + xp[:, 0:s] * conv_w[0]
    for j in range(1, CONV_WIDTH):
        xc = xc + xp[:, j:j + s] * conv_w[j]
    y = (rglru_scan(xc, w_a[0], b_a[0], w_x[0], b_x[0], lam[0], reverse=False)
         + rglru_scan(xc, w_a[1], b_a[1], w_x[1], b_x[1], lam[1], reverse=True))
    return x + (y.astype(x.dtype) * jax.nn.silu(gate)) @ w_out

def second_inputs(seed: int = 0) -> dict:
    key = jax.random.key(seed)
    ks = jax.random.split(key, 20)
    n_even = (DEPTH_2 + 1) // 2
    n_odd = DEPTH_2 // 2

    def nrm(k, shape, scale):
        return jax.random.normal(k, shape, jnp.float32) * scale

    x = nrm(ks[0], (BATCH, SEQ, D_MODEL), 1.0)
    even_norm = 1.0 + nrm(ks[1], (n_even, D_MODEL), 0.02)
    even_w_in = nrm(ks[2], (n_even, D_MODEL, EVEN_IN_WIDTH), D_MODEL ** -0.5)
    fourier_w = nrm(ks[3], (n_even, N_FOURIER_GROUPS, FOURIER_GROUP, FOURIER_GROUP), FOURIER_GROUP ** -0.5)
    q_gain = 1.0 + nrm(ks[4], (n_even, HEAD_DIM), 0.02)
    k_gain = 1.0 + nrm(ks[5], (n_even, HEAD_DIM), 0.02)
    even_w_out = nrm(ks[6], (n_even, MIX_WIDTH, D_MODEL), MIX_WIDTH ** -0.5)
    odd_norm = 1.0 + nrm(ks[7], (n_odd, D_MODEL), 0.02)
    odd_w_in = nrm(ks[8], (n_odd, D_MODEL, 2 * RNN_WIDTH), D_MODEL ** -0.5)
    conv_w = nrm(ks[9], (n_odd, CONV_WIDTH, RNN_WIDTH), CONV_WIDTH ** -0.5)
    conv_b = nrm(ks[10], (n_odd, RNN_WIDTH), 0.01)
    gate_a_w = nrm(ks[11], (n_odd, 2, N_RNN_BLOCKS, RNN_BLOCK, RNN_BLOCK), RNN_BLOCK ** -0.5)
    gate_a_b = nrm(ks[12], (n_odd, 2, N_RNN_BLOCKS, RNN_BLOCK), 0.01)
    gate_x_w = nrm(ks[13], (n_odd, 2, N_RNN_BLOCKS, RNN_BLOCK, RNN_BLOCK), RNN_BLOCK ** -0.5)
    gate_x_b = nrm(ks[14], (n_odd, 2, N_RNN_BLOCKS, RNN_BLOCK), 0.01)
    a_pow = jax.random.uniform(ks[15], (n_odd, 2, RNN_WIDTH), jnp.float32, minval=0.9, maxval=0.999)
    a0 = a_pow ** (1.0 / RG_LRU_C)
    rglru_lambda = jnp.log(a0) - jnp.log1p(-a0)
    odd_w_out = nrm(ks[16], (n_odd, RNN_WIDTH, D_MODEL), RNN_WIDTH ** -0.5)
    final_norm = 1.0 + nrm(ks[17], (D_MODEL,), 0.02)
    return {"x": x, "even_norm": even_norm, "even_w_in": even_w_in, "fourier_w": fourier_w,
            "q_gain": q_gain, "k_gain": k_gain, "even_w_out": even_w_out,
            "odd_norm": odd_norm, "odd_w_in": odd_w_in, "conv_w": conv_w, "conv_b": conv_b,
            "gate_a_w": gate_a_w, "gate_a_b": gate_a_b, "gate_x_w": gate_x_w, "gate_x_b": gate_x_b,
            "rglru_lambda": rglru_lambda, "odd_w_out": odd_w_out, "final_norm": final_norm}

def second_block(x, even_norm, even_w_in, fourier_w, q_gain, k_gain, even_w_out,
              odd_norm, odd_w_in, conv_w, conv_b, gate_a_w, gate_a_b, gate_x_w, gate_x_b,
              rglru_lambda, odd_w_out, final_norm):
    rope = axial_rope_tables(x.shape[1])
    h = x
    for layer in range(DEPTH_2):
        i = layer // 2
        if layer % 2 == 0:
            h = fourier_attention_layer(h, even_norm[i], even_w_in[i], fourier_w[i],
                                        q_gain[i], k_gain[i], even_w_out[i], rope)
        else:
            h = rglru_layer(h, odd_norm[i], odd_w_in[i], conv_w[i], conv_b[i],
                            gate_a_w[i], gate_a_b[i], gate_x_w[i], gate_x_b[i],
                            rglru_lambda[i], odd_w_out[i])
    return rms_norm_2(h, final_norm)


def setup_inputs(seed=0):
    out = dict(first_inputs(seed))
    for name, value in second_inputs(seed + 1).items():
        if name != "x":
            out[name + "_2"] = value
    return out


def reference(
    x, ffn1_norm, ffn1_w_gate, ffn1_w_up, ffn1_w_down, mix_norm, w_in, conv_w, w_out_a, mu_b,
    w0, w_decay_up, a0, w_iclr_up, w_gate_up, k_k, k_a, r_k, ln_x_w, ln_x_b, w_out_b, w_o,
    ffn2_norm, ffn2_w_gate, ffn2_w_up, ffn2_w_down, final_norm, even_norm_2, even_w_in_2,
    fourier_w_2, q_gain_2, k_gain_2, even_w_out_2, odd_norm_2, odd_w_in_2, conv_w_2, conv_b_2,
    gate_a_w_2, gate_a_b_2, gate_x_w_2, gate_x_b_2, rglru_lambda_2, odd_w_out_2, final_norm_2,
):
    x = first_block(
        x, ffn1_norm, ffn1_w_gate, ffn1_w_up, ffn1_w_down, mix_norm, w_in, conv_w, w_out_a,
        mu_b, w0, w_decay_up, a0, w_iclr_up, w_gate_up, k_k, k_a, r_k, ln_x_w, ln_x_b, w_out_b,
        w_o, ffn2_norm, ffn2_w_gate, ffn2_w_up, ffn2_w_down, final_norm,
    )
    return second_block(
        x, even_norm_2, even_w_in_2, fourier_w_2, q_gain_2, k_gain_2, even_w_out_2, odd_norm_2,
        odd_w_in_2, conv_w_2, conv_b_2, gate_a_w_2, gate_a_b_2, gate_x_w_2, gate_x_b_2,
        rglru_lambda_2, odd_w_out_2, final_norm_2,
    )


_drawn_inputs = setup_inputs


def setup_inputs(seed=0):
    import zlib

    import numpy as np

    out = dict(_drawn_inputs(seed))
    spreads = {}
    factors = {'even_norm_2': 8.0,
     'even_w_in_2': 5.885,
     'fourier_w_2': 5.977,
     'q_gain_2': 8.0,
     'k_gain_2': 8.0,
     'even_w_out_2': 5.898,
     'odd_norm_2': 64.0,
     'odd_w_in_2': 26.776,
     'conv_w_2': 27.6,
     'conv_b_2': 64.0,
     'gate_a_w_2': 64.0,
     'gate_a_b_2': 64.0,
     'gate_x_w_2': 60.144,
     'gate_x_b_2': 64.0,
     'rglru_lambda_2': 64.0,
     'odd_w_out_2': 26.592,
     'final_norm_2': 8.091}
    for name, (base, spread) in spreads.items():
        noise = np.random.default_rng([zlib.crc32(name.encode()), seed]).standard_normal(out[name].shape)
        drawn = base * np.exp(spread * noise) if base else spread * noise
        out[name] = __import__('jax').numpy.asarray(drawn.astype(out[name].dtype))
    for name, factor in factors.items():
        out[name] = (out[name] * factor).astype(out[name].dtype)
    return out
```

```python
from contextlib import ExitStack

import concourse.bass as bass
from concourse import mybir

ACT = mybir.ActivationFunctionType
ALU = mybir.AluOpType
AX_X = mybir.AxisListType.X
F32 = mybir.dt.float32
FR = mybir.dt.float32r
I32 = mybir.dt.int32
I8 = mybir.dt.int8

P = 128
T = 512
D = 1024
KD = D // P
KF = 2816 // P
BLK = 8
HEADS, HS = 8, 64
NJ = HEADS * HS // P
CH = 128
NCH = T // CH
LEVELS = 7
QT = T // P
NRB = 16
INV_SQRT_E = 0.6065306597126334

COLS = {}
_at = 0
for _name, _n in (
    ("ffn1_norm", 8), ("mix_norm", 8), ("ffn2_norm", 8), ("final_norm", 8), ("even_norm_2", 8),
    ("odd_norm_2", 8), ("final_norm_2", 8), ("conv_w", 12), ("mu_b", 14), ("w0", 4), ("a0", 4),
    ("k_k", 4), ("k_a", 4), ("r_k", 4), ("ln_x_w", 4), ("ln_x_b", 4), ("q_gain_2", 1), ("k_gain_2", 1),
    ("conv_w_2", 64), ("conv_b_2", 16), ("gate_a_b_2", 32), ("gate_x_b_2", 32), ("rglru_lambda_2", 32),
    ("eps_rms", 1), ("eps_gn", 1),
):
    COLS[_name] = _at
    _at += _n
NCOLS = _at

N_UP, N_DOWN = 2 * KF, KF
N_CONV, N_MIX, N_MERGE, N_WO = 12, 14, 24, 8
N_PAIR, N_KV, N_HALF, N_RNN = 16, 4, 8, 32
NBLOCKS = 2 * (N_UP + N_DOWN) + N_CONV + N_MIX + N_MERGE + N_WO + 2 * N_PAIR + N_KV + 2 * N_HALF + N_RNN + 16


def col(par, name, i=0, n=1):
    return par[:, bass.ds(COLS[name] + i, n)]


def tile(buf, i):
    return buf[:, bass.ds(i, 1), :].rearrange("p a t -> p (a t)")


class Chain:

    def __init__(self, eng, sem):
        self.eng, self.sem, self.base, self.k, self.at = eng, sem, 0, 0, None

    def link(self, ins):
        ins.then_inc(self.sem, 1)
        self.k += 1
        self.eng.wait_ge(self.sem, self.base + self.k if self.at is None else self.at + (self.base + self.k))

    def enter(self, i, per):
        self.base, self.k, self.per, self.at = self.base + self.k, 0, per, i * per

    def leave(self, trips):
        assert self.k == self.per, (self.k, self.per)
        self.base, self.k, self.at = self.base + trips * self.per, 0, None


def program(nc, xT, wstream, params, mats, masks, lora, gup, rope, dft_c, dft_s, fw, rgates, outT):
    with ExitStack() as ctx:
        def sb(name, shape, dt=F32, on=ctx):
            return on.enter_context(nc.sbuf_tensor(name, shape, dt))

        def sem(name):
            return ctx.enter_context(nc.semaphore(name))

        ps = ctx.enter_context(nc.psum_tensor("ps", [P, 8, T], F32))

        x = sb("x", [P, KD, T])
        w_raw = sb("w_raw", [P, 2, BLK * P])
        w_hi = sb("w_hi", [P, 2, BLK * P], FR)
        w_lo = sb("w_lo", [P, 2, BLK * P], FR)
        par = sb("par", [P, NCOLS])
        mat = sb("mat", [P, 4, P])
        ones, bones, ident, perm = (mat[:, k, :] for k in range(4))
        lev8 = sb("lev8", [P, LEVELS, 2, P], I8)
        tri8 = sb("tri8", [P, 4, P], I8)
        sq = sb("sq", [P, 2, T])
        root = sb("root", [P, 1, T])
        rinv = sb("rinv", [P, 1, T])
        tmp = sb("tmp", [P, 2, T])
        h_hi = sb("h_hi", [P, KD, T], FR)
        h_lo = sb("h_lo", [P, KD, T], FR)

        with ExitStack() as a:
            hid_hi = sb("hid_hi", [P, KF, T], FR, a)
            hid_lo = sb("hid_lo", [P, KF, T], FR, a)
            gate_s = sb("gate_s", [P, 2, T], F32, a)
            hid_t = sb("hid_t", [P, 2, T], F32, a)
            m32 = sb("m32", [P, (LEVELS * 2 + 4) * P], I32, a)
        with ExitStack() as a:
            scores = sb("scores", [P, HEADS, 4, P], F32, a)
            xx = sb("xx", [P, HEADS, 2, P], F32, a)
            t1 = sb("t1", [P, HEADS, P], F32, a)
            ar = sb("ar", [P, NJ, 2, CH], F32, a)
            bc = sb("bc", [P, NJ, CH], F32, a)
            kc_ = sb("kc_", [P, NJ, CH], F32, a)
            tok = sb("tok", [P, 3, T], F32, a)
            st = sb("st", [P, NJ, HS], F32, a)
            st0 = sb("st0", [P, NJ, HS], F32, a)
            pe_ = sb("pe_", [P, NJ, CH + 1], F32, a)
            pn = sb("pn", [P, NJ, CH + 1], F32, a)
            rmid = sb("rmid", [P, NJ, 1], F32, a)
            ya = sb("ya", [P, NJ, T], F32, a)
            mix = sb("mix", [P, 14, T], F32, a)
            wd = sb("wd", [P, NJ, T], F32, a)
            kk = sb("kk", [P, NJ, T], F32, a)
            bb = sb("bb", [P, NJ, T], F32, a)
            gg = sb("gg", [P, NJ, T], F32, a)
        with ExitStack() as a:
            padc = sb("padc", [P, 2, T + 2], F32, a)
            csb = sb("csb", [P, 2, T], F32, a)
            padm = sb("padm", [P, 2, T + 1], F32, a)
            dif = sb("dif", [P, 2, T], F32, a)
            lora_s = sb("lora_s", [P, T], F32, a)
            gup_s = sb("gup_s", [P, T], F32, a)
        with ExitStack() as a:
            ya_hi = sb("ya_hi", [P, NJ, T], FR, a)
            ya_lo = sb("ya_lo", [P, NJ, T], FR, a)
            yb_hi = sb("yb_hi", [P, NJ, T], FR, a)
            yb_lo = sb("yb_lo", [P, NJ, T], FR, a)
            gap = sb("gap", [P, 13, T], F32, a)
            mg_hi = sb("mg_hi", [P, KD, T], FR, a)
            mg_lo = sb("mg_lo", [P, KD, T], FR, a)
            sga = sb("sga", [P, 2, 2, T], F32, a)
            mt = sb("mt", [P, 2, 2, T], F32, a)
        with ExitStack() as a:
            z_hi = sb("z_hi", [P, KD, T], FR, a)
            z_lo = sb("z_lo", [P, KD, T], FR, a)
            left = sb("left", [P, KD, T], F32, a)
            right = sb("right", [P, KD, T], F32, a)
            with ExitStack() as b:
                dftc = sb("dftc", [P, 2, T], F32, b)
                dfts = sb("dfts", [P, 2 * QT, T], F32, b)
                fws = sb("fws", [P, 16, P], F32, b)
                chan = sb("chan", [P, QT, T], F32, b)
                fmix = sb("fmix", [P, 2, T], F32, b)
            with ExitStack() as b:
                kt = sb("kt", [P, 2, T], F32, b)
                vt = sb("vt", [P, QT, 256], F32, b)
                rope_s = sb("rope_s", [P, 2, T], F32, b)
                prob = sb("prob", [P, QT, T], F32, b)
                probT = sb("probT", [P, QT, T], F32, b)
                qr = sb("qr", [P, 1, T], F32, b)
                mx = sb("mx", [P, 4 * QT], F32, b)
        with ExitStack() as a:
            y_hi = sb("y_hi", [P, NRB, T], FR, a)
            y_lo = sb("y_lo", [P, NRB, T], FR, a)
            rg_w = sb("rg_w", [P, 2, 4, P], F32, a)
            xp = sb("xp", [P, 2, T + 3], F32, a)
            xc = sb("xc", [P, 2, T], F32, a)
            sgate = sb("sgate", [P, 2, T], F32, a)
            ri = sb("ri", [P, 4, T], F32, a)
            aa = sb("aa", [P, 2, T], F32, a)
            th = sb("th", [P, 2, T], F32, a)
            uu = sb("uu", [P, 2, T], F32, a)
            hh = sb("hh", [P, 2, T], F32, a)
            lam = sb("lam", [P, 6, 32], F32, a)

        s_x = sem("x_loaded")
        s_par = sem("params_loaded")
        landed = [sem(f"weights_landed_{s}") for s in range(2)]
        w_hi_done = sem("w_hi_done")
        w_split = sem("w_split")
        w_done = sem("w_done")
        v_chain = sem("vector_chain")
        a_chain = sem("scalar_chain")
        s_pass = sem("vector_passed")
        s_pool_pass = sem("pool_passed")
        nrm = {q: sem(f"norm_{q}") for q in ("x", "sq", "sqmm", "root", "t", "hi", "h")}

        def x_at(k):
            return KD * (k - 1 if k < 5 else k)

        def h_at(k):
            return KD * (k if k < 3 else k - 1)

        ffn = [{q: sem(f"ffn{k}_{q}") for q in ("silu", "t", "hi", "hid")} for k in range(2)]
        mx_s = {q: sem(f"mixer_{q}") for q in (
            "small_loaded", "c", "ya", "raw", "mix", "lora_in", "lora_mm", "lora_ev", "kk_sq", "kk_ss", "kk_root", "kk_done", "kk_w")}
        rw = {q: sem(f"rwkv_{q}") for q in (
            "ops", "vc", "reset", "tr", "tok", "mat", "sc", "t1mm", "t1", "xmm", "xx", "rhsmm", "rhs", "umm", "u",
            "ysmm", "y", "s")}
        po = {q: sem(f"post_{q}") for q in (
            "mean", "yc", "sq", "var", "root", "rk", "bonus", "t", "hi", "done", "yahi", "ya", "sig", "mg_t", "mg_hi", "mg")}
        ev = {q: sem(f"even_{q}") for q in ("loaded", "l0", "r0", "l1", "r1", "k", "v", "chmm", "chan", "sqmm", "fmix",
                                             "fwmm", "t", "hi", "z")}
        at = {q: sem(f"attn_{q}") for q in ("rope", "sq", "ssmm", "root", "qn", "rot", "qr", "smm", "max", "exp", "prob",
                                             "tr", "pt", "pv", "t", "hi", "z")}
        rg = {q: sem(f"rglru_{q}") for q in ("w0", "w1", "wuse", "x", "sg", "lexp", "xc", "gmm", "ri", "nla", "a", "th",
                                              "w", "root", "y", "t", "hi", "z")}
        s_out_t = sem("out_tile")
        s_out = sem("out_stored")

        block = ctx.enter_context(nc.Block())

        first = {}
        n = 0
        for name, size in (("up0", N_UP), ("down0", N_DOWN), ("conv", N_CONV), ("mix", N_MIX), ("merge", N_MERGE),
                           ("wo", N_WO), ("up1", N_UP), ("down1", N_DOWN), ("pair0", N_PAIR), ("eo0", N_HALF),
                           ("pair1", N_PAIR), ("kv", N_KV), ("eo1", N_HALF), ("rnn", N_RNN), ("ro", 16)):
            first[name] = n
            n += size
        assert n == NBLOCKS and NBLOCKS % 2 == 0

        @block.sync
        def _(sp):
            sp.dma_start(x[:], xT).then_inc(s_x, 16)
            for s in range(2):
                sp.dma_start(w_raw[:, s, :], wstream[s]).then_inc(landed[s], 16)
            sp.dma_start(par[:], params).then_inc(s_par, 16)
            sp.dma_start(mat[:], mats).then_inc(s_par, 16)
            sp.dma_start(m32[:], masks).then_inc(s_par, 16)
            with sp.Fori(0, NBLOCKS // 2 - 1) as i:
                for s in range(2):
                    sp.wait_ge(w_split, 2 * i + (s + 1))
                    sp.dma_start(w_raw[:, s, :], wstream[bass.ds(2 * i + (2 + s), 1)].rearrange("a p q -> p (a q)")
                                 ).then_inc(landed[s], 16)
            for m in range(KD):
                sp.wait_ge(s_out_t, m + 1)
                sp.dma_start(outT[:, m, :], x[:, m, :]).then_inc(s_out, 16)
            sp.wait_ge(s_out, 16 * KD)

        @block.gpsimd
        def _(pool):
            def split(s):
                nc.gpsimd.tensor_scalar(w_hi[:, s, :], w_raw[:, s, :], 1.0, 0.0, ALU.mult, ALU.add).then_inc(w_hi_done, 1)

            def rest(s):
                nc.gpsimd.tensor_tensor(w_lo[:, s, :], w_raw[:, s, :], w_hi[:, s, :].bitcast(F32), ALU.subtract
                                        ).then_inc(w_split, 1)

            for s in range(2):
                pool.wait_ge(landed[s], 16)
                split(s)
                pool.wait_ge(w_hi_done, s + 1)
                rest(s)
            with pool.Fori(0, NBLOCKS // 2 - 1) as i:
                for s in range(2):
                    pool.wait_ge(landed[s], 16 * i + 32)
                    pool.wait_ge(w_done, 2 * i + (s + 1))
                    pool.sem_inc(s_pool_pass, 1)
                    split(s)
                    pool.wait_ge(w_hi_done, 2 * i + (s + 3))
                    rest(s)

        @block.tensor
        def _(pe):
            mm = nc.tensor.matmul

            def mm3(out, s, k, hi, lo, start, stop, n=P):
                w = slice(k * n, (k + 1) * n)
                mm(out, w_hi[:, s, w], hi, start=start, stop=False)
                mm(out, w_hi[:, s, w], lo, start=False, stop=False)
                return mm(out, w_lo[:, s, w], hi, start=False, stop=stop)

            def dense(n, s, bank, hi, lo):
                pe.wait_ge(w_split, n + 1)
                for k in range(BLK):
                    last = mm3(ps[:, bank, :], s, k, hi[:, k, :], lo[:, k, :], k == 0, k == BLK - 1)
                last.then_inc(w_done, 1)

            def sum_squares(k):
                q = nrm
                for m in range(KD):
                    pe.wait_ge(q["sq"], KD * k + m + 1)
                    mm(ps[:, 0, :], ones, sq[:, m % 2, :], start=(m == 0), stop=(m == KD - 1)).then_inc(q["sqmm"], 1)

            def residual(name, nk, hi, lo, ready):
                def step(n, s, k, start, stop):
                    pe.wait_ge(w_split, n + 1)
                    for m in range(KD):
                        last = mm3(ps[:, m, :], s, m, tile(hi, k), tile(lo, k), start, stop)
                    last.then_inc(w_done, 1)
                f = first[name]
                ready()
                for k in range(2):
                    step(f + k, k, k, k == 0, False)
                with pe.Fori(0, nk // 2 - 2) as i:
                    for s in range(2):
                        step(2 * i + (f + 2 + s), s, 2 * i + (2 + s), False, False)
                for k in range(nk - 2, nk):
                    step(f + k, k % 2, k, False, k == nk - 1)

            def ffn_up(k, name):
                q = ffn[k]
                f = first[name]
                pe.wait_ge(nrm["h"], h_at(2 * k) + KD)
                for s in range(4):
                    dense(f + s, s % 2, s, h_hi, h_lo)
                with pe.Fori(0, KF // 2 - 1) as i:
                    for s in range(4):
                        if s % 2 == 0:
                            pe.wait_ge(q["t"], 2 * i + (s // 2 + 1))
                        dense(4 * i + (f + 4 + s), s % 2, s, h_hi, h_lo)

            pe.wait_ge(s_par, 48)
            sum_squares(0)
            ffn_up(0, "up0")
            residual("down0", KF, hid_hi, hid_lo, lambda: pe.wait_ge(ffn[0]["hid"], KF))

            sum_squares(1)
            pe.wait_ge(nrm["h"], h_at(1) + KD)
            f = first["conv"]
            for s in range(3):
                dense(f + s, s % 2, s, h_hi, h_lo)
            for s in range(3, 6):
                dense(f + s, s % 2, s, h_hi, h_lo)
            for s in range(6, 12):
                if s % 3 == 0:
                    pe.wait_ge(mx_s["ya"], s // 3 - 1)
                dense(f + s, s % 2, s % 6, h_hi, h_lo)
            f = first["mix"]
            with pe.Fori(0, 7) as i:
                for s in range(2):
                    if s == 0:
                        pe.wait_ge(mx_s["raw"], 2 * i + 1)
                    else:
                        pe.wait_ge(mx_s["raw"], 2 * i + 2)
                    dense(2 * i + (f + s), s, 6 + s, h_hi, h_lo)
            pe.wait_ge(mx_s["small_loaded"], 32)
            pe.wait_ge(mx_s["lora_in"], 3)
            pe.wait_ge(mx_s["ya"], NJ)
            pe.wait_ge(mx_s["raw"], 16)
            for j in range(NJ):
                w = slice(j * P, (j + 1) * P)
                mm(ps[:, j, :], lora_s[0:64, w], sq[0:64, 0, :], start=True, stop=True).then_inc(mx_s["lora_mm"], 1)
            for j in range(NJ):
                w = slice(j * P, (j + 1) * P)
                mm(ps[:, 4 + j, :], lora_s[64:128, w], tmp[64:128, 0, :], start=True, stop=True).then_inc(mx_s["lora_mm"], 1)
            for j in range(NJ):
                w = slice(j * P, (j + 1) * P)
                pe.wait_ge(mx_s["lora_ev"], j + 1)
                mm(ps[:, j, :], gup_s[:, w], sq[:, 1, :], start=True, stop=True).then_inc(mx_s["lora_mm"], 1)
            for j in range(NJ):
                pe.wait_ge(mx_s["kk_sq"], j + 1)
                pe.wait_ge(mx_s["lora_ev"], 5 + j)
                mm(ps[:, 4 + j, :], bones, dif[:, j % 2, :], start=True, stop=True).then_inc(mx_s["kk_ss"], 1)

            pe.wait_ge(mx_s["lora_ev"], 12)
            pe.wait_ge(mx_s["kk_root"], NJ)
            with pe.Fori(0, NCH) as c:
                pe.wait_ge(rw["ops"], c + 1)
                pe.wait_ge(rw["vc"], c + 1)
                for q, src in enumerate((bc, kc_, root)):
                    for j in range(NJ):
                        w = slice(j * P, (j + 1) * P)
                        a = src[:, j, :] if q < 2 else root[:, 0, w]
                        last = nc.tensor.transpose(ps[:, q, w], a, ident)
                    last.then_inc(rw["tr"], 1)
                for h in range(HEADS):
                    j, p0 = h // 2, HS * (h % 2)
                    pp = slice(p0, p0 + HS)
                    bank = 4 + h % 4
                    if h >= 4:
                        pe.wait_ge(rw["sc"], HEADS * c + (h - 3))
                    mm(ps[:, bank, 0:256], bc[pp, j, :], ar[pp, j, :, :].rearrange("p a t -> p (a t)"), start=True, stop=True)
                    mm(ps[:, bank, 256:512], kc_[pp, j, :], ar[pp, j, :, :].rearrange("p a t -> p (a t)"),
                       start=True, stop=True).then_inc(rw["mat"], 1)
                pe.wait_ge(rw["reset"], c + 1)
                pe.wait_ge(rw["tok"], 3 * c + 3)
                pe.wait_ge(rw["sc"], HEADS * c + HEADS)
                for l in range(LEVELS):
                    for g in range(2):
                        if l >= 1:
                            pe.wait_ge(rw["xx"], 4 * LEVELS * c + (4 * (l - 1) + 2 * g + 2))
                        for h in range(4 * g, 4 * g + 4):
                            last = mm(ps[:, g, (h % 4) * P:(h % 4 + 1) * P], scores[:, h, 0, :], xx[:, h, 0, :],
                                      start=True, stop=True)
                        last.then_inc(rw["t1mm"], 1)
                    for g in range(2):
                        pe.wait_ge(rw["t1"], 2 * LEVELS * c + (2 * l + g + 1))
                        for h in range(4 * g, 4 * g + 4):
                            bank, o = 4 + h // 2, 256 * (h % 2)
                            mm(ps[:, bank, o:o + P], xx[:, h, 1, :], t1[:, h, :], start=True, stop=True)
                            last = mm(ps[:, bank, o + P:o + 2 * P], t1[:, h, :], xx[:, h, 1, :], start=True, stop=True)
                            if h % 2 == 1:
                                last.then_inc(rw["xmm"], 1)
                pe.wait_ge(rw["xx"], 4 * LEVELS * c + 4 * LEVELS)
                for h in range(HEADS):
                    j, p0 = h // 2, HS * (h % 2)
                    pp = slice(p0, p0 + HS)
                    o = slice(j * HS, (j + 1) * HS)
                    out = ps[:, 2 + h % 2, o]
                    mm(out, ar[pp, j, 0, :], st0[pp, j, :], start=True, stop=False)
                    last = mm(out, scores[:, h, 2, :], tok[:, 2, h * HS:(h + 1) * HS], start=False, stop=True)
                last.then_inc(rw["rhsmm"], 1)
                pe.wait_ge(rw["rhs"], c + 1)
                for h in range(HEADS):
                    o = slice(h * HS, (h + 1) * HS)
                    last = mm(ps[:, 0, o], xx[:, h, 1, :], sq[:, 0, o], start=True, stop=True)
                last.then_inc(rw["umm"], 1)
                pe.wait_ge(rw["u"], c + 1)
                for h in range(HEADS):
                    j, p0 = h // 2, HS * (h % 2)
                    pp = slice(p0, p0 + HS)
                    o = slice(h * HS, (h + 1) * HS)
                    out = ps[pp, 4 + h % 2, j * CH:(j + 1) * CH]
                    mm(out, sq[:, 1, o], scores[:, h, 1, :], start=True, stop=False)
                    mm(out, tok[:, 2, o], scores[:, h, 3, :], start=False, stop=False)
                    mm(out, st0[pp, j, :], ar[pp, j, 1, :], start=False, stop=True)
                for h in range(HEADS):
                    j, p0 = h // 2, HS * (h % 2)
                    pp = slice(p0, p0 + HS)
                    o = slice(h * HS, (h + 1) * HS)
                    out = ps[pp, 6, j * HS:(j + 1) * HS]
                    mm(out, tok[:, 0, o], sq[:, 1, o], start=True, stop=False)
                    last = mm(out, tok[:, 1, o], tok[:, 2, o], start=False, stop=True)
                last.then_inc(rw["ysmm"], 1)

            pe.wait_ge(rw["y"], 2 * NCH)
            pe.wait_ge(rw["s"], NCH + 1)
            with pe.Fori(0, NJ) as j:
                mm(ps[:, 0, :], bones, tile(wd, j), start=True, stop=True).then_inc(po["mean"], 1)
                pe.wait_ge(po["rk"], j + 1)
                mm(ps[:, 2, :], bones, sq[:, 1, :], start=True, stop=True).then_inc(po["bonus"], 1)
                pe.wait_ge(po["sq"], j + 1)
                mm(ps[:, 1, :], bones, sq[:, 0, :], start=True, stop=True).then_inc(po["var"], 1)
                pe.wait_ge(po["done"], j + 1)

            f = first["merge"]
            pe.wait_ge(po["ya"], NJ)

            def merge(n, s, half):
                b = 4 * half
                pe.wait_ge(w_split, n + 1)
                for k in range(NJ):
                    mm3(ps[:, b, :], s, k, ya_hi[:, k, :], ya_lo[:, k, :], k == 0, k == NJ - 1)
                for k in range(NJ):
                    last = mm3(ps[:, b + 1, :], s, NJ + k, yb_hi[:, k, :], yb_lo[:, k, :], k == 0, k == NJ - 1)
                last.then_inc(w_done, 1)
                dense(n + 1, (s + 1) % 2, b + 2, h_hi, h_lo)
                dense(n + 2, s, b + 3, h_hi, h_lo)

            merge(f, 0, 0)
            merge(f + 3, 1, 1)
            with pe.Fori(0, 3) as i:
                for half in range(2):
                    pe.wait_ge(po["mg_t"], 2 * i + (half + 1))
                    merge(6 * i + (f + 6 + 3 * half), half, half)
            residual("wo", KD, mg_hi, mg_lo, lambda: pe.wait_ge(po["mg"], KD))

            sum_squares(2)
            ffn_up(1, "up1")
            residual("down1", KF, hid_hi, hid_lo, lambda: pe.wait_ge(ffn[1]["hid"], KF))
            sum_squares(3)

            sum_squares(4)

            def pairs(name, ls, rs):
                f = first[name]
                for s in range(4):
                    dense(f + s, s % 2, s, h_hi, h_lo)
                with pe.Fori(0, 3) as i:
                    for s in range(4):
                        pe.wait_ge(rs if s % 2 else ls, 2 * i + (s // 2 + 1))
                        dense(4 * i + (f + 4 + s), s % 2, s, h_hi, h_lo)

            pe.wait_ge(nrm["h"], h_at(4) + KD)
            pairs("pair0", ev["l0"], ev["r0"])
            pe.wait_ge(ev["l0"], KD)
            pe.wait_ge(ev["r0"], KD)
            pe.wait_ge(ev["loaded"], 48)
            for g in range(4):
                for t in range(QT):
                    if g >= 1:
                        pe.wait_ge(ev["fmix"], 2 * g)
                    for k in range(2):
                        last = mm(ps[:, t, :], left[:, 2 * g + k, t * P:(t + 1) * P], dftc[:, k, :],
                                  start=(k == 0), stop=(k == 1))
                    last.then_inc(ev["chmm"], 1)
                pe.wait_ge(ev["chan"], QT * (g + 1))
                for e in range(2):
                    if g >= 1:
                        pe.wait_ge(ev["fmix"], 2 * g - 1 + e)
                    for part in range(2):
                        for t in range(QT):
                            o = 256 * part + P * e
                            last = mm(ps[:, 4 + e, :], chan[:, t, o:o + P], dfts[:, part * QT + t, :],
                                      start=(part == 0 and t == 0), stop=(part == 1 and t == QT - 1))
                    last.then_inc(ev["sqmm"], 1)
                pe.wait_ge(ev["fmix"], 2 * g + 2)
                for e in range(2):
                    if g >= 1:
                        pe.wait_ge(ev["t"], 2 * g - 1 + e)
                    for k in range(2):
                        last = mm(ps[:, 6 + e, :], fws[:, (2 * g + k) * 2 + e, :], fmix[:, k, :],
                                  start=(k == 0), stop=(k == 1))
                    last.then_inc(ev["fwmm"], 1)
            pe.wait_ge(ev["t"], KD)
            residual("eo0", KD, z_hi, z_lo, lambda: pe.wait_ge(ev["z"], KD))

            pe.wait_ge(at["rope"], 48)
            pairs("pair1", ev["l1"], ev["r1"])
            f = first["kv"]
            for s in range(2):
                dense(f + s, s, 4 + s, h_hi, h_lo)
            pe.wait_ge(ev["l1"], KD)
            pe.wait_ge(ev["r1"], KD)
            for b in range(2):
                pe.wait_ge(w_split, f + 3 + b)
                for t in range(QT):
                    tt = slice(t * P, (t + 1) * P)
                    for k in range(4):
                        w = slice(k * 256, (k + 1) * 256)
                        kk_ = 4 * b + k
                        mm(ps[:, t, 0:256], h_hi[:, kk_, tt], w_hi[:, b, w], start=(kk_ == 0), stop=False)
                        mm(ps[:, t, 0:256], h_lo[:, kk_, tt], w_hi[:, b, w], start=False, stop=False)
                        last = mm(ps[:, t, 0:256], h_hi[:, kk_, tt], w_lo[:, b, w], start=False, stop=(kk_ == KD - 1))
                last.then_inc(w_done, 1)

            def head_prep(u):
                pe.wait_ge(at["sq"], u + 1)
                mm(ps[:, 0, :], ones, sq[:, 0, :], start=True, stop=True).then_inc(at["ssmm"], 1)
                pe.wait_ge(at["qn"], u + 1)
                mm(ps[:, 1, :], perm, tmp[:, 0, :], start=True, stop=True).then_inc(at["rot"], 1)

            pe.wait_ge(ev["k"], 2)
            pe.wait_ge(ev["v"], QT)
            for u in range(2):
                head_prep(u)
            for g in range(2):
                with pe.Fori(0, 4) as i:
                    hq = i + 4 * g
                    head_prep(i + (2 + 4 * g))
                    pe.wait_ge(at["qr"], i + (3 + 4 * g))
                    for t in range(QT):
                        mm(ps[:, 4 + t, :], qr[:, 0, t * P:(t + 1) * P], kt[:, g, :], start=True, stop=True).then_inc(at["smm"], 1)
                    for t in range(QT):
                        pe.wait_ge(at["prob"], QT * hq + (t + 1))
                        for kt_ in range(QT):
                            last = nc.tensor.transpose(ps[:, kt_, t * P:(t + 1) * P], prob[:, t, kt_ * P:(kt_ + 1) * P], ident)
                    last.then_inc(at["tr"], 1)
                    pe.wait_ge(at["pt"], QT * hq + QT)
                    for t in range(QT):
                        last = mm(ps[:, 4, :], vt[:, t, g * P:(g + 1) * P], probT[:, t, :], start=(t == 0), stop=(t == QT - 1))
                    last.then_inc(at["pv"], 1)
                    pe.wait_ge(at["t"], hq + 1)
            residual("eo1", KD, z_hi, z_lo, lambda: pe.wait_ge(at["z"], KD))

            sum_squares(5)
            f = first["rnn"]
            pe.wait_ge(nrm["h"], h_at(5) + KD)
            with pe.Fori(0, NRB // 2) as i:
                for s in range(2):
                    pe.wait_ge(rg["x"], 2 * i + (s + 1))
                    dense(4 * i + (f + 2 * s), 0, s, h_hi, h_lo)
                    pe.wait_ge(rg["sg"], 2 * i + (s + 1))
                    dense(4 * i + (f + 2 * s + 1), 1, 2 + s, h_hi, h_lo)
                for s in range(2):
                    pe.wait_ge(rg[f"w{s}"], 16 * i + 16)
                    pe.wait_ge(rg["xc"], 2 * i + (s + 1))
                    pe.wait_ge(rg["ri"], 8 * i + (4 * s + 4))
                    for k in range(4):
                        last = mm(ps[:, 4 + k, :], rg_w[:, s, k, :], xc[:, s, :], start=True, stop=True)
                    last.then_inc(rg["gmm"], 1)
            pe.wait_ge(rg["ri"], 4 * NRB + 4)
            pe.wait_ge(rg["sg"], NRB + 2)
            residual("ro", NRB, y_hi, y_lo, lambda: pe.wait_ge(rg["z"], NRB + 1))
            sum_squares(6)

        @block.scalar
        def _(act):
            A = nc.scalar.activation
            own = Chain(act, a_chain)

            def norm(k, where):
                q = nrm
                for m in range(KD):
                    if k == 0:
                        if m == 0:
                            act.wait_ge(s_x, 16)
                    else:
                        act.wait_ge(q["x"], x_at(k) + m + 1)
                    if m >= 2:
                        act.wait_ge(q["sqmm"], KD * k + m - 1)
                    A(sq[:, m % 2, :], x[:, m, :], ACT.Square).then_inc(q["sq"], 1)
                if k == 0:
                    act.wait_ge(s_par, 48)
                act.wait_ge(q["sqmm"], KD * k + KD)
                A(root[:, 0, :], ps[:, 0, :], ACT.Sqrt, bias=col(par, "eps_rms"), scale=1.0 / D).then_inc(q["root"], 1)
                if where == "h":
                    for m in range(KD):
                        act.wait_ge(q["t"], h_at(k) + m + 1)
                        nc.scalar.copy(h_hi[:, m, :], tmp[:, m % 2, :]).then_inc(q["hi"], 1)

            def ffn_up(k, name):
                q, f = ffn[k], first[name]

                def step(n, m, s, wait_free):
                    act.wait_ge(w_done, n + 1)
                    if wait_free is not None:
                        act.wait_ge(q["t"], wait_free)
                    A(gate_s[:, s, :], ps[:, 2 * s, :], ACT.Silu).then_inc(q["silu"], 1)
                    act.wait_ge(q["t"], m + 1)
                    nc.scalar.copy(tile(hid_hi, m), hid_t[:, s, :]).then_inc(q["hi"], 1)
                for s in range(2):
                    step(f + 2 * s, s, s, None)
                with act.Fori(0, KF // 2 - 1) as i:
                    for s in range(2):
                        step(4 * i + (f + 4 + 2 * s), 2 * i + (2 + s), s, 2 * i + (s + 1))

            norm(0, "h")
            ffn_up(0, "up0")
            act.wait_ge(w_done, first["conv"])
            act.dma_start(lora_s[:], lora).then_inc(mx_s["small_loaded"], 16)
            act.dma_start(gup_s[:], gup).then_inc(mx_s["small_loaded"], 16)
            norm(1, "h")

            f = first["conv"]
            for j in range(NJ):
                act.wait_ge(w_done, f + 3 * j + 1)
                if j >= 2:
                    act.wait_ge(mx_s["ya"], j - 1)
                nc.scalar.copy(csb[:, j % 2, :], ps[:, 3 * (j % 2), :]).then_inc(mx_s["c"], 1)
            act.sem_inc(mx_s["raw"], 2)
            f = first["mix"]
            with act.Fori(0, 7) as i:
                for s in range(2):
                    act.wait_ge(w_done, 2 * i + (f + s + 1))
                    act.wait_ge(mx_s["mix"], 2 * i + (s + 1))
                    nc.scalar.copy(padm[:, s, 1:T + 1], ps[:, 6 + s, :]).then_inc(mx_s["raw"], 1)
            act.wait_ge(mx_s["mix"], 16)
            A(sq[0:64, 0, :], mix[0:64, 12, :], ACT.Tanh).then_inc(mx_s["lora_in"], 1)
            nc.scalar.copy(tmp[64:128, 0, :], mix[64:128, 12, :]).then_inc(mx_s["lora_in"], 1)
            A(sq[:, 1, :], mix[:, 13, :], ACT.Sigmoid).then_inc(mx_s["lora_in"], 1)
            for j in range(NJ):
                act.wait_ge(mx_s["lora_mm"], j + 1)
                A(wd[:, j, :], ps[:, j, :], ACT.Sigmoid, bias=col(par, "w0", j)).then_inc(mx_s["lora_ev"], 1)
            for j in range(NJ):
                act.wait_ge(mx_s["lora_mm"], NJ + j + 1)
                A(bb[:, j, :], ps[:, 4 + j, :], ACT.Sigmoid, bias=col(par, "a0", j)).then_inc(mx_s["lora_ev"], 1)
            for j in range(NJ):
                act.wait_ge(mx_s["lora_mm"], 2 * NJ + j + 1)
                nc.scalar.copy(gg[:, j, :], ps[:, j, :]).then_inc(mx_s["lora_ev"], 1)
            act.wait_ge(mx_s["lora_ev"], NJ)
            for j in range(NJ):
                A(wd[:, j, :], wd[:, j, :], ACT.Exp, scale=-INV_SQRT_E).then_inc(mx_s["kk_w"], 1)
            for j in range(NJ):
                act.wait_ge(mx_s["kk_ss"], j + 1)
                if j >= 2:
                    act.wait_ge(mx_s["kk_done"], j - 1)
                A(tmp[:, j % 2, :], ps[:, 4 + j, :], ACT.Sqrt).then_inc(mx_s["kk_root"], 1)

            act.wait_ge(mx_s["kk_done"], NJ)
            with act.Fori(0, NCH) as c:
                act.wait_ge(rw["s"], c + 1)
                nc.scalar.copy(root[:, 0, :].rearrange("p (j t) -> p j t", j=NJ),
                               mix[:, 8:12, bass.ds(c * CH, CH)]).then_inc(rw["vc"], 1)
                for h in range(HEADS):
                    for z in range(2):
                        last = nc.scalar.copy(xx[:, h, z, :], ident)
                last.then_inc(rw["reset"], 1)
                for q in range(3):
                    act.wait_ge(rw["tr"], 3 * c + (q + 1))
                    nc.scalar.copy(tok[:, q, :], ps[:, q, :]).then_inc(rw["tok"], 1)
                for l in range(LEVELS):
                    for g in range(2):
                        act.wait_ge(rw["t1mm"], 2 * LEVELS * c + (2 * l + g + 1))
                        nc.scalar.copy(t1[:, 4 * g:4 * g + 4, :].rearrange("p h t -> p (h t)"), ps[:, g, :]).then_inc(rw["t1"], 1)
                act.wait_ge(rw["rhsmm"], c + 1)
                rhs = sq[:, 0, :].rearrange("p (j e v) -> p e j v", j=NJ, e=2)
                for e in range(2):
                    last = nc.scalar.copy(rhs[:, e], ps[:, 2 + e, 0:256].rearrange("p (j v) -> p j v", j=NJ))
                last.then_inc(rw["rhs"], 1)
                act.wait_ge(rw["umm"], c + 1)
                nc.scalar.copy(sq[:, 1, :], ps[:, 0, :]).then_inc(rw["u"], 1)

            with act.Fori(0, NJ) as j:
                act.wait_ge(po["yc"], j + 1)
                A(sq[:, 0, :], tmp[:, 0, :], ACT.Square).then_inc(po["sq"], 1)
                act.wait_ge(po["var"], j + 1)
                A(root[:, 0, :], ps[:, 1, :], ACT.Sqrt, bias=col(par, "eps_gn"), scale=1.0 / HS).then_inc(po["root"], 1)
                act.wait_ge(po["t"], j + 1)
                nc.scalar.copy(tile(yb_hi, j), tmp[:, 1, :]).then_inc(po["hi"], 1)
            for j in range(NJ):
                nc.scalar.copy(ya_hi[:, j, :], ya[:, j, :]).then_inc(po["yahi"], 1)

            f = first["merge"]
            act.wait_ge(po["done"], NJ)
            with act.Fori(0, KD // 2) as i:
                for half in range(2):
                    act.wait_ge(w_done, 6 * i + (f + 3 * half + 3))
                    A(sga[:, half, 0, :], ps[:, 4 * half + 2, :], ACT.Sigmoid)
                    A(sga[:, half, 1, :], ps[:, 4 * half + 3, :], ACT.Sigmoid).then_inc(po["sig"], 1)
                    act.wait_ge(po["mg_t"], 2 * i + (half + 1))
                    nc.scalar.copy(tile(mg_hi, 2 * i + half), mt[:, half, 1, :]).then_inc(po["mg_hi"], 1)

            norm(2, "h")
            ffn_up(1, "up1")
            act.wait_ge(w_done, first["pair0"])
            act.dma_start(dftc[:], dft_c).then_inc(ev["loaded"], 16)
            act.dma_start(dfts[:], dft_s).then_inc(ev["loaded"], 16)
            act.dma_start(fws[:], fw).then_inc(ev["loaded"], 16)
            norm(3, "x")
            norm(4, "h")

            def pairs(name, rs):
                f = first[name]
                with act.Fori(0, 4) as i:
                    for s in range(2):
                        act.wait_ge(w_done, 4 * i + (f + 2 * s + 2))
                        A(tile(right, 2 * i + s), ps[:, 2 * s + 1, :], ACT.Silu).then_inc(rs, 1)

            pairs("pair0", ev["r0"])
            for g in range(4):
                for t in range(QT):
                    act.wait_ge(ev["chmm"], QT * g + t + 1)
                    if g >= 1:
                        act.wait_ge(ev["sqmm"], 2 * g)
                    nc.scalar.copy(chan[:, t, :], ps[:, t, :]).then_inc(ev["chan"], 1)
                for e in range(2):
                    act.wait_ge(ev["t"], 2 * g + e + 1)
                    nc.scalar.copy(z_hi[:, 2 * g + e, :], tmp[:, e, :]).then_inc(ev["hi"], 1)
            act.wait_ge(w_done, first["pair1"])
            act.dma_start(rope_s[:], rope).then_inc(at["rope"], 16)
            act.wait_ge(at["rope"], 16)
            act.wait_ge(nrm["x"], x_at(5))
            act.sem_inc(at["rope"], 32)
            pairs("pair1", ev["r1"])
            f = first["kv"]
            for s in range(2):
                act.wait_ge(w_done, f + s + 1)
                nc.scalar.copy(kt[:, s, :], ps[:, 4 + s, :]).then_inc(ev["k"], 1)
            act.wait_ge(w_done, f + 4)
            for t in range(QT):
                nc.scalar.copy(vt[:, t, :], ps[:, t, 0:256]).then_inc(ev["v"], 1)

            def head_prep(u, src):
                A(sq[:, 0, :], src, ACT.Square).then_inc(at["sq"], 1)
                act.wait_ge(at["ssmm"], u + 1)
                A(root[:, 0, :], ps[:, 0, :], ACT.Sqrt, bias=col(par, "eps_rms"), scale=1.0 / P).then_inc(at["root"], 1)

            act.wait_ge(ev["k"], 2)
            for u in range(2):
                head_prep(u, kt[:, u, :])
                act.wait_ge(at["qr"], u + 1)
            for g in range(2):
                with act.Fori(0, 4) as i:
                    hq = i + 4 * g
                    head_prep(i + (2 + 4 * g), tile(left, hq))
                    for t in range(QT):
                        act.wait_ge(at["max"], QT * hq + (t + 1))
                        A(prob[:, t, :], ps[:, 4 + t, :], ACT.Exp, bias=mx[:, t:t + 1], scale=P ** -0.5,
                          accum_out=mx[:, 4 + t:5 + t]).then_inc(at["exp"], 1)
                    act.wait_ge(at["tr"], hq + 1)
                    for t in (0, 2):
                        nc.scalar.copy(probT[:, t, :], ps[:, t, :]).then_inc(at["pt"], 1)
                    act.wait_ge(at["t"], hq + 1)
                    nc.scalar.copy(tile(z_hi, hq), tmp[:, 1, :]).then_inc(at["hi"], 1)

            norm(5, "h")

            act.wait_ge(rg["lexp"], 1)
            A(lam[:, 1, :], lam[:, 0, :], ACT.Exp, scale=-1.0).then_inc(rg["lexp"], 1)
            f = first["rnn"]
            for s in range(2):
                act.dma_start(rg_w[:, s], rgates[s]).then_inc(rg[f"w{s}"], 16)
            act.sem_inc(rg["x"], 2)
            act.sem_inc(rg["sg"], 2)
            act.sem_inc(rg["ri"], 4)
            with act.Fori(0, NRB // 2) as i:
                for s in range(2):
                    act.wait_ge(w_done, 4 * i + (f + 2 * s + 1))
                    act.wait_ge(rg["z"], 2 * i + 1)
                    nc.scalar.copy(xp[:, s, 2:T + 2], ps[:, s, :]).then_inc(rg["x"], 1)
                    act.wait_ge(w_done, 4 * i + (f + 2 * s + 2))
                    A(sgate[:, s, :], ps[:, 2 + s, :], ACT.Silu).then_inc(rg["sg"], 1)
                for s in range(2):
                    act.wait_ge(rg["gmm"], 2 * i + (s + 1))
                    act.wait_ge(rg["y"], 2 * i + (s + 1))
                    for k in range(4):
                        name, d = ("gate_a_b_2", "gate_x_b_2")[k % 2], k // 2
                        A(ri[:, k, :], ps[:, 4 + k, :], ACT.Sigmoid, bias=col(par, name, 2 * i + (16 * d + s))
                          ).then_inc(rg["ri"], 1)
                    act.wait_ge(rg["nla"], 4 * i + (2 * s + 2))
                    for d in range(2):
                        A(aa[:, d, :], ri[:, 2 * d, :], ACT.Exp, scale=-1.0).then_inc(rg["a"], 1)
                    for d in range(2):
                        A(th[:, d, :], ri[:, 2 * d, :], ACT.Tanh).then_inc(rg["th"], 1)
                    act.wait_ge(rg["w"], 4 * i + (2 * s + 2))
                    for d in range(2):
                        A(uu[:, d, :], th[:, d, :], ACT.Sqrt).then_inc(rg["root"], 1)
                    act.wait_ge(rg["t"], 2 * i + (s + 1))
                    nc.scalar.copy(tile(y_hi, 2 * i + s), hh[:, 1, :]).then_inc(rg["hi"], 1)
                    act.dma_start(rg_w[:, s], rgates[bass.ds(2 * i + (2 + s), 1)].rearrange("a p k q -> p (a k) q")
                                  ).then_inc(rg[f"w{s}"], 16)
            norm(6, "out")
            for s in range(2):
                act.wait_ge(rg[f"w{s}"], 16 * (NRB // 2 + 1))

        @block.vector
        def _(dve):
            V = nc.vector
            own = Chain(dve, v_chain)

            def norm(k, where, g):
                q = nrm
                dve.wait_ge(q["root"], k + 1)
                own.link(V.reciprocal(rinv[:, 0, :], root[:, 0, :]))
                if where == "h":
                    for m in range(KD + 1):
                        if m < KD:
                            if m >= 2:
                                dve.wait_ge(q["h"], h_at(k) + m - 1)
                            V.scalar_tensor_tensor(out=tmp[:, m % 2, :], in0=x[:, m, :], scalar=col(par, g, m),
                                                   in1=rinv[:, 0, :], op0=ALU.mult, op1=ALU.mult).then_inc(q["t"], 1)
                        if m >= 1:
                            dve.wait_ge(q["hi"], h_at(k) + m)
                            V.tensor_tensor(h_lo[:, m - 1, :], tmp[:, (m - 1) % 2, :], h_hi[:, m - 1, :].bitcast(F32),
                                            ALU.subtract).then_inc(q["h"], 1)
                else:
                    done = s_out_t if where == "out" else nrm["x"]
                    for m in range(KD):
                        V.scalar_tensor_tensor(out=x[:, m, :], in0=x[:, m, :], scalar=col(par, g, m),
                                               in1=rinv[:, 0, :], op0=ALU.mult, op1=ALU.mult).then_inc(done, 1)

            def ffn_up(k, name):
                q, f = ffn[k], first[name]

                def step(n, m, s, wait_free):
                    dve.wait_ge(w_done, n + 2)
                    dve.wait_ge(q["silu"], m + 1)
                    if wait_free is not None:
                        dve.wait_ge(q["hid"], wait_free)
                    V.tensor_tensor(hid_t[:, s, :], gate_s[:, s, :], ps[:, 2 * s + 1, :], ALU.mult).then_inc(q["t"], 1)
                    dve.wait_ge(q["hi"], m + 1)
                    V.tensor_tensor(tile(hid_lo, m), hid_t[:, s, :], tile(hid_hi, m).bitcast(F32), ALU.subtract
                                    ).then_inc(q["hid"], 1)
                for s in range(2):
                    step(f + 2 * s, s, s, None)
                with dve.Fori(0, KF // 2 - 1) as i:
                    for s in range(2):
                        step(4 * i + (f + 4 + 2 * s), 2 * i + (2 + s), s, 2 * i + (s + 1))

            def add_to_x(k, until, scale):
                dve.wait_ge(w_done, until)
                for m in range(KD):
                    V.scalar_tensor_tensor(out=x[:, m, :], in0=ps[:, m, :], scalar=scale, in1=x[:, m, :],
                                           op0=ALU.mult, op1=ALU.add).then_inc(nrm["x"], 1)

            dve.wait_ge(s_par, 48)
            V.tensor_copy(lev8[:].rearrange("p a b c -> p (a b c)"), m32[:, 0:LEVELS * 2 * P])
            own.link(V.tensor_copy(tri8[:].rearrange("p a b -> p (a b)"), m32[:, LEVELS * 2 * P:]))
            norm(0, "h", "ffn1_norm")
            ffn_up(0, "up0")
            add_to_x(1, first["conv"], 0.5)
            norm(1, "h", "mix_norm")

            own.link(V.memset(padc[:, :, 0:2], 0.0))
            own.link(V.memset(padm[:, :, 0:1], 0.0))
            f = first["conv"]
            for j in range(NJ):
                s = j % 2
                dve.wait_ge(mx_s["c"], j + 1)
                dve.wait_ge(w_done, f + 3 * j + 2)
                own.link(V.tensor_tensor(padc[:, s, 2:T + 2], csb[:, s, :], ps[:, 3 * s + 1, :], ALU.mult))
                own.link(V.tensor_scalar(dif[:, s, :], padc[:, s, 0:T], col(par, "conv_w", j), None, ALU.mult))
                for tap in (1, 2):
                    own.link(V.scalar_tensor_tensor(out=dif[:, s, :], in0=padc[:, s, tap:T + tap],
                                                    scalar=col(par, "conv_w", 4 * tap + j), in1=dif[:, s, :],
                                                    op0=ALU.mult, op1=ALU.add))
                dve.wait_ge(w_done, f + 3 * j + 3)
                V.tensor_tensor(ya[:, j, :], dif[:, s, :], ps[:, 3 * s + 2, :], ALU.mult).then_inc(mx_s["ya"], 1)
            dve.sem_inc(mx_s["mix"], 1)
            dve.sem_inc(mx_s["mix"], 1)
            with dve.Fori(0, 7) as i:
                own.enter(i, 2)
                for s in range(2):
                    dve.wait_ge(mx_s["raw"], 2 * i + (s + 3))
                    own.link(V.tensor_tensor(dif[:, s, :], padm[:, s, 0:T], padm[:, s, 1:T + 1], ALU.subtract))
                    V.scalar_tensor_tensor(out=tile(mix, 2 * i + s), in0=dif[:, s, :], scalar=col(par, "mu_b", 2 * i + s),
                                           in1=padm[:, s, 1:T + 1], op0=ALU.mult, op1=ALU.add).then_inc(mx_s["mix"], 1)
            own.leave(7)
            dve.wait_ge(mx_s["mix"], 16)
            for j in range(NJ):
                s = j % 2
                own.link(V.tensor_scalar(kk[:, j, :], mix[:, 4 + j, :], col(par, "k_k", j), None, ALU.mult))
                if j >= 2:
                    dve.wait_ge(mx_s["kk_ss"], j - 1)
                V.tensor_tensor(dif[:, s, :], kk[:, j, :], kk[:, j, :], ALU.mult).then_inc(mx_s["kk_sq"], 1)
            for j in range(NJ):
                s = j % 2
                dve.wait_ge(mx_s["kk_root"], j + 1)
                own.link(V.tensor_scalar(csb[:, s, :], tmp[:, s, :], 1e-12, None, ALU.max))
                own.link(V.reciprocal(csb[:, s, :], csb[:, s, :]))
                own.link(V.tensor_tensor(kk[:, j, :], kk[:, j, :], csb[:, s, :], ALU.mult))
                dve.wait_ge(mx_s["lora_ev"], NJ + j + 1)
                own.link(V.tensor_scalar(csb[:, s, :], bb[:, j, :], 1.0, col(par, "k_a", j), ALU.subtract, ALU.mult))
                own.link(V.scalar_tensor_tensor(out=mix[:, 4 + j, :], in0=csb[:, s, :], scalar=1.0, in1=mix[:, 4 + j, :],
                                                op0=ALU.add, op1=ALU.mult))
                own.link(V.scalar_tensor_tensor(out=bb[:, j, :], in0=kk[:, j, :], scalar=-1.0, in1=bb[:, j, :],
                                                op0=ALU.mult, op1=ALU.mult))
                dve.sem_inc(mx_s["kk_done"], 1)

            dve.wait_ge(mx_s["kk_w"], NJ)
            dve.wait_ge(mx_s["lora_mm"], 3 * NJ)
            own.link(V.memset(scores[:], 0.0))
            own.link(V.memset(st[:], 0.0))
            own.link(V.memset(pe_[:], 1.0))
            own.link(V.memset(rinv[:], 0.0))
            dve.sem_inc(rw["s"], 1)
            PER = 4 + 4 + 3 + 1
            with dve.Fori(0, NCH) as c:
                own.enter(c, PER)
                tt = bass.ds(c * CH, CH)
                for j in range(NJ):
                    own.link(V.tensor_tensor_scan(pe_[:, j, 1:CH + 1], wd[:, j, tt], rinv[:, 0, 0:CH], 1.0, ALU.mult, ALU.add))
                own.link(V.reciprocal(rmid[:], pe_[:, :, 64:65]))
                own.link(V.tensor_tensor(pn[:], pe_[:], rmid[:].broadcast_to([P, NJ, CH + 1]), ALU.mult))
                pinv = tmp[:, 0, :].rearrange("p (j t) -> p j t", j=NJ)
                own.link(V.reciprocal(pinv, pn[:, :, 1:CH + 1]))
                own.link(V.tensor_tensor(st0[:], st[:], pe_[:, :, 64:65].broadcast_to([P, NJ, HS]), ALU.mult))
                own.link(V.tensor_tensor(ar[:, :, 0, :], kk[:, :, tt], pn[:, :, 0:CH], ALU.mult))
                own.link(V.tensor_tensor(ar[:, :, 1, :], mix[:, 0:4, tt], pn[:, :, 1:CH + 1], ALU.mult))
                own.link(V.tensor_tensor(bc[:], bb[:, :, tt], pinv, ALU.mult))
                V.tensor_tensor(kc_[:], mix[:, 4:8, tt], pinv, ALU.mult).then_inc(rw["ops"], 1)
                for h in range(HEADS):
                    dve.wait_ge(rw["mat"], HEADS * c + (h + 1))
                    dve.sem_inc(s_pass, 1)
                    V.copy_predicated(scores[:, h].rearrange("p a t -> p (a t)"), tri8[:].rearrange("p a t -> p (a t)"),
                                      ps[:, 4 + h % 4, :]).then_inc(rw["sc"], 1)
                for l in range(LEVELS):
                    for hp in range(4):
                        dve.wait_ge(rw["xmm"], 4 * LEVELS * c + (4 * l + hp + 1))
                        dve.sem_inc(s_pass, 1)
                        for e in range(2):
                            last = V.copy_predicated(xx[:, 2 * hp + e].rearrange("p a t -> p (a t)"),
                                                     lev8[:, l].rearrange("p a t -> p (a t)"),
                                                     ps[:, 4 + hp, 256 * e:256 * e + 256])
                        last.then_inc(rw["xx"], 1)
                dve.wait_ge(rw["ysmm"], c + 1)
                for e in range(2):
                    pp = slice(64 * e, 64 * e + 64)
                    V.tensor_scalar(wd[pp, :, tt], ps[pp, 4 + e, :].rearrange("p (j t) -> p j t", j=NJ), 1.0, None, ALU.mult
                                    ).then_inc(rw["y"], 1)
                own.link(V.tensor_tensor(st0[:], st0[:], ps[:, 6, 0:256].rearrange("p (j v) -> p j v", j=NJ), ALU.add))
                V.tensor_tensor(st[:], st0[:], pn[:, :, CH:CH + 1].broadcast_to([P, NJ, HS]), ALU.mult).then_inc(rw["s"], 1)
                dve.wait_ge(rw["s"], c + 2)
            own.leave(NCH)

            with dve.Fori(0, NJ) as j:
                own.enter(j, 7)
                dve.wait_ge(po["mean"], j + 1)
                own.link(V.tensor_scalar(rinv[:, 0, :], ps[:, 0, :], 1.0 / HS, None, ALU.mult))
                V.tensor_tensor(tmp[:, 0, :], tile(wd, j), rinv[:, 0, :], ALU.subtract).then_inc(po["yc"], 1)
                V.scalar_tensor_tensor(out=sq[:, 1, :], in0=tile(mix, j), scalar=col(par, "r_k", j),
                                       in1=tile(mix, j + 4), op0=ALU.mult, op1=ALU.mult).then_inc(po["rk"], 1)
                dve.wait_ge(po["bonus"], j + 1)
                own.link(V.tensor_tensor(tmp[:, 1, :], ps[:, 2, :], tile(mix, j + 8), ALU.mult))
                dve.wait_ge(po["root"], j + 1)
                own.link(V.reciprocal(rinv[:, 0, :], root[:, 0, :]))
                own.link(V.tensor_tensor(tmp[:, 0, :], tmp[:, 0, :], rinv[:, 0, :], ALU.mult))
                own.link(V.tensor_scalar(tmp[:, 0, :], tmp[:, 0, :], col(par, "ln_x_w", j), col(par, "ln_x_b", j),
                                         ALU.mult, ALU.add))
                own.link(V.tensor_tensor(tmp[:, 1, :], tmp[:, 0, :], tmp[:, 1, :], ALU.add))
                own.link(V.tensor_tensor(tmp[:, 1, :], tmp[:, 1, :], tile(gg, j), ALU.mult))
                dve.sem_inc(po["t"], 1)
                dve.wait_ge(po["hi"], j + 1)
                V.tensor_tensor(tile(yb_lo, j), tmp[:, 1, :], tile(yb_hi, j).bitcast(F32), ALU.subtract).then_inc(po["done"], 1)
            own.leave(NJ)
            for j in range(NJ):
                dve.wait_ge(po["yahi"], j + 1)
                V.tensor_tensor(ya_lo[:, j, :], ya[:, j, :], ya_hi[:, j, :].bitcast(F32), ALU.subtract).then_inc(po["ya"], 1)

            dve.wait_ge(po["ya"], NJ)
            with dve.Fori(0, KD // 2) as i:
                own.enter(i, 4)
                for half in range(2):
                    dve.wait_ge(po["sig"], 2 * i + (half + 1))
                    own.link(V.tensor_tensor(mt[:, half, 0, :], sga[:, half, 0, :], ps[:, 4 * half, :], ALU.mult))
                    own.link(V.tensor_tensor(mt[:, half, 1, :], sga[:, half, 1, :], ps[:, 4 * half + 1, :], ALU.mult))
                    V.tensor_tensor(mt[:, half, 1, :], mt[:, half, 0, :], mt[:, half, 1, :], ALU.add).then_inc(po["mg_t"], 1)
                    dve.wait_ge(po["mg_hi"], 2 * i + (half + 1))
                    V.tensor_tensor(tile(mg_lo, 2 * i + half), mt[:, half, 1, :], tile(mg_hi, 2 * i + half).bitcast(F32),
                                    ALU.subtract).then_inc(po["mg"], 1)
            own.leave(KD // 2)
            add_to_x(2, first["up1"], 1.0)
            norm(2, "h", "ffn2_norm")
            ffn_up(1, "up1")
            add_to_x(3, first["pair0"], 0.5)
            norm(3, "x", "final_norm")
            norm(4, "h", "even_norm_2")

            def pairs(name, ls):
                f = first[name]
                with dve.Fori(0, 4) as i:
                    for s in range(2):
                        dve.wait_ge(w_done, 4 * i + (f + 2 * s + 1))
                        V.tensor_scalar(tile(left, 2 * i + s), ps[:, 2 * s, :], 1.0, None, ALU.mult).then_inc(ls, 1)

            pairs("pair0", ev["l0"])
            for g in range(4):
                for e in range(2):
                    dve.wait_ge(ev["sqmm"], 2 * g + e + 1)
                    if g >= 1:
                        dve.wait_ge(ev["fwmm"], 2 * g)
                    V.tensor_copy(fmix[:, e, :], ps[:, 4 + e, :]).then_inc(ev["fmix"], 1)
                for e in range(2):
                    m = 2 * g + e
                    dve.wait_ge(ev["fwmm"], m + 1)
                    if m == 0:
                        dve.wait_ge(ev["r0"], KD)
                    if g >= 1:
                        dve.wait_ge(ev["z"], m - 1)
                    V.tensor_tensor(tmp[:, e, :], ps[:, 6 + e, :], right[:, m, :], ALU.mult).then_inc(ev["t"], 1)
                    dve.wait_ge(ev["hi"], m + 1)
                    V.tensor_tensor(z_lo[:, m, :], tmp[:, e, :], z_hi[:, m, :].bitcast(F32), ALU.subtract).then_inc(ev["z"], 1)
            add_to_x(5, first["pair1"], 1.0)
            pairs("pair1", ev["l1"])

            def head_prep(u, src, gain, out):
                dve.wait_ge(at["root"], u + 1)
                own.link(V.reciprocal(rinv[:, 0, :], root[:, 0, :]))
                V.scalar_tensor_tensor(out=tmp[:, 0, :], in0=src, scalar=gain, in1=rinv[:, 0, :],
                                       op0=ALU.mult, op1=ALU.mult).then_inc(at["qn"], 1)
                dve.wait_ge(at["rot"], u + 1)
                own.link(V.tensor_tensor(sq[:, 1, :], ps[:, 1, :], rope_s[:, 1, :], ALU.mult))
                own.link(V.tensor_tensor(tmp[:, 0, :], tmp[:, 0, :], rope_s[:, 0, :], ALU.mult))
                V.tensor_tensor(out, tmp[:, 0, :], sq[:, 1, :], ALU.add).then_inc(at["qr"], 1)

            for u in range(2):
                head_prep(u, kt[:, u, :], col(par, "k_gain_2"), kt[:, u, :])
            for g in range(2):
                with dve.Fori(0, 4) as i:
                    own.enter(i, 3 + 2 * QT)
                    hq = i + 4 * g
                    head_prep(i + (2 + 4 * g), tile(left, hq), col(par, "q_gain_2"), qr[:, 0, :])
                    for t in range(QT):
                        dve.wait_ge(at["smm"], QT * hq + (t + 1))
                        own.link(V.tensor_reduce(mx[:, 8 + t:9 + t], ps[:, 4 + t, :], AX_X, ALU.max))
                        V.tensor_scalar(mx[:, t:t + 1], mx[:, 8 + t:9 + t], -(P ** -0.5), None, ALU.mult).then_inc(at["max"], 1)
                    for t in range(QT):
                        dve.wait_ge(at["exp"], QT * hq + (t + 1))
                        own.link(V.reciprocal(mx[:, 12 + t:13 + t], mx[:, 4 + t:5 + t]))
                        V.tensor_scalar(prob[:, t, :], prob[:, t, :], mx[:, 12 + t:13 + t], None, ALU.mult).then_inc(at["prob"], 1)
                    dve.wait_ge(at["tr"], hq + 1)
                    for t in (1, 3):
                        V.tensor_copy(probT[:, t, :], ps[:, t, :]).then_inc(at["pt"], 1)
                    dve.wait_ge(at["pv"], hq + 1)
                    V.tensor_tensor(tmp[:, 1, :], ps[:, 4, :], tile(right, hq), ALU.mult).then_inc(at["t"], 1)
                    dve.wait_ge(at["hi"], hq + 1)
                    V.tensor_tensor(tile(z_lo, hq), tmp[:, 1, :], tile(z_hi, hq).bitcast(F32), ALU.subtract).then_inc(at["z"], 1)
                own.leave(4)
            dve.wait_ge(w_done, first["rnn"])
            for m in range(KD):
                V.tensor_tensor(x[:, m, :], ps[:, m, :], x[:, m, :], ALU.add).then_inc(nrm["x"], 1)
            norm(5, "h", "odd_norm_2")

            lm = par[:, COLS["rglru_lambda_2"]:COLS["rglru_lambda_2"] + 32]
            own.link(V.tensor_scalar(lam[:, 0, :], lm, -1.0, None, ALU.mult))
            own.link(V.tensor_tensor(lam[:, 0, :], lam[:, 0, :], lm, ALU.max))
            own.link(V.memset(xp[:], 0.0))
            dve.sem_inc(rg["lexp"], 1)
            dve.wait_ge(rg["lexp"], 2)
            own.link(V.tensor_scalar(lam[:, 2, :], lam[:, 1, :], 2.0, None, ALU.add))
            own.link(V.reciprocal(lam[:, 2, :], lam[:, 2, :]))
            own.link(V.tensor_tensor(lam[:, 2, :], lam[:, 2, :], lam[:, 1, :], ALU.mult))
            own.link(V.tensor_tensor(lam[:, 3, :], lam[:, 2, :], lam[:, 2, :], ALU.mult))
            own.link(V.tensor_scalar(lam[:, 4, :], lam[:, 3, :], 1.0 / 17, 1.0 / 15, ALU.mult, ALU.add))
            for k in (13, 11, 9, 7, 5, 3, 1):
                own.link(V.tensor_tensor(lam[:, 4, :], lam[:, 4, :], lam[:, 3, :], ALU.mult))
                own.link(V.tensor_scalar(lam[:, 4, :], lam[:, 4, :], 1.0 / k, None, ALU.add))
            own.link(V.tensor_tensor(lam[:, 4, :], lam[:, 4, :], lam[:, 2, :], ALU.mult))
            own.link(V.tensor_scalar(lam[:, 5, :], lm, -1.0, 0.0, ALU.mult, ALU.max))
            own.link(V.scalar_tensor_tensor(out=lam[:, 5, :], in0=lam[:, 4, :], scalar=2.0, in1=lam[:, 5, :],
                                            op0=ALU.mult, op1=ALU.add))
            own.link(V.tensor_scalar(lam[:, 5, :], lam[:, 5, :], 8.0, None, ALU.mult))

            dve.sem_inc(rg["z"], 1)
            dve.sem_inc(rg["y"], 1)
            with dve.Fori(0, NRB // 2) as i:
                own.enter(i, 2 * (4 + 2 * 5 + 1 + 1))
                for s in range(2):
                    b = 2 * i + s
                    dve.wait_ge(rg["x"], b + 3)
                    own.link(V.tensor_scalar(xc[:, s, :], xp[:, s, 0:T], col(par, "conv_w_2", b), col(par, "conv_b_2", b),
                                             ALU.mult, ALU.add))
                    for tap in range(1, 4):
                        ins = V.scalar_tensor_tensor(out=xc[:, s, :], in0=xp[:, s, tap:T + tap],
                                                     scalar=col(par, "conv_w_2", b + 16 * tap), in1=xc[:, s, :],
                                                     op0=ALU.mult, op1=ALU.add)
                        own.link(ins)
                    dve.sem_inc(rg["xc"], 1)
                for s in range(2):
                    b = 2 * i + s
                    dve.wait_ge(rg["ri"], 4 * b + 8)
                    for d in range(2):
                        V.tensor_scalar(ri[:, 2 * d, :], ri[:, 2 * d, :], lam[:, 5, bass.ds(b + 16 * d, 1)], None, ALU.mult
                                        ).then_inc(rg["nla"], 1)
                        own.link(V.tensor_tensor(ri[:, 2 * d + 1, :], ri[:, 2 * d + 1, :], xc[:, s, :], ALU.mult))
                    for d in range(2):
                        dve.wait_ge(rg["a"], 2 * b + (d + 1))
                        own.link(V.tensor_tensor(hh[:, d, :], aa[:, d, :], aa[:, d, :], ALU.mult))
                        dve.wait_ge(rg["th"], 2 * b + (d + 1))
                        own.link(V.scalar_tensor_tensor(out=th[:, d, :], in0=hh[:, d, :], scalar=1.0, in1=th[:, d, :],
                                                        op0=ALU.add, op1=ALU.mult))
                        dve.sem_inc(rg["w"], 1)
                    for d in range(2):
                        dve.wait_ge(rg["root"], 2 * b + (d + 1))
                        own.link(V.tensor_tensor(uu[:, d, :], uu[:, d, :], ri[:, 2 * d + 1, :], ALU.mult))
                        if d == 0:
                            own.link(V.tensor_tensor_scan(hh[:, 0, :], aa[:, 0, :], uu[:, 0, :], 0.0, ALU.mult, ALU.add))
                        else:
                            own.link(V.tensor_tensor_scan(hh[:, 1, ::-1], aa[:, 1, ::-1], uu[:, 1, ::-1], 0.0, ALU.mult, ALU.add))
                    dve.sem_inc(rg["y"], 1)
                    own.link(V.tensor_tensor(hh[:, 0, :], hh[:, 0, :], hh[:, 1, :], ALU.add))
                    own.link(V.tensor_tensor(hh[:, 1, :], hh[:, 0, :], sgate[:, s, :], ALU.mult))
                    dve.sem_inc(rg["t"], 1)
                    dve.wait_ge(rg["hi"], b + 1)
                    V.tensor_tensor(tile(y_lo, b), hh[:, 1, :], tile(y_hi, b).bitcast(F32), ALU.subtract).then_inc(rg["z"], 1)
            own.leave(NRB // 2)
            add_to_x(6, NBLOCKS, 1.0)
            norm(6, "out", "final_norm_2")


def weight_stream(w):
    import numpy as np

    def by_output(m, cols):
        k = m.shape[0] // 128
        return m[:, cols].reshape(k, 128, -1, 128).transpose(2, 1, 0, 3)

    def by_input(m):
        return m.reshape(m.shape[0] // 128, 128, 8, 128)

    def turns(*parts):
        return np.stack(parts, 1).reshape(-1, 128, 8, 128)

    c = slice
    w_in = w["w_in"][0]
    conv, rwkv = 3 * 512, 3 * 512 + 1792
    even = w["even_w_in_2"][0]
    odd = w["odd_w_in_2"][0]
    oa, ob = by_output(w["w_out_a"][0], c(None)), by_output(w["w_out_b"][0], c(None))
    out_ab = np.concatenate([oa, ob], axis=2)
    v = even[:, 3328:3584].reshape(2, 4, 128, 256).transpose(0, 2, 1, 3).reshape(2, 128, 8, 128)
    parts = [
        turns(by_output(w["ffn1_w_gate"][0], c(None)), by_output(w["ffn1_w_up"][0], c(None))),
        by_input(w["ffn1_w_down"][0]),
        turns(by_output(w_in, c(512, 1024)), by_output(w_in, c(1024, 1536)), by_output(w_in, c(0, 512))),
        by_output(w_in, c(conv, rwkv)),
        turns(out_ab, by_output(w_in, c(rwkv, rwkv + 1024)), by_output(w_in, c(rwkv + 1024, rwkv + 2048))),
        by_input(w["w_o"][0]),
        turns(by_output(w["ffn2_w_gate"][0], c(None)), by_output(w["ffn2_w_up"][0], c(None))),
        by_input(w["ffn2_w_down"][0]),
        turns(by_output(even, c(0, 1024)), by_output(even, c(1024, 2048))),
        by_input(w["even_w_out_2"][0])[:8],
        turns(by_output(even, c(2048, 3072)), by_output(even, c(3584, 4608))),
        by_output(even, c(3072, 3328)),
        v,
        by_input(w["even_w_out_2"][0])[8:],
        turns(by_output(odd, c(0, 2048)), by_output(odd, c(2048, 4096))),
        by_input(w["odd_w_out_2"][0]),
    ]
    return np.ascontiguousarray(np.concatenate([p.reshape(-1, 128, 1024) for p in parts]))


def constants():
    import numpy as np

    f = np.float32
    bones = np.kron(np.eye(2), np.ones((64, 64)))
    perm = np.zeros((128, 128))
    for half in (0, 64):
        for i in range(32):
            perm[half + i + 32, half + i] = -1.0
            perm[half + i, half + i + 32] = 1.0
    mats = np.stack([np.ones((128, 128)), bones, np.eye(128), perm], 1).astype(f)
    r, q = np.arange(128)[:, None], np.arange(128)[None, :]
    levels = []
    for l in range(7):
        low = (r // (2 << l) == q // (2 << l)) & (r // (1 << l) > q // (1 << l))
        levels += [low, low.T]
    tri = [r < q, r <= q, r < q, r <= q]
    masks = np.stack(levels + tri, 1).reshape(128, -1).astype(np.int32)
    inv = (f(10000.0) ** (-np.arange(0, 64, 2, dtype=f) / f(64))).astype(f)
    t = np.arange(512)
    ang = np.stack([(t // 64).astype(f)[:, None] * inv, (t % 64).astype(f)[:, None] * inv])
    full = np.concatenate([ang[0].T, ang[0].T, ang[1].T, ang[1].T])
    rope = np.stack([np.cos(full.astype(np.float64)), np.sin(full.astype(np.float64))], 1).astype(f)
    ch = 2 * np.pi * np.outer(np.arange(256), np.arange(256)) / 256
    sq = 2 * np.pi * np.outer(np.arange(512), np.arange(512)) / 512
    dft_c = np.concatenate([np.cos(ch), -np.sin(ch)], 1) / 16.0
    dft_s = np.concatenate([np.cos(sq), np.sin(sq)], 0) / np.sqrt(512.0)
    dft_c = dft_c.reshape(2, 128, 512).transpose(1, 0, 2).astype(f)
    dft_s = dft_s.reshape(8, 128, 512).transpose(1, 0, 2).astype(f)
    return mats, masks, rope, dft_c, dft_s


def kernel(**inputs):
    import numpy as np
    import concourse.bacc as bacc
    from concourse.bass_utils import run_bass_kernel_spmd

    w = {k: np.asarray(v) for k, v in inputs.items()}
    par = np.zeros((NCOLS, 128), np.float32)
    for name, at in COLS.items():
        if name in w:
            v = w[name].reshape(-1, 128)
            par[at:at + v.shape[0]] = v
    par[COLS["eps_rms"]], par[COLS["eps_gn"]] = 1e-6, 64e-5
    mats, masks, rope, dft_c, dft_s = constants()
    gates = np.stack([w["gate_a_w_2"][0, 0], w["gate_x_w_2"][0, 0], w["gate_a_w_2"][0, 1], w["gate_x_w_2"][0, 1]])
    gates = gates.transpose(1, 2, 0, 3)
    gates = np.concatenate([gates, gates[:2]])
    fw = w["fourier_w_2"][0].reshape(4, 2, 128, 2, 128).transpose(2, 0, 1, 3, 4).reshape(128, 16, 128)
    arrays = {
        "xT": w["x"][0].T.reshape(8, 128, 512).transpose(1, 0, 2),
        "wstream": weight_stream(w),
        "params": par.T,
        "mats": mats,
        "masks": masks,
        "lora": np.concatenate([w["w_decay_up"][0], w["w_iclr_up"][0]], 0),
        "gup": w["w_gate_up"][0],
        "rope": rope,
        "dft_c": dft_c,
        "dft_s": dft_s,
        "fw": fw,
        "rgates": gates,
    }
    from concourse import mybir as mb
    nc = bacc.Bacc("TRN2", target_bir_lowering=False, num_devices=1)
    aps, feed = [], {}
    for name, a in arrays.items():
        feed[name] = np.ascontiguousarray(a)
        aps.append(nc.dram_tensor(name, a.shape, mb.dt.from_np(a.dtype), kind="ExternalInput").ap())
    aps.append(nc.dram_tensor("outT", (128, 8, 512), mb.dt.float32, kind="ExternalOutput").ap())
    program(nc, *aps)
    got = run_bass_kernel_spmd(nc, [feed], core_ids=[0]).results[0]["outT"]
    return np.ascontiguousarray(got.transpose(1, 0, 2).reshape(1024, 512).T).reshape(1, 512, 1024)
```

```python
from contextlib import ExitStack

import concourse.bass as bass
from concourse import mybir

ACT = mybir.ActivationFunctionType
ALU = mybir.AluOpType
AX_X = mybir.AxisListType.X
F32 = mybir.dt.float32
FR = mybir.dt.float32r
I32 = mybir.dt.int32
I8 = mybir.dt.int8

P = 128
T = 512
D = 1024
KD = D // P
KF = 2816 // P
BLK = 8
HEADS, HS = 8, 64
NJ = HEADS * HS // P
CH = 128
NCH = T // CH
LEVELS = 7
QT = T // P
NRB = 16
INV_SQRT_E = 0.6065306597126334

COLS = {}
_at = 0
for _name, _n in (
    ("ffn1_norm", 8), ("mix_norm", 8), ("ffn2_norm", 8), ("final_norm", 8), ("even_norm_2", 8),
    ("odd_norm_2", 8), ("final_norm_2", 8), ("conv_w", 12), ("mu_b", 14), ("w0", 4), ("a0", 4),
    ("k_k", 4), ("k_a", 4), ("r_k", 4), ("ln_x_w", 4), ("ln_x_b", 4), ("q_gain_2", 1), ("k_gain_2", 1),
    ("conv_w_2", 64), ("conv_b_2", 16), ("gate_a_b_2", 32), ("gate_x_b_2", 32), ("rglru_lambda_2", 32),
    ("eps_rms", 1), ("eps_gn", 1),
):
    COLS[_name] = _at
    _at += _n
NCOLS = _at

N_UP, N_DOWN = 2 * KF, KF
N_CONV, N_MIX, N_MERGE, N_WO = 12, 14, 24, 8
N_PAIR, N_KV, N_HALF, N_RNN = 16, 4, 8, 32
NBLOCKS = 2 * (N_UP + N_DOWN) + N_CONV + N_MIX + N_MERGE + N_WO + 2 * N_PAIR + N_KV + 2 * N_HALF + N_RNN + 16


def col(par, name, i=0, n=1):
    return par[:, bass.ds(COLS[name] + i, n)]


def tile(buf, i):
    return buf[:, bass.ds(i, 1), :].rearrange("p a t -> p (a t)")


class Chain:

    def __init__(self, eng, sem):
        self.eng, self.sem, self.base, self.k, self.at = eng, sem, 0, 0, None

    def link(self, ins):
        ins.then_inc(self.sem, 1)
        self.k += 1
        self.eng.wait_ge(self.sem, self.base + self.k if self.at is None else self.at + (self.base + self.k))

    def enter(self, i, per):
        self.base, self.k, self.per, self.at = self.base + self.k, 0, per, i * per

    def leave(self, trips):
        assert self.k == self.per, (self.k, self.per)
        self.base, self.k, self.at = self.base + trips * self.per, 0, None


def program(nc, xT, wstream, params, mats, masks, lora, gup, rope, dft_c, dft_s, fw, rgates, outT):
    with ExitStack() as ctx:
        def sb(name, shape, dt=F32, on=ctx):
            return on.enter_context(nc.sbuf_tensor(name, shape, dt))

        def sem(name):
            return ctx.enter_context(nc.semaphore(name))

        ps = ctx.enter_context(nc.psum_tensor("ps", [P, 8, T], F32))

        x = sb("x", [P, KD, T])
        w_raw = sb("w_raw", [P, 2, BLK * P])
        w_hi = sb("w_hi", [P, 2, BLK * P], FR)
        w_lo = sb("w_lo", [P, 2, BLK * P], FR)
        par = sb("par", [P, NCOLS])
        mat = sb("mat", [P, 4, P])
        ones, bones, ident, perm = (mat[:, k, :] for k in range(4))
        lev8 = sb("lev8", [P, LEVELS, 2, P], I8)
        tri8 = sb("tri8", [P, 4, P], I8)
        sq = sb("sq", [P, 2, T])
        root = sb("root", [P, 1, T])
        rinv = sb("rinv", [P, 1, T])
        tmp = sb("tmp", [P, 2, T])
        h_hi = sb("h_hi", [P, KD, T], FR)
        h_lo = sb("h_lo", [P, KD, T], FR)

        with ExitStack() as a:
            hid_hi = sb("hid_hi", [P, KF, T], FR, a)
            hid_lo = sb("hid_lo", [P, KF, T], FR, a)
            gate_s = sb("gate_s", [P, 2, T], F32, a)
            hid_t = sb("hid_t", [P, 2, T], F32, a)
            m32 = sb("m32", [P, (LEVELS * 2 + 4) * P], I32, a)
        with ExitStack() as a:
            scores = sb("scores", [P, HEADS, 4, P], F32, a)
            xx = sb("xx", [P, HEADS, 2, P], F32, a)
            t1 = sb("t1", [P, HEADS, P], F32, a)
            ar = sb("ar", [P, NJ, 2, CH], F32, a)
            bc = sb("bc", [P, NJ, CH], F32, a)
            kc_ = sb("kc_", [P, NJ, CH], F32, a)
            tok = sb("tok", [P, 3, T], F32, a)
            st = sb("st", [P, NJ, HS], F32, a)
            st0 = sb("st0", [P, NJ, HS], F32, a)
            pe_ = sb("pe_", [P, NJ, CH + 1], F32, a)
            pn = sb("pn", [P, NJ, CH + 1], F32, a)
            rmid = sb("rmid", [P, NJ, 1], F32, a)
            ya = sb("ya", [P, NJ, T], F32, a)
            mix = sb("mix", [P, 14, T], F32, a)
            wd = sb("wd", [P, NJ, T], F32, a)
            kk = sb("kk", [P, NJ, T], F32, a)
            bb = sb("bb", [P, NJ, T], F32, a)
            gg = sb("gg", [P, NJ, T], F32, a)
        with ExitStack() as a:
            padc = sb("padc", [P, 2, T + 2], F32, a)
            csb = sb("csb", [P, 2, T], F32, a)
            padm = sb("padm", [P, 2, T + 1], F32, a)
            dif = sb("dif", [P, 2, T], F32, a)
            lora_s = sb("lora_s", [P, T], F32, a)
            gup_s = sb("gup_s", [P, T], F32, a)
        with ExitStack() as a:
            ya_hi = sb("ya_hi", [P, NJ, T], FR, a)
            ya_lo = sb("ya_lo", [P, NJ, T], FR, a)
            yb_hi = sb("yb_hi", [P, NJ, T], FR, a)
            yb_lo = sb("yb_lo", [P, NJ, T], FR, a)
            gap = sb("gap", [P, 13, T], F32, a)
            mg_hi = sb("mg_hi", [P, KD, T], FR, a)
            mg_lo = sb("mg_lo", [P, KD, T], FR, a)
            sga = sb("sga", [P, 2, 2, T], F32, a)
            mt = sb("mt", [P, 2, 2, T], F32, a)
        with ExitStack() as a:
            z_hi = sb("z_hi", [P, KD, T], FR, a)
            z_lo = sb("z_lo", [P, KD, T], FR, a)
            left = sb("left", [P, KD, T], F32, a)
            right = sb("right", [P, KD, T], F32, a)
            with ExitStack() as b:
                dftc = sb("dftc", [P, 2, T], F32, b)
                dfts = sb("dfts", [P, 2 * QT, T], F32, b)
                fws = sb("fws", [P, 16, P], F32, b)
                chan = sb("chan", [P, QT, T], F32, b)
                fmix = sb("fmix", [P, 2, T], F32, b)
            with ExitStack() as b:
                kt = sb("kt", [P, 2, T], F32, b)
                vt = sb("vt", [P, QT, 256], F32, b)
                rope_s = sb("rope_s", [P, 2, T], F32, b)
                prob = sb("prob", [P, 2, QT, T], F32, b)
                probT = sb("probT", [P, QT, T], F32, b)
                qr = sb("qr", [P, 2, T], F32, b)
                mx = sb("mx", [P, 36], F32, b)
        with ExitStack() as a:
            y_hi = sb("y_hi", [P, NRB, T], FR, a)
            y_lo = sb("y_lo", [P, NRB, T], FR, a)
            rg_w = sb("rg_w", [P, 2, 4, P], F32, a)
            xp = sb("xp", [P, 2, T + 3], F32, a)
            xc = sb("xc", [P, 2, T], F32, a)
            sgate = sb("sgate", [P, 2, T], F32, a)
            ri = sb("ri", [P, 2, 4, T], F32, a)
            aa = sb("aa", [P, 2, 2, T], F32, a)
            th = sb("th", [P, 2, 2, T], F32, a)
            lam = sb("lam", [P, 6, 32], F32, a)

        s_x = sem("x_loaded")
        s_par = sem("params_loaded")
        landed = [sem(f"weights_landed_{s}") for s in range(2)]
        w_hi_done = sem("w_hi_done")
        w_split = sem("w_split")
        w_done = sem("w_done")
        v_chain = sem("vector_chain")
        a_chain = sem("scalar_chain")
        s_pass = sem("vector_passed")
        s_act_pass = sem("scalar_passed")
        s_pool_pass = sem("pool_passed")
        nrm = {q: sem(f"norm_{q}") for q in ("x", "sq", "acc", "ss", "root", "hi", "h")}

        def x_at(k):
            return KD * (k - 1 if k < 5 else k)

        def h_at(k):
            return KD * (k if k < 3 else k - 1)

        ffn = [{q: sem(f"ffn{k}_{q}") for q in ("g", "u", "silu", "t", "hi", "hid")} for k in range(2)]
        mx_s = {q: sem(f"mixer_{q}") for q in (
            "small_loaded", "ya", "raw", "mix", "lora_in", "lora_mm", "lora_ev", "kk_sq", "kk_ss", "kk_root", "kk_done", "kk_w")}
        rw = {q: sem(f"rwkv_{q}") for q in (
            "ops", "vc", "reset", "tr", "tok", "mat", "sc", "t1mm", "t1", "xmm", "xx", "rhsmm", "rhs", "umm", "u",
            "ysmm", "y", "s")}
        po = {q: sem(f"post_{q}") for q in (
            "mean", "yc", "sq", "var", "root", "rk", "bonus", "t", "hi", "done", "yahi", "ya", "g", "sig", "mg_t", "mg_hi", "mg")}
        ev = {q: sem(f"even_{q}") for q in ("loaded", "l0", "g0", "r0", "l1", "g1", "r1", "k", "col", "v", "chmm", "chan", "sqmm",
                                             "fmix", "fwmm", "t", "hi", "z")}
        at = {q: sem(f"attn_{q}") for q in ("rope", "sq", "ssmm", "root", "qn", "rot", "qr", "smm", "max", "exp", "prob",
                                             "tr", "pt", "pv", "t", "hi", "z")}
        rg = {q: sem(f"rglru_{q}") for q in ("w0", "w1", "x", "g", "sg", "lexp", "xc", "gmm", "ri", "nla", "a", "a2", "th",
                                              "w", "root", "y", "t", "hi", "z")}
        s_bank = sem("residual_bank_done")
        s_out_t = sem("out_tile")
        s_out = sem("out_stored")

        block = ctx.enter_context(nc.Block())

        first = {}
        n = 0
        for name, size in (("up0", N_UP), ("down0", N_DOWN), ("conv", N_CONV), ("mix", N_MIX), ("merge", N_MERGE),
                           ("wo", N_WO), ("up1", N_UP), ("down1", N_DOWN), ("pair0", N_PAIR), ("eo0", N_HALF),
                           ("pair1", N_PAIR), ("kv", N_KV), ("eo1", N_HALF), ("rnn", N_RNN), ("ro", 16)):
            first[name] = n
            n += size
        assert n == NBLOCKS and NBLOCKS % 2 == 0

        @block.sync
        def _(sp):
            sp.dma_start(x[:], xT).then_inc(s_x, 16)
            for s in range(2):
                sp.dma_start(w_raw[:, s, :], wstream[s]).then_inc(landed[s], 16)
            sp.dma_start(par[:], params).then_inc(s_par, 16)
            sp.dma_start(mat[:], mats).then_inc(s_par, 16)
            sp.dma_start(m32[:], masks).then_inc(s_par, 16)
            with sp.Fori(0, NBLOCKS // 2 - 1) as i:
                for s in range(2):
                    sp.wait_ge(w_split, 2 * i + (s + 1))
                    sp.dma_start(w_raw[:, s, :], wstream[bass.ds(2 * i + (2 + s), 1)].rearrange("a p q -> p (a q)")
                                 ).then_inc(landed[s], 16)
            for m in range(KD):
                sp.wait_ge(s_out_t, m + 1)
                sp.dma_start(outT[:, m, :], x[:, m, :]).then_inc(s_out, 16)
            sp.wait_ge(s_out, 16 * KD)

        @block.gpsimd
        def _(pool):
            def split(s):
                nc.gpsimd.tensor_scalar(w_hi[:, s, :], w_raw[:, s, :], 1.0, 0.0, ALU.mult, ALU.add).then_inc(w_hi_done, 1)

            def rest(s):
                nc.gpsimd.tensor_tensor(w_lo[:, s, :], w_raw[:, s, :], w_hi[:, s, :].bitcast(F32), ALU.subtract
                                        ).then_inc(w_split, 1)

            for s in range(2):
                pool.wait_ge(landed[s], 16)
                split(s)
                pool.wait_ge(w_hi_done, s + 1)
                rest(s)
            with pool.Fori(0, NBLOCKS // 2 - 1) as i:
                for s in range(2):
                    pool.wait_ge(landed[s], 16 * i + 32)
                    pool.wait_ge(w_done, 2 * i + (s + 1))
                    pool.sem_inc(s_pool_pass, 1)
                    split(s)
                    pool.wait_ge(w_hi_done, 2 * i + (s + 3))
                    rest(s)

        @block.tensor
        def _(pe):
            mm = nc.tensor.matmul

            def mm3(out, s, k, hi, lo, start, stop, n=P):
                w = slice(k * n, (k + 1) * n)
                mm(out, w_hi[:, s, w], hi, start=start, stop=False)
                mm(out, w_hi[:, s, w], lo, start=False, stop=False)
                return mm(out, w_lo[:, s, w], hi, start=False, stop=stop)

            def dense(n, s, bank, hi, lo):
                pe.wait_ge(w_split, n + 1)
                for k in range(BLK):
                    last = mm3(ps[:, bank, :], s, k, hi[:, k, :], lo[:, k, :], k == 0, k == BLK - 1)
                last.then_inc(w_done, 1)

            def sum_squares(k):
                pe.wait_ge(nrm["acc"], (KD - 1) * (k + 1))
                mm(ps[:, 7, :], ones, root[:, 0, :], start=True, stop=True).then_inc(nrm["ss"], 1)

            def dense_first(k, n):
                pe.wait_ge(w_split, n + 1)
                for m in range(KD):
                    pe.wait_ge(nrm["h"], h_at(k) + m + 1)
                    last = mm3(ps[:, 0, :], 0, m, h_hi[:, m, :], h_lo[:, m, :], m == 0, m == KD - 1)
                last.then_inc(w_done, 1)

            def residual(name, nk, hi, lo, ready):
                def step(n, s, k, start, stop):
                    pe.wait_ge(w_split, n + 1)
                    for m in range(KD):
                        last = mm3(ps[:, m, :], s, m, tile(hi, k), tile(lo, k), start, stop)
                        if stop and m < KD - 1:
                            last.then_inc(s_bank, 1)
                    last.then_inc(w_done, 1)
                f = first[name]
                ready()
                for k in range(2):
                    step(f + k, k, k, k == 0, False)
                with pe.Fori(0, nk // 2 - 2) as i:
                    for s in range(2):
                        step(2 * i + (f + 2 + s), s, 2 * i + (2 + s), False, False)
                for k in range(nk - 2, nk):
                    step(f + k, k % 2, k, False, k == nk - 1)

            def ffn_up(k, name):
                q = ffn[k]
                f = first[name]
                dense_first(2 * k, f)
                dense(f + 1, 1, 1, h_hi, h_lo)
                sum_squares(2 * k)
                for s in range(2, 4):
                    dense(f + s, s % 2, s, h_hi, h_lo)
                with pe.Fori(0, KF // 2 - 1) as i:
                    for s in range(4):
                        pe.wait_ge(q["u"] if s % 2 else q["g"], 2 * i + (s // 2 + 1))
                        dense(4 * i + (f + 4 + s), s % 2, s, h_hi, h_lo)

            pe.wait_ge(s_par, 48)
            ffn_up(0, "up0")
            residual("down0", KF, hid_hi, hid_lo, lambda: pe.wait_ge(ffn[0]["hid"], KF))

            f = first["conv"]
            dense_first(1, f)
            dense(f + 1, 1, 1, h_hi, h_lo)
            sum_squares(1)
            for s in range(2, 6):
                dense(f + s, s % 2, s, h_hi, h_lo)
            for s in range(6, 12):
                if s % 3 == 0:
                    pe.wait_ge(mx_s["ya"], s // 3 - 1)
                dense(f + s, s % 2, s % 6, h_hi, h_lo)
            f = first["mix"]
            with pe.Fori(0, 7) as i:
                for s in range(2):
                    if s == 0:
                        pe.wait_ge(mx_s["raw"], 2 * i + 1)
                    else:
                        pe.wait_ge(mx_s["raw"], 2 * i + 2)
                    dense(2 * i + (f + s), s, 6 + s, h_hi, h_lo)
            pe.wait_ge(mx_s["small_loaded"], 32)
            pe.wait_ge(mx_s["lora_in"], 3)
            pe.wait_ge(mx_s["ya"], NJ)
            pe.wait_ge(mx_s["raw"], 16)
            for j in range(NJ):
                w = slice(j * P, (j + 1) * P)
                mm(ps[:, j, :], lora_s[0:64, w], sq[0:64, 0, :], start=True, stop=True).then_inc(mx_s["lora_mm"], 1)
            for j in range(NJ):
                w = slice(j * P, (j + 1) * P)
                mm(ps[:, 4 + j, :], lora_s[64:128, w], tmp[64:128, 0, :], start=True, stop=True).then_inc(mx_s["lora_mm"], 1)
            for j in range(NJ):
                w = slice(j * P, (j + 1) * P)
                pe.wait_ge(mx_s["lora_ev"], j + 1)
                mm(ps[:, j, :], gup_s[:, w], sq[:, 1, :], start=True, stop=True).then_inc(mx_s["lora_mm"], 1)
            for j in range(NJ):
                pe.wait_ge(mx_s["kk_sq"], j + 1)
                pe.wait_ge(mx_s["lora_ev"], 5 + j)
                mm(ps[:, 4 + j, :], bones, dif[:, j % 2, :], start=True, stop=True).then_inc(mx_s["kk_ss"], 1)

            pe.wait_ge(mx_s["lora_ev"], 12)
            pe.wait_ge(mx_s["kk_root"], NJ)
            with pe.Fori(0, NCH) as c:
                pe.wait_ge(rw["ops"], c + 1)
                pe.wait_ge(rw["vc"], c + 1)
                for q, src in enumerate((bc, kc_, root)):
                    for j in range(NJ):
                        w = slice(j * P, (j + 1) * P)
                        a = src[:, j, :] if q < 2 else root[:, 0, w]
                        last = nc.tensor.transpose(ps[:, q, w], a, ident)
                    last.then_inc(rw["tr"], 1)
                for h in range(HEADS):
                    j, p0 = h // 2, HS * (h % 2)
                    pp = slice(p0, p0 + HS)
                    bank = 4 + h % 4
                    if h >= 4:
                        pe.wait_ge(rw["sc"], HEADS * c + (h - 3))
                    mm(ps[:, bank, 0:256], bc[pp, j, :], ar[pp, j, :, :].rearrange("p a t -> p (a t)"), start=True, stop=True)
                    mm(ps[:, bank, 256:512], kc_[pp, j, :], ar[pp, j, :, :].rearrange("p a t -> p (a t)"),
                       start=True, stop=True).then_inc(rw["mat"], 1)
                pe.wait_ge(rw["reset"], c + 1)
                pe.wait_ge(rw["tok"], 3 * c + 3)
                pe.wait_ge(rw["sc"], HEADS * c + HEADS)
                for l in range(LEVELS):
                    for g in range(2):
                        if l >= 1:
                            pe.wait_ge(rw["xx"], 4 * LEVELS * c + (4 * (l - 1) + 2 * g + 2))
                        for h in range(4 * g, 4 * g + 4):
                            last = mm(ps[:, g, (h % 4) * P:(h % 4 + 1) * P], scores[:, h, 0, :], xx[:, h, 0, :],
                                      start=True, stop=True)
                        last.then_inc(rw["t1mm"], 1)
                    for g in range(2):
                        pe.wait_ge(rw["t1"], 2 * LEVELS * c + (2 * l + g + 1))
                        for h in range(4 * g, 4 * g + 4):
                            bank, o = 4 + h // 2, 256 * (h % 2)
                            mm(ps[:, bank, o:o + P], xx[:, h, 1, :], t1[:, h, :], start=True, stop=True)
                            last = mm(ps[:, bank, o + P:o + 2 * P], t1[:, h, :], xx[:, h, 1, :], start=True, stop=True)
                            if h % 2 == 1:
                                last.then_inc(rw["xmm"], 1)
                pe.wait_ge(rw["xx"], 4 * LEVELS * c + 4 * LEVELS)
                for h in range(HEADS):
                    j, p0 = h // 2, HS * (h % 2)
                    pp = slice(p0, p0 + HS)
                    o = slice(j * HS, (j + 1) * HS)
                    out = ps[:, 2 + h % 2, o]
                    mm(out, ar[pp, j, 0, :], st0[pp, j, :], start=True, stop=False)
                    last = mm(out, scores[:, h, 2, :], tok[:, 2, h * HS:(h + 1) * HS], start=False, stop=True)
                last.then_inc(rw["rhsmm"], 1)
                pe.wait_ge(rw["rhs"], c + 1)
                for h in range(HEADS):
                    o = slice(h * HS, (h + 1) * HS)
                    last = mm(ps[:, 0, o], xx[:, h, 1, :], sq[:, 0, o], start=True, stop=True)
                last.then_inc(rw["umm"], 1)
                pe.wait_ge(rw["u"], c + 1)
                for h in range(HEADS):
                    j, p0 = h // 2, HS * (h % 2)
                    pp = slice(p0, p0 + HS)
                    o = slice(h * HS, (h + 1) * HS)
                    out = ps[pp, 4 + h % 2, j * CH:(j + 1) * CH]
                    mm(out, sq[:, 1, o], scores[:, h, 1, :], start=True, stop=False)
                    mm(out, tok[:, 2, o], scores[:, h, 3, :], start=False, stop=False)
                    mm(out, st0[pp, j, :], ar[pp, j, 1, :], start=False, stop=True)
                for h in range(HEADS):
                    j, p0 = h // 2, HS * (h % 2)
                    pp = slice(p0, p0 + HS)
                    o = slice(h * HS, (h + 1) * HS)
                    out = ps[pp, 6, j * HS:(j + 1) * HS]
                    mm(out, tok[:, 0, o], sq[:, 1, o], start=True, stop=False)
                    last = mm(out, tok[:, 1, o], tok[:, 2, o], start=False, stop=True)
                last.then_inc(rw["ysmm"], 1)

            pe.wait_ge(rw["y"], 2 * NCH)
            pe.wait_ge(rw["s"], NCH + 1)
            with pe.Fori(0, NJ) as j:
                mm(ps[:, 0, :], bones, tile(wd, j), start=True, stop=True).then_inc(po["mean"], 1)
                pe.wait_ge(po["rk"], j + 1)
                mm(ps[:, 2, :], bones, sq[:, 1, :], start=True, stop=True).then_inc(po["bonus"], 1)
                pe.wait_ge(po["sq"], j + 1)
                mm(ps[:, 1, :], bones, sq[:, 0, :], start=True, stop=True).then_inc(po["var"], 1)
                pe.wait_ge(po["done"], j + 1)

            f = first["merge"]
            pe.wait_ge(po["ya"], NJ)

            def merge(n, s, half):
                b = 4 * half
                pe.wait_ge(w_split, n + 1)
                for k in range(NJ):
                    mm3(ps[:, b, :], s, k, ya_hi[:, k, :], ya_lo[:, k, :], k == 0, k == NJ - 1)
                for k in range(NJ):
                    last = mm3(ps[:, b + 1, :], s, NJ + k, yb_hi[:, k, :], yb_lo[:, k, :], k == 0, k == NJ - 1)
                last.then_inc(w_done, 1)
                dense(n + 1, (s + 1) % 2, b + 2, h_hi, h_lo)
                dense(n + 2, s, b + 3, h_hi, h_lo)

            merge(f, 0, 0)
            merge(f + 3, 1, 1)
            with pe.Fori(0, 3) as i:
                for half in range(2):
                    pe.wait_ge(po["mg_t"], 2 * i + (half + 1))
                    merge(6 * i + (f + 6 + 3 * half), half, half)
            residual("wo", KD, mg_hi, mg_lo, lambda: pe.wait_ge(po["mg"], KD))

            ffn_up(1, "up1")
            residual("down1", KF, hid_hi, hid_lo, lambda: pe.wait_ge(ffn[1]["hid"], KF))
            sum_squares(3)

            def pairs(name, ls, gs, behind_norm):
                f = first[name]
                if behind_norm:
                    dense_first(4, f)
                    dense(f + 1, 1, 1, h_hi, h_lo)
                    sum_squares(4)
                for s in range(2 if behind_norm else 0, 4):
                    dense(f + s, s % 2, s, h_hi, h_lo)
                with pe.Fori(0, 3) as i:
                    for s in range(4):
                        pe.wait_ge(gs if s % 2 else ls, 2 * i + (s // 2 + 1))
                        dense(4 * i + (f + 4 + s), s % 2, s, h_hi, h_lo)

            pairs("pair0", ev["l0"], ev["g0"], True)
            pe.wait_ge(ev["l0"], KD)
            pe.wait_ge(ev["r0"], KD)
            pe.wait_ge(ev["loaded"], 48)
            for g in range(4):
                for t in range(QT):
                    if g >= 1:
                        pe.wait_ge(ev["fmix"], 2 * g)
                    for k in range(2):
                        last = mm(ps[:, t, :], left[:, 2 * g + k, t * P:(t + 1) * P], dftc[:, k, :],
                                  start=(k == 0), stop=(k == 1))
                    last.then_inc(ev["chmm"], 1)
                pe.wait_ge(ev["chan"], QT * (g + 1))
                for e in range(2):
                    if g >= 1:
                        pe.wait_ge(ev["fmix"], 2 * g - 1 + e)
                    for part in range(2):
                        for t in range(QT):
                            o = 256 * part + P * e
                            last = mm(ps[:, 4 + e, :], chan[:, t, o:o + P], dfts[:, part * QT + t, :],
                                      start=(part == 0 and t == 0), stop=(part == 1 and t == QT - 1))
                    last.then_inc(ev["sqmm"], 1)
                pe.wait_ge(ev["fmix"], 2 * g + 2)
                for e in range(2):
                    if g >= 1:
                        pe.wait_ge(ev["t"], 2 * g - 1 + e)
                    for k in range(2):
                        last = mm(ps[:, 6 + e, :], fws[:, (2 * g + k) * 2 + e, :], fmix[:, k, :],
                                  start=(k == 0), stop=(k == 1))
                    last.then_inc(ev["fwmm"], 1)
            pe.wait_ge(ev["t"], KD)
            residual("eo0", KD, z_hi, z_lo, lambda: pe.wait_ge(ev["z"], KD))

            pe.wait_ge(at["rope"], 48)
            pairs("pair1", ev["l1"], ev["g1"], False)
            f = first["kv"]
            for s in range(2):
                dense(f + s, s, 4 + s, h_hi, h_lo)
            for t in range(QT):
                last = nc.tensor.transpose(ps[:, 6, t * P:(t + 1) * P], rinv[:, 0, t * P:(t + 1) * P], ident)
            last.then_inc(ev["col"], 1)
            pe.wait_ge(ev["l1"], KD)
            pe.wait_ge(ev["r1"], KD)
            for b in range(2):
                pe.wait_ge(w_split, f + 3 + b)
                for t in range(QT):
                    tt = slice(t * P, (t + 1) * P)
                    for k in range(4):
                        w = slice(k * 256, (k + 1) * 256)
                        kk_ = 4 * b + k
                        mm(ps[:, t, 0:256], h_hi[:, kk_, tt], w_hi[:, b, w], start=(kk_ == 0), stop=False)
                        mm(ps[:, t, 0:256], h_lo[:, kk_, tt], w_hi[:, b, w], start=False, stop=False)
                        last = mm(ps[:, t, 0:256], h_hi[:, kk_, tt], w_lo[:, b, w], start=False, stop=(kk_ == KD - 1))
                last.then_inc(w_done, 1)

            def sum_head(u):
                pe.wait_ge(at["sq"], u + 1)
                if type(u) is not int or u >= 1:
                    pe.wait_ge(at["qr"], u)
                mm(ps[:, 3, :], ones, sq[:, 0, :], start=True, stop=True).then_inc(at["ssmm"], 1)

            def swap_halves(u):
                pe.wait_ge(at["qn"], u + 1)
                mm(ps[:, 3, :], perm, tmp[:, 0, :], start=True, stop=True).then_inc(at["rot"], 1)

            def score(v, g):
                pe.wait_ge(at["qr"], v + 3)
                if type(v) is not int or v >= 1:
                    pe.wait_ge(at["exp"], QT * v)
                for t in range(QT):
                    mm(ps[:, 4 + t, :], qr[:, g, t * P:(t + 1) * P], kt[:, g, :], start=True, stop=True).then_inc(at["smm"], 1)

            def turn(v, g):
                for t in range(QT):
                    pe.wait_ge(at["prob"], QT * v + (t + 1))
                    if type(v) is not int or QT * v + t >= 2:
                        pe.wait_ge(at["pt"], QT * v + (t - 1))
                    for k in range(QT):
                        last = nc.tensor.transpose(ps[:, t % 2, k * P:(k + 1) * P], prob[:, g, t, k * P:(k + 1) * P], ident)
                    last.then_inc(at["tr"], 1)

            def weigh(v, g):
                pe.wait_ge(at["pt"], QT * v + QT)
                if type(v) is not int or v >= 1:
                    pe.wait_ge(at["t"], v)
                for t in range(QT):
                    last = mm(ps[:, 2, :], vt[:, t, g * P:(g + 1) * P], probT[:, t, :], start=(t == 0), stop=(t == QT - 1))
                last.then_inc(at["pv"], 1)

            def head(v, g, is_first=False, is_last=False):
                score(v, g)
                if not is_last:
                    sum_head(v + 3)
                if not is_first:
                    turn(v - 1, 1 - g)
                if not is_last:
                    swap_halves(v + 3)
                if not is_first:
                    weigh(v - 1, 1 - g)

            pe.wait_ge(ev["k"], 2)
            pe.wait_ge(ev["v"], QT)
            for u in range(3):
                sum_head(u)
                swap_halves(u)
            head(0, 0, is_first=True)
            head(1, 1)
            with pe.Fori(0, 2) as i:
                for g in range(2):
                    head(2 * i + (2 + g), g)
            head(6, 0)
            head(7, 1, is_last=True)
            turn(7, 1)
            weigh(7, 1)
            residual("eo1", KD, z_hi, z_lo, lambda: pe.wait_ge(at["z"], KD))

            f = first["rnn"]

            def gates(b, s):
                pe.wait_ge(rg[f"w{s}"], 8 * b + (16 - 8 * s))
                pe.wait_ge(rg["xc"], b + 1)
                if type(b) is not int or b >= 1:
                    pe.wait_ge(rg["ri"], 4 * b)
                for k in range(4):
                    last = mm(ps[:, 4 + k, :], rg_w[:, s, k, :], xc[:, s, :], start=True, stop=True)
                last.then_inc(rg["gmm"], 1)

            dense_first(5, f)
            dense(f + 1, 1, 1, h_hi, h_lo)
            sum_squares(5)
            dense(f + 2, 0, 2, h_hi, h_lo)
            dense(f + 3, 1, 3, h_hi, h_lo)
            pe.wait_ge(nrm["root"], 6)
            gates(0, 0)
            pe.wait_ge(rg["x"], 1)
            dense(f + 4, 0, 0, h_hi, h_lo)
            gates(1, 1)
            pe.wait_ge(rg["x"], 2)
            dense(f + 5, 1, 1, h_hi, h_lo)
            for s in range(2):
                pe.wait_ge(rg["g"], s + 1)
                dense(f + 6 + s, s, 2 + s, h_hi, h_lo)
            with pe.Fori(0, NRB // 2 - 2) as i:
                for s in range(2):
                    gates(2 * i + (2 + s), s)
                    pe.wait_ge(rg["x"], 2 * i + (3 + s))
                    dense(4 * i + (f + 8 + s), s, s, h_hi, h_lo)
                for s in range(2):
                    pe.wait_ge(rg["g"], 2 * i + (3 + s))
                    dense(4 * i + (f + 10 + s), s, 2 + s, h_hi, h_lo)
            for s in range(2):
                gates(NRB - 2 + s, s)
            pe.wait_ge(rg["ri"], 4 * NRB)
            pe.wait_ge(rg["g"], NRB)
            residual("ro", NRB, y_hi, y_lo, lambda: pe.wait_ge(rg["z"], NRB))
            sum_squares(6)

        @block.scalar
        def _(act):
            A = nc.scalar.activation
            own = Chain(act, a_chain)

            def norm(k, where, g=None):
                def x_stands(m):
                    if k > 0:
                        act.wait_ge(nrm["x"], x_at(k) + m + 1)
                    elif m == 0:
                        act.wait_ge(s_x, 16)
                        act.wait_ge(s_par, 48)
                if where == "h":
                    for m in range(KD):
                        x_stands(m)
                        A(h_hi[:, m, :], x[:, m, :], ACT.Copy, scale=col(par, g, m)).then_inc(nrm["hi"], 1)
                for m in range(KD):
                    if where != "h":
                        x_stands(m)
                    if m >= 2:
                        act.wait_ge(nrm["acc"], (KD - 1) * k + max(1, m - 2))
                    A(sq[:, m % 2, :], x[:, m, :], ACT.Square).then_inc(nrm["sq"], 1)
                act.wait_ge(nrm["ss"], k + 1)
                A(root[:, 0, :], ps[:, 7, :], ACT.Sqrt, bias=col(par, "eps_rms"), scale=1.0 / D).then_inc(nrm["root"], 1)

            def ffn_up(k, name):
                q = ffn[k]
                with act.Fori(0, KF // 2) as i:
                    for s in range(2):
                        act.wait_ge(q["g"], 2 * i + (s + 1))
                        A(gate_s[:, s, :], gate_s[:, s, :], ACT.Silu).then_inc(q["silu"], 1)
                        act.wait_ge(q["t"], 2 * i + (s + 1))
                        act.sem_inc(s_act_pass, 1)
                        nc.scalar.copy(tile(hid_hi, 2 * i + s), hid_t[:, s, :]).then_inc(q["hi"], 1)

            norm(0, "h", "ffn1_norm")
            ffn_up(0, "up0")
            act.wait_ge(w_done, first["conv"])
            act.dma_start(lora_s[:], lora).then_inc(mx_s["small_loaded"], 16)
            act.dma_start(gup_s[:], gup).then_inc(mx_s["small_loaded"], 16)
            norm(1, "h", "mix_norm")

            act.wait_ge(mx_s["mix"], 14)
            A(sq[0:64, 0, :], mix[0:64, 12, :], ACT.Tanh).then_inc(mx_s["lora_in"], 1)
            nc.scalar.copy(tmp[64:128, 0, :], mix[64:128, 12, :]).then_inc(mx_s["lora_in"], 1)
            A(sq[:, 1, :], mix[:, 13, :], ACT.Sigmoid).then_inc(mx_s["lora_in"], 1)
            for j in range(NJ):
                act.wait_ge(mx_s["lora_mm"], j + 1)
                A(wd[:, j, :], ps[:, j, :], ACT.Sigmoid, bias=col(par, "w0", j)).then_inc(mx_s["lora_ev"], 1)
            for j in range(NJ):
                act.wait_ge(mx_s["lora_mm"], NJ + j + 1)
                A(bb[:, j, :], ps[:, 4 + j, :], ACT.Sigmoid, bias=col(par, "a0", j)).then_inc(mx_s["lora_ev"], 1)
            for j in range(NJ):
                act.wait_ge(mx_s["lora_mm"], 2 * NJ + j + 1)
                nc.scalar.copy(gg[:, j, :], ps[:, j, :]).then_inc(mx_s["lora_ev"], 1)
            act.wait_ge(mx_s["lora_ev"], NJ)
            for j in range(NJ):
                A(wd[:, j, :], wd[:, j, :], ACT.Exp, scale=-INV_SQRT_E).then_inc(mx_s["kk_w"], 1)
            for j in range(NJ):
                act.wait_ge(mx_s["kk_ss"], j + 1)
                if j >= 2:
                    act.wait_ge(mx_s["kk_done"], j - 1)
                A(tmp[:, j % 2, :], ps[:, 4 + j, :], ACT.Sqrt).then_inc(mx_s["kk_root"], 1)

            act.wait_ge(mx_s["kk_done"], NJ)
            with act.Fori(0, NCH) as c:
                act.wait_ge(rw["s"], c + 1)
                nc.scalar.copy(root[:, 0, :].rearrange("p (j t) -> p j t", j=NJ),
                               mix[:, 8:12, bass.ds(c * CH, CH)]).then_inc(rw["vc"], 1)
                for h in range(HEADS):
                    for z in range(2):
                        last = nc.scalar.copy(xx[:, h, z, :], ident)
                last.then_inc(rw["reset"], 1)
                for q in range(3):
                    act.wait_ge(rw["tr"], 3 * c + (q + 1))
                    nc.scalar.copy(tok[:, q, :], ps[:, q, :]).then_inc(rw["tok"], 1)
                for l in range(LEVELS):
                    for g in range(2):
                        act.wait_ge(rw["t1mm"], 2 * LEVELS * c + (2 * l + g + 1))
                        nc.scalar.copy(t1[:, 4 * g:4 * g + 4, :].rearrange("p h t -> p (h t)"), ps[:, g, :]).then_inc(rw["t1"], 1)
                act.wait_ge(rw["rhsmm"], c + 1)
                rhs = sq[:, 0, :].rearrange("p (j e v) -> p e j v", j=NJ, e=2)
                for e in range(2):
                    last = nc.scalar.copy(rhs[:, e], ps[:, 2 + e, 0:256].rearrange("p (j v) -> p j v", j=NJ))
                last.then_inc(rw["rhs"], 1)
                act.wait_ge(rw["umm"], c + 1)
                nc.scalar.copy(sq[:, 1, :], ps[:, 0, :]).then_inc(rw["u"], 1)

            with act.Fori(0, NJ) as j:
                act.wait_ge(po["yc"], j + 1)
                A(sq[:, 0, :], tmp[:, 0, :], ACT.Square).then_inc(po["sq"], 1)
                act.wait_ge(po["var"], j + 1)
                A(root[:, 0, :], ps[:, 1, :], ACT.Sqrt, bias=col(par, "eps_gn"), scale=1.0 / HS).then_inc(po["root"], 1)
                act.wait_ge(po["t"], j + 1)
                nc.scalar.copy(tile(yb_hi, j), tmp[:, 1, :]).then_inc(po["hi"], 1)
            for j in range(NJ):
                nc.scalar.copy(ya_hi[:, j, :], ya[:, j, :]).then_inc(po["yahi"], 1)

            f = first["merge"]
            act.wait_ge(po["done"], NJ)
            with act.Fori(0, KD // 2) as i:
                for half in range(2):
                    act.wait_ge(po["g"], 2 * i + (half + 1))
                    A(sga[:, half].rearrange("p a t -> p (a t)"), sga[:, half].rearrange("p a t -> p (a t)"), ACT.Sigmoid
                      ).then_inc(po["sig"], 1)
                    act.wait_ge(po["mg_t"], 2 * i + (half + 1))
                    nc.scalar.copy(tile(mg_hi, 2 * i + half), mt[:, half, 1, :]).then_inc(po["mg_hi"], 1)

            norm(2, "h", "ffn2_norm")
            ffn_up(1, "up1")
            act.wait_ge(w_done, first["pair0"])
            act.dma_start(dftc[:], dft_c).then_inc(ev["loaded"], 16)
            act.dma_start(dfts[:], dft_s).then_inc(ev["loaded"], 16)
            act.dma_start(fws[:], fw).then_inc(ev["loaded"], 16)
            norm(3, "x")
            norm(4, "h", "even_norm_2")

            def pairs(gs, rs):
                with act.Fori(0, 4) as i:
                    for s in range(2):
                        act.wait_ge(gs, 2 * i + (s + 1))
                        act.sem_inc(s_act_pass, 1)
                        A(tile(right, 2 * i + s), tile(right, 2 * i + s), ACT.Silu).then_inc(rs, 1)

            pairs(ev["g0"], ev["r0"])
            for g in range(4):
                for t in range(QT):
                    act.wait_ge(ev["chmm"], QT * g + t + 1)
                    if g >= 1:
                        act.wait_ge(ev["sqmm"], 2 * g)
                    nc.scalar.copy(chan[:, t, :], ps[:, t, :]).then_inc(ev["chan"], 1)
                for e in range(2):
                    act.wait_ge(ev["t"], 2 * g + e + 1)
                    nc.scalar.copy(z_hi[:, 2 * g + e, :], tmp[:, e, :]).then_inc(ev["hi"], 1)
            act.wait_ge(w_done, first["pair1"])
            act.dma_start(rope_s[:], rope).then_inc(at["rope"], 16)
            act.wait_ge(at["rope"], 16)
            act.wait_ge(nrm["x"], x_at(5))
            act.sem_inc(at["rope"], 32)
            pairs(ev["g1"], ev["r1"])

            def square_head(u, src):
                if type(u) is not int or u >= 1:
                    act.wait_ge(at["ssmm"], u)
                    act.sem_inc(s_act_pass, 1)
                A(sq[:, 0, :], src, ACT.Square).then_inc(at["sq"], 1)

            def root_head(u):
                act.wait_ge(at["ssmm"], u + 1)
                A(root[:, 0, :], ps[:, 3, :], ACT.Sqrt, bias=col(par, "eps_rms"), scale=1.0 / P).then_inc(at["root"], 1)

            def copy_turned(v):
                if type(v) is not int or v >= 1:
                    act.wait_ge(at["pv"], v)
                for t in range(QT):
                    act.wait_ge(at["tr"], QT * v + (t + 1))
                    nc.scalar.copy(probT[:, :, t * P:(t + 1) * P], ps[:, t % 2, :].rearrange("p (k t) -> p k t", k=QT)
                                   ).then_inc(at["pt"], 1)

            def z_part(v, i, g):
                act.wait_ge(at["t"], v + 1)
                act.sem_inc(s_act_pass, 1)
                nc.scalar.copy(tile(z_hi, i + 4 * g), tmp[:, 1, :]).then_inc(at["hi"], 1)

            def head(v, i, g, is_first=False, nexts=2):
                if type(v) is not int or v >= 2:
                    act.wait_ge(at["tr"], QT * v - QT)
                for t in range(QT):
                    act.wait_ge(at["max"], QT * v + (t + 1))
                    A(prob[:, g, t, :], ps[:, 4 + t, :], ACT.Exp, bias=mx[:, 16 * g + t:16 * g + t + 1], scale=P ** -0.5,
                      accum_out=mx[:, 16 * g + 4 + t:16 * g + 5 + t]).then_inc(at["exp"], 1)
                if nexts >= 1:
                    root_head(v + 3)
                if nexts >= 2:
                    square_head(v + 4, tile(left, i + 1 + 4 * g))
                if not is_first:
                    copy_turned(v - 1)
                    z_part(v - 1, i if g else i - 1, 1 - g)

            act.wait_ge(ev["k"], 2)
            act.wait_ge(ev["l1"], KD)
            square_head(0, kt[:, 0, :])
            root_head(0)
            square_head(1, kt[:, 1, :])
            root_head(1)
            square_head(2, left[:, 0, :])
            root_head(2)
            square_head(3, left[:, 4, :])
            head(0, 0, 0, is_first=True)
            head(1, 0, 1)
            with act.Fori(0, 2) as i:
                for g in range(2):
                    head(2 * i + (2 + g), i + 1, g)
            head(6, 3, 0, nexts=1)
            head(7, 3, 1, nexts=0)
            copy_turned(7)
            z_part(7, 3, 1)

            norm(5, "h", "odd_norm_2")

            act.wait_ge(rg["lexp"], 1)
            A(lam[:, 1, :], lam[:, 0, :], ACT.Exp, scale=-1.0).then_inc(rg["lexp"], 1)
            f = first["rnn"]
            for s in range(2):
                act.dma_start(rg_w[:, s], rgates[s]).then_inc(rg[f"w{s}"], 16)
            def block_gates(b, s, acquire):
                act.wait_ge(rg["gmm"], b + 1)
                if acquire:
                    act.wait_ge(rg["y"], b - 1)
                for k in range(4):
                    name, d = ("gate_a_b_2", "gate_x_b_2")[k % 2], k // 2
                    A(ri[:, s, k, :], ps[:, 4 + k, :], ACT.Sigmoid, bias=col(par, name, b + 16 * d)).then_inc(rg["ri"], 1)
                act.dma_start(rg_w[:, s], rgates[bass.ds(b + 2, 1)].rearrange("a p k q -> p (a k) q")
                              ).then_inc(rg[f"w{s}"], 16)

            def pair_maps(b):
                for s in range(2):
                    act.wait_ge(rg["nla"], 2 * b + 2 * (s + 1))
                    for d in range(2):
                        A(aa[:, s, d, :], ri[:, s, 2 * d, :], ACT.Exp, scale=-1.0).then_inc(rg["a"], 1)
                    for d in range(2):
                        A(th[:, s, d, :], ri[:, s, 2 * d, :], ACT.Tanh).then_inc(rg["th"], 1)
                act.wait_ge(rg["th"], 2 * b + 4)
                for s in range(2):
                    for d in range(2):
                        A(ri[:, s, 2 * d, :], aa[:, s, d, :], ACT.Square).then_inc(rg["a2"], 1)
                for s in range(2):
                    for d in range(2):
                        act.wait_ge(rg["w"], 2 * b + (2 * s + d + 1))
                        A(th[:, s, d, :], th[:, s, d, :], ACT.Sqrt).then_inc(rg["root"], 1)

            def pair_values(b):
                for s in range(2):
                    act.wait_ge(rg["t"], b + (s + 1))
                    act.sem_inc(s_act_pass, 1)
                    nc.scalar.copy(tile(y_hi, b + s), ri[:, s, 2, :]).then_inc(rg["hi"], 1)

            def gate_silu(b):
                for s in range(2):
                    act.wait_ge(rg["g"], b + (s + 1))
                    A(sgate[:, s, :], sgate[:, s, :], ACT.Silu).then_inc(rg["sg"], 1)

            gate_silu(0)
            for s in range(2):
                block_gates(s, s, False)
            pair_maps(0)
            pair_values(0)
            with act.Fori(0, NRB // 2 - 1) as i:
                gate_silu(2 * i + 2)
                for s in range(2):
                    block_gates(2 * i + (2 + s), s, True)
                pair_maps(2 * i + 2)
                pair_values(2 * i + 2)
            norm(6, "out")
            for s in range(2):
                act.wait_ge(rg[f"w{s}"], 16 * (NRB // 2 + 1))

        @block.vector
        def _(dve):
            V = nc.vector
            own = Chain(dve, v_chain)

            def norm(k, where, g):
                if where == "h":
                    for m in range(KD):
                        dve.wait_ge(nrm["hi"], h_at(k) + m + 1)
                        rest_of_h(m, g)
                sum_up(k)
                if where != "h":
                    done = s_out_t if where == "out" else nrm["x"]
                    for m in range(KD):
                        V.scalar_tensor_tensor(out=x[:, m, :], in0=x[:, m, :], scalar=col(par, g, m),
                                               in1=rinv[:, 0, :], op0=ALU.mult, op1=ALU.mult).then_inc(done, 1)

            def rest_of_h(m, g):
                V.scalar_tensor_tensor(out=h_lo[:, m, :], in0=x[:, m, :], scalar=col(par, g, m),
                                       in1=h_hi[:, m, :].bitcast(F32), op0=ALU.mult, op1=ALU.subtract
                                       ).then_inc(nrm["h"], 1)

            def sum_up(k):
                for m in range(1, KD):
                    dve.wait_ge(nrm["sq"], KD * k + m + 1)
                    if m >= 2:
                        dve.wait_ge(nrm["acc"], (KD - 1) * k + m - 1)
                    V.tensor_tensor(root[:, 0, :], sq[:, 0, :] if m == 1 else root[:, 0, :], sq[:, m % 2, :], ALU.add
                                    ).then_inc(nrm["acc"], 1)
                dve.wait_ge(nrm["root"], k + 1)
                own.link(V.reciprocal(rinv[:, 0, :], root[:, 0, :]))

            def divided(out, bank):
                return V.tensor_tensor(out, ps[:, bank, :], rinv[:, 0, :], ALU.mult)

            def ffn_up(k, name):
                q, f = ffn[k], first[name]
                with dve.Fori(0, KF // 2) as i:
                    own.enter(i, 0)
                    for s in range(2):
                        m = 2 * i + s
                        dve.wait_ge(w_done, 4 * i + (f + 2 * s + 1))
                        divided(gate_s[:, s, :], 2 * s).then_inc(q["g"], 1)
                        dve.wait_ge(w_done, 4 * i + (f + 2 * s + 2))
                        divided(hid_t[:, s, :], 2 * s + 1).then_inc(q["u"], 1)
                        dve.wait_ge(q["u"], m + 1)
                        dve.wait_ge(q["silu"], m + 1)
                        V.tensor_tensor(hid_t[:, s, :], gate_s[:, s, :], hid_t[:, s, :], ALU.mult).then_inc(q["t"], 1)
                        dve.wait_ge(q["hi"], m + 1)
                        V.tensor_tensor(tile(hid_lo, m), hid_t[:, s, :], tile(hid_hi, m).bitcast(F32), ALU.subtract
                                        ).then_inc(q["hid"], 1)
                        dve.wait_ge(q["hid"], m + 1)
                    own.leave(0)

            BANKS = {1: 0, 2: 1, 3: 2, 5: 3, 6: 4, 7: 5}

            def add_to_x(k, until, scale, g=None):
                for m in range(KD + 1):
                    if m < KD:
                        if m < KD - 1:
                            dve.wait_ge(s_bank, (KD - 1) * BANKS[k] + m + 1)
                        else:
                            dve.wait_ge(w_done, until)
                        V.scalar_tensor_tensor(out=x[:, m, :], in0=ps[:, m, :], scalar=scale, in1=x[:, m, :],
                                               op0=ALU.mult, op1=ALU.add).then_inc(nrm["x"], 1)
                    if g is not None and m >= 1:
                        n = {6: 5}.get(k, k)
                        dve.wait_ge(nrm["hi"], h_at(n) + m)
                        rest_of_h(m - 1, g)

            dve.wait_ge(s_par, 48)
            V.tensor_copy(lev8[:].rearrange("p a b c -> p (a b c)"), m32[:, 0:LEVELS * 2 * P])
            own.link(V.tensor_copy(tri8[:].rearrange("p a b -> p (a b)"), m32[:, LEVELS * 2 * P:]))
            dve.wait_ge(s_x, 16)
            norm(0, "h", "ffn1_norm")
            ffn_up(0, "up0")
            add_to_x(1, first["conv"], 0.5, "mix_norm")
            sum_up(1)

            own.link(V.memset(padc[:, :, 0:2], 0.0))
            own.link(V.memset(padm[:, :, 0:1], 0.0))
            f = first["conv"]
            for j in range(NJ):
                s = j % 2
                dve.wait_ge(w_done, f + 3 * j + 1)
                own.link(divided(csb[:, s, :], 3 * s))
                dve.wait_ge(w_done, f + 3 * j + 2)
                own.link(divided(dif[:, s, :], 3 * s + 1))
                own.link(V.tensor_tensor(padc[:, s, 2:T + 2], csb[:, s, :], dif[:, s, :], ALU.mult))
                own.link(V.tensor_scalar(dif[:, s, :], padc[:, s, 0:T], col(par, "conv_w", j), None, ALU.mult))
                for tap in (1, 2):
                    own.link(V.scalar_tensor_tensor(out=dif[:, s, :], in0=padc[:, s, tap:T + tap],
                                                    scalar=col(par, "conv_w", 4 * tap + j), in1=dif[:, s, :],
                                                    op0=ALU.mult, op1=ALU.add))
                dve.wait_ge(w_done, f + 3 * j + 3)
                own.link(divided(csb[:, s, :], 3 * s + 2))
                V.tensor_tensor(ya[:, j, :], dif[:, s, :], csb[:, s, :], ALU.mult).then_inc(mx_s["ya"], 1)
            f = first["mix"]
            dve.sem_inc(mx_s["raw"], 2)
            with dve.Fori(0, 7) as i:
                own.enter(i, 4)
                for s in range(2):
                    dve.wait_ge(w_done, 2 * i + (f + s + 1))
                    divided(padm[:, s, 1:T + 1], 6 + s).then_inc(mx_s["raw"], 1)
                    dve.wait_ge(mx_s["raw"], 2 * i + (s + 3))
                    own.link(V.tensor_tensor(dif[:, s, :], padm[:, s, 0:T], padm[:, s, 1:T + 1], ALU.subtract))
                    own.link(V.scalar_tensor_tensor(out=tile(mix, 2 * i + s), in0=dif[:, s, :],
                                                    scalar=col(par, "mu_b", 2 * i + s), in1=padm[:, s, 1:T + 1],
                                                    op0=ALU.mult, op1=ALU.add))
                    dve.sem_inc(mx_s["mix"], 1)
            own.leave(7)
            for j in range(NJ):
                s = j % 2
                own.link(V.tensor_scalar(kk[:, j, :], mix[:, 4 + j, :], col(par, "k_k", j), None, ALU.mult))
                if j >= 2:
                    dve.wait_ge(mx_s["kk_ss"], j - 1)
                V.tensor_tensor(dif[:, s, :], kk[:, j, :], kk[:, j, :], ALU.mult).then_inc(mx_s["kk_sq"], 1)
            for j in range(NJ):
                s = j % 2
                dve.wait_ge(mx_s["kk_root"], j + 1)
                own.link(V.tensor_scalar(csb[:, s, :], tmp[:, s, :], 1e-12, None, ALU.max))
                own.link(V.reciprocal(csb[:, s, :], csb[:, s, :]))
                own.link(V.tensor_tensor(kk[:, j, :], kk[:, j, :], csb[:, s, :], ALU.mult))
                dve.wait_ge(mx_s["lora_ev"], NJ + j + 1)
                own.link(V.tensor_scalar(csb[:, s, :], bb[:, j, :], 1.0, col(par, "k_a", j), ALU.subtract, ALU.mult))
                own.link(V.scalar_tensor_tensor(out=mix[:, 4 + j, :], in0=csb[:, s, :], scalar=1.0, in1=mix[:, 4 + j, :],
                                                op0=ALU.add, op1=ALU.mult))
                own.link(V.scalar_tensor_tensor(out=bb[:, j, :], in0=kk[:, j, :], scalar=-1.0, in1=bb[:, j, :],
                                                op0=ALU.mult, op1=ALU.mult))
                dve.sem_inc(mx_s["kk_done"], 1)

            dve.wait_ge(mx_s["kk_w"], NJ)
            dve.wait_ge(mx_s["lora_mm"], 3 * NJ)
            own.link(V.memset(scores[:], 0.0))
            own.link(V.memset(st[:], 0.0))
            own.link(V.memset(pe_[:], 1.0))
            dve.sem_inc(rw["s"], 1)
            PER = 4 + 4 + 3 + 1
            with dve.Fori(0, NCH) as c:
                own.enter(c, PER)
                tt = bass.ds(c * CH, CH)
                for j in range(NJ):
                    own.link(V.tensor_tensor_scan(pe_[:, j, 1:CH + 1], wd[:, j, tt], wd[:, j, tt], 1.0, ALU.mult, ALU.bypass))
                own.link(V.reciprocal(rmid[:], pe_[:, :, 64:65]))
                own.link(V.tensor_tensor(pn[:], pe_[:], rmid[:].broadcast_to([P, NJ, CH + 1]), ALU.mult))
                pinv = tmp[:, 0, :].rearrange("p (j t) -> p j t", j=NJ)
                own.link(V.reciprocal(pinv, pn[:, :, 1:CH + 1]))
                own.link(V.tensor_tensor(st0[:], st[:], pe_[:, :, 64:65].broadcast_to([P, NJ, HS]), ALU.mult))
                own.link(V.tensor_tensor(ar[:, :, 0, :], kk[:, :, tt], pn[:, :, 0:CH], ALU.mult))
                own.link(V.tensor_tensor(ar[:, :, 1, :], mix[:, 0:4, tt], pn[:, :, 1:CH + 1], ALU.mult))
                own.link(V.tensor_tensor(bc[:], bb[:, :, tt], pinv, ALU.mult))
                V.tensor_tensor(kc_[:], mix[:, 4:8, tt], pinv, ALU.mult).then_inc(rw["ops"], 1)
                for h in range(HEADS):
                    dve.wait_ge(rw["mat"], HEADS * c + (h + 1))
                    dve.sem_inc(s_pass, 1)
                    V.copy_predicated(scores[:, h].rearrange("p a t -> p (a t)"), tri8[:].rearrange("p a t -> p (a t)"),
                                      ps[:, 4 + h % 4, :]).then_inc(rw["sc"], 1)
                for l in range(LEVELS):
                    for hp in range(4):
                        dve.wait_ge(rw["xmm"], 4 * LEVELS * c + (4 * l + hp + 1))
                        dve.sem_inc(s_pass, 1)
                        for e in range(2):
                            last = V.copy_predicated(xx[:, 2 * hp + e].rearrange("p a t -> p (a t)"),
                                                     lev8[:, l].rearrange("p a t -> p (a t)"),
                                                     ps[:, 4 + hp, 256 * e:256 * e + 256])
                        last.then_inc(rw["xx"], 1)
                dve.wait_ge(rw["ysmm"], c + 1)
                for e in range(2):
                    pp = slice(64 * e, 64 * e + 64)
                    V.tensor_scalar(wd[pp, :, tt], ps[pp, 4 + e, :].rearrange("p (j t) -> p j t", j=NJ), 1.0, None, ALU.mult
                                    ).then_inc(rw["y"], 1)
                own.link(V.tensor_tensor(st0[:], st0[:], ps[:, 6, 0:256].rearrange("p (j v) -> p j v", j=NJ), ALU.add))
                V.tensor_tensor(st[:], st0[:], pn[:, :, CH:CH + 1].broadcast_to([P, NJ, HS]), ALU.mult).then_inc(rw["s"], 1)
                dve.wait_ge(rw["s"], c + 2)
            own.leave(NCH)

            with dve.Fori(0, NJ) as j:
                own.enter(j, 6)
                dve.wait_ge(po["mean"], j + 1)
                V.scalar_tensor_tensor(out=tmp[:, 0, :], in0=ps[:, 0, :], scalar=-1.0 / HS, in1=tile(wd, j),
                                       op0=ALU.mult, op1=ALU.add).then_inc(po["yc"], 1)
                V.scalar_tensor_tensor(out=sq[:, 1, :], in0=tile(mix, j), scalar=col(par, "r_k", j),
                                       in1=tile(mix, j + 4), op0=ALU.mult, op1=ALU.mult).then_inc(po["rk"], 1)
                dve.wait_ge(po["bonus"], j + 1)
                own.link(V.tensor_tensor(tmp[:, 1, :], ps[:, 2, :], tile(mix, j + 8), ALU.mult))
                dve.wait_ge(po["root"], j + 1)
                own.link(V.reciprocal(sq[:, 0, :], root[:, 0, :]))
                own.link(V.tensor_tensor(tmp[:, 0, :], tmp[:, 0, :], sq[:, 0, :], ALU.mult))
                own.link(V.tensor_scalar(tmp[:, 0, :], tmp[:, 0, :], col(par, "ln_x_w", j), col(par, "ln_x_b", j),
                                         ALU.mult, ALU.add))
                own.link(V.tensor_tensor(tmp[:, 1, :], tmp[:, 0, :], tmp[:, 1, :], ALU.add))
                own.link(V.tensor_tensor(tmp[:, 1, :], tmp[:, 1, :], tile(gg, j), ALU.mult))
                dve.sem_inc(po["t"], 1)
                dve.wait_ge(po["hi"], j + 1)
                V.tensor_tensor(tile(yb_lo, j), tmp[:, 1, :], tile(yb_hi, j).bitcast(F32), ALU.subtract).then_inc(po["done"], 1)
            own.leave(NJ)
            for j in range(NJ):
                dve.wait_ge(po["yahi"], j + 1)
                V.tensor_tensor(ya_lo[:, j, :], ya[:, j, :], ya_hi[:, j, :].bitcast(F32), ALU.subtract).then_inc(po["ya"], 1)

            dve.wait_ge(po["ya"], NJ)
            f = first["merge"]
            with dve.Fori(0, KD // 2) as i:
                own.enter(i, 8)
                for half in range(2):
                    dve.wait_ge(w_done, 6 * i + (f + 3 * half + 3))
                    own.link(divided(sga[:, half, 0, :], 4 * half + 2))
                    own.link(divided(sga[:, half, 1, :], 4 * half + 3))
                    dve.sem_inc(po["g"], 1)
                    dve.wait_ge(po["sig"], 2 * i + (half + 1))
                    own.link(V.tensor_tensor(mt[:, half, 0, :], sga[:, half, 0, :], ps[:, 4 * half, :], ALU.mult))
                    own.link(V.tensor_tensor(mt[:, half, 1, :], sga[:, half, 1, :], ps[:, 4 * half + 1, :], ALU.mult))
                    V.tensor_tensor(mt[:, half, 1, :], mt[:, half, 0, :], mt[:, half, 1, :], ALU.add).then_inc(po["mg_t"], 1)
                    dve.wait_ge(po["mg_hi"], 2 * i + (half + 1))
                    V.tensor_tensor(tile(mg_lo, 2 * i + half), mt[:, half, 1, :], tile(mg_hi, 2 * i + half).bitcast(F32),
                                    ALU.subtract).then_inc(po["mg"], 1)
            own.leave(KD // 2)
            add_to_x(2, first["up1"], 1.0, "ffn2_norm")
            sum_up(2)
            ffn_up(1, "up1")
            add_to_x(3, first["pair0"], 0.5)
            norm(3, "x", "final_norm")
            norm(4, "h", "even_norm_2")

            def pairs(name, ls, gs):
                f = first[name]
                with dve.Fori(0, 4) as i:
                    for s in range(2):
                        dve.wait_ge(w_done, 4 * i + (f + 2 * s + 1))
                        divided(tile(left, 2 * i + s), 2 * s).then_inc(ls, 1)
                        dve.wait_ge(w_done, 4 * i + (f + 2 * s + 2))
                        divided(tile(right, 2 * i + s), 2 * s + 1).then_inc(gs, 1)

            pairs("pair0", ev["l0"], ev["g0"])
            for g in range(4):
                for e in range(2):
                    dve.wait_ge(ev["sqmm"], 2 * g + e + 1)
                    if g >= 1:
                        dve.wait_ge(ev["fwmm"], 2 * g)
                    V.tensor_copy(fmix[:, e, :], ps[:, 4 + e, :]).then_inc(ev["fmix"], 1)
                for e in range(2):
                    m = 2 * g + e
                    dve.wait_ge(ev["fwmm"], m + 1)
                    if m == 0:
                        dve.wait_ge(ev["r0"], KD)
                    if g >= 1:
                        dve.wait_ge(ev["z"], m - 1)
                    V.tensor_tensor(tmp[:, e, :], ps[:, 6 + e, :], right[:, m, :], ALU.mult).then_inc(ev["t"], 1)
                    dve.wait_ge(ev["hi"], m + 1)
                    V.tensor_tensor(z_lo[:, m, :], tmp[:, e, :], z_hi[:, m, :].bitcast(F32), ALU.subtract).then_inc(ev["z"], 1)
            add_to_x(5, first["pair1"], 1.0)
            pairs("pair1", ev["l1"], ev["g1"])
            f = first["kv"]
            for s in range(2):
                dve.wait_ge(w_done, f + s + 1)
                divided(kt[:, s, :], 4 + s).then_inc(ev["k"], 1)
            dve.wait_ge(ev["col"], 1)
            own.link(V.tensor_copy(mx[:, 32:36], ps[:, 6, ::P]))
            dve.wait_ge(w_done, f + 4)
            for t in range(QT):
                V.tensor_scalar(vt[:, t, :], ps[:, t, 0:256], mx[:, 32 + t:33 + t], None, ALU.mult).then_inc(ev["v"], 1)

            def scale_head(u, src, gain):
                dve.wait_ge(at["root"], u + 1)
                own.link(V.reciprocal(sq[:, 1, :], root[:, 0, :]))
                V.scalar_tensor_tensor(out=tmp[:, 0, :], in0=src, scalar=gain, in1=sq[:, 1, :],
                                       op0=ALU.mult, op1=ALU.mult).then_inc(at["qn"], 1)

            def rotate(u, out):
                dve.wait_ge(at["rot"], u + 1)
                own.link(V.tensor_tensor(sq[:, 1, :], ps[:, 3, :], rope_s[:, 1, :], ALU.mult))
                own.link(V.tensor_tensor(tmp[:, 0, :], tmp[:, 0, :], rope_s[:, 0, :], ALU.mult))
                V.tensor_tensor(out, tmp[:, 0, :], sq[:, 1, :], ALU.add).then_inc(at["qr"], 1)

            def z_part(v, i, g):
                dve.wait_ge(at["pv"], v + 1)
                V.tensor_tensor(tmp[:, 1, :], ps[:, 2, :], tile(right, i + 4 * g), ALU.mult).then_inc(at["t"], 1)
                dve.wait_ge(at["hi"], v + 1)
                V.tensor_tensor(tile(z_lo, i + 4 * g), tmp[:, 1, :], tile(z_hi, i + 4 * g).bitcast(F32), ALU.subtract
                                ).then_inc(at["z"], 1)
                dve.wait_ge(at["z"], v + 1)

            def head(v, i, g, is_first=False, is_last=False):
                o = 16 * g
                for t in range(QT):
                    dve.wait_ge(at["smm"], QT * v + (t + 1))
                    own.link(V.tensor_reduce(mx[:, o + 8 + t:o + 9 + t], ps[:, 4 + t, :], AX_X, ALU.max))
                    V.tensor_scalar(mx[:, o + t:o + t + 1], mx[:, o + 8 + t:o + 9 + t], -(P ** -0.5), None, ALU.mult
                                    ).then_inc(at["max"], 1)
                if not is_last:
                    scale_head(v + 3, tile(left, i + 4 if g == 0 else i + 1), col(par, "q_gain_2"))
                for t in range(QT):
                    dve.wait_ge(at["exp"], QT * v + (t + 1))
                    own.link(V.reciprocal(mx[:, o + 12 + t:o + 13 + t], mx[:, o + 4 + t:o + 5 + t]))
                    V.tensor_scalar(prob[:, g, t, :], prob[:, g, t, :], mx[:, o + 12 + t:o + 13 + t], None, ALU.mult
                                    ).then_inc(at["prob"], 1)
                if not is_last:
                    rotate(v + 3, qr[:, 1 - g, :])
                if not is_first:
                    z_part(v - 1, i if g else i - 1, 1 - g)

            dve.wait_ge(at["rope"], 48)
            for u in range(2):
                scale_head(u, kt[:, u, :], col(par, "k_gain_2"))
                rotate(u, kt[:, u, :])
            scale_head(2, left[:, 0, :], col(par, "q_gain_2"))
            rotate(2, qr[:, 0, :])
            head(0, 0, 0, is_first=True)
            head(1, 0, 1)
            with dve.Fori(0, 2) as i:
                own.enter(i, 2 * (3 + 2 * QT))
                for g in range(2):
                    head(2 * i + (2 + g), i + 1, g)
            own.leave(2)
            head(6, 3, 0)
            head(7, 3, 1, is_last=True)
            z_part(7, 3, 1)
            add_to_x(6, first["rnn"], 1.0, "odd_norm_2")
            sum_up(5)

            lm = par[:, COLS["rglru_lambda_2"]:COLS["rglru_lambda_2"] + 32]
            own.link(V.tensor_scalar(lam[:, 0, :], lm, -1.0, None, ALU.mult))
            own.link(V.tensor_tensor(lam[:, 0, :], lam[:, 0, :], lm, ALU.max))
            own.link(V.memset(xp[:], 0.0))
            dve.sem_inc(rg["lexp"], 1)
            dve.wait_ge(rg["lexp"], 2)
            own.link(V.tensor_scalar(lam[:, 2, :], lam[:, 1, :], 2.0, None, ALU.add))
            own.link(V.reciprocal(lam[:, 2, :], lam[:, 2, :]))
            own.link(V.tensor_tensor(lam[:, 2, :], lam[:, 2, :], lam[:, 1, :], ALU.mult))
            own.link(V.tensor_tensor(lam[:, 3, :], lam[:, 2, :], lam[:, 2, :], ALU.mult))
            own.link(V.tensor_scalar(lam[:, 4, :], lam[:, 3, :], 1.0 / 17, 1.0 / 15, ALU.mult, ALU.add))
            for k in (13, 11, 9, 7, 5, 3, 1):
                own.link(V.tensor_tensor(lam[:, 4, :], lam[:, 4, :], lam[:, 3, :], ALU.mult))
                own.link(V.tensor_scalar(lam[:, 4, :], lam[:, 4, :], 1.0 / k, None, ALU.add))
            own.link(V.tensor_tensor(lam[:, 4, :], lam[:, 4, :], lam[:, 2, :], ALU.mult))
            own.link(V.tensor_scalar(lam[:, 5, :], lm, -1.0, 0.0, ALU.mult, ALU.max))
            own.link(V.scalar_tensor_tensor(out=lam[:, 5, :], in0=lam[:, 4, :], scalar=2.0, in1=lam[:, 5, :],
                                            op0=ALU.mult, op1=ALU.add))
            own.link(V.tensor_scalar(lam[:, 5, :], lam[:, 5, :], 8.0, None, ALU.mult))

            f = first["rnn"]

            def values(n, b, s):
                dve.wait_ge(w_done, n + (s + 1))
                divided(xp[:, s, 2:T + 2], s).then_inc(rg["x"], 1)
                dve.wait_ge(rg["x"], b + 1)
                if type(b) is not int or b >= 2:
                    dve.wait_ge(rg["gmm"], b - 1)
                own.link(V.tensor_scalar(xc[:, s, :], xp[:, s, 0:T], col(par, "conv_w_2", b), col(par, "conv_b_2", b),
                                         ALU.mult, ALU.add))
                for tap in range(1, 4):
                    own.link(V.scalar_tensor_tensor(out=xc[:, s, :], in0=xp[:, s, tap:T + tap],
                                                    scalar=col(par, "conv_w_2", b + 16 * tap), in1=xc[:, s, :],
                                                    op0=ALU.mult, op1=ALU.add))
                dve.sem_inc(rg["xc"], 1)

            def gate(n, b, s):
                dve.wait_ge(w_done, n + (s + 3))
                divided(sgate[:, s, :], 2 + s).then_inc(rg["g"], 1)

            def rates(b, s):
                dve.wait_ge(rg["ri"], 4 * b + 4)
                for d in range(2):
                    V.tensor_scalar(ri[:, s, 2 * d, :], ri[:, s, 2 * d, :], lam[:, 5, bass.ds(b + 16 * d, 1)], None, ALU.mult
                                    ).then_inc(rg["nla"], 1)
                    own.link(V.tensor_tensor(ri[:, s, 2 * d + 1, :], ri[:, s, 2 * d + 1, :], xc[:, s, :], ALU.mult))

            def recurrences(b):
                for s in range(2):
                    for d in range(2):
                        dve.wait_ge(rg["a2"], 2 * b + (2 * s + d + 1))
                        own.link(V.scalar_tensor_tensor(out=th[:, s, d, :], in0=ri[:, s, 2 * d, :], scalar=1.0,
                                                        in1=th[:, s, d, :], op0=ALU.add, op1=ALU.mult))
                        dve.sem_inc(rg["w"], 1)
                for s in range(2):
                    for d in range(2):
                        dve.wait_ge(rg["root"], 2 * b + (2 * s + d + 1))
                        own.link(V.tensor_tensor(th[:, s, d, :], th[:, s, d, :], ri[:, s, 2 * d + 1, :], ALU.mult))
                        o = slice(None, None, -1) if d else slice(None)
                        own.link(V.tensor_tensor_scan(ri[:, s, 2 * d, o], aa[:, s, d, o], th[:, s, d, o], 0.0,
                                                      ALU.mult, ALU.add))
                    own.link(V.tensor_tensor(ri[:, s, 0, :], ri[:, s, 0, :], ri[:, s, 2, :], ALU.add))
                    dve.wait_ge(rg["sg"], b + (s + 1))
                    own.link(V.tensor_tensor(ri[:, s, 2, :], ri[:, s, 0, :], sgate[:, s, :], ALU.mult))
                    dve.sem_inc(rg["t"], 1)

            def rests(b):
                for s in range(2):
                    dve.wait_ge(rg["hi"], b + (s + 1))
                    V.tensor_tensor(tile(y_lo, b + s), ri[:, s, 2, :], tile(y_hi, b + s).bitcast(F32), ALU.subtract
                                    ).then_inc(rg["z"], 1)
                    dve.wait_ge(rg["z"], b + (s + 1))
                    dve.sem_inc(rg["y"], 1)

            for s in range(2):
                values(f, s, s)
            for s in range(2):
                gate(f, s, s)
            with dve.Fori(0, NRB // 2 - 1) as i:
                own.enter(i, 2 * (2 + 4) + 4 + 2 * (2 * 2 + 2))
                for s in range(2):
                    rates(2 * i + s, s)
                    values(4 * i + (f + 4), 2 * i + (2 + s), s)
                recurrences(2 * i)
                rests(2 * i)
                for s in range(2):
                    gate(4 * i + (f + 4), 2 * i + (2 + s), s)
            own.leave(NRB // 2 - 1)
            for s in range(2):
                rates(NRB - 2 + s, s)
            recurrences(NRB - 2)
            rests(NRB - 2)
            add_to_x(7, NBLOCKS, 1.0)
            norm(6, "out", "final_norm_2")


def weight_stream(w):
    import numpy as np

    def by_output(m, cols):
        k = m.shape[0] // 128
        return m[:, cols].reshape(k, 128, -1, 128).transpose(2, 1, 0, 3)

    def by_input(m):
        return m.reshape(m.shape[0] // 128, 128, 8, 128)

    def turns(*parts):
        return np.stack(parts, 1).reshape(-1, 128, 8, 128)

    c = slice
    w_in = w["w_in"][0]
    conv, rwkv = 3 * 512, 3 * 512 + 1792
    even = w["even_w_in_2"][0]
    odd = w["odd_w_in_2"][0]
    oa, ob = by_output(w["w_out_a"][0], c(None)), by_output(w["w_out_b"][0], c(None))
    out_ab = np.concatenate([oa, ob], axis=2)
    v = even[:, 3328:3584].reshape(2, 4, 128, 256).transpose(0, 2, 1, 3).reshape(2, 128, 8, 128)
    parts = [
        turns(by_output(w["ffn1_w_gate"][0], c(None)), by_output(w["ffn1_w_up"][0], c(None))),
        by_input(w["ffn1_w_down"][0]),
        turns(by_output(w_in, c(512, 1024)), by_output(w_in, c(1024, 1536)), by_output(w_in, c(0, 512))),
        by_output(w_in, c(conv, rwkv)),
        turns(out_ab, by_output(w_in, c(rwkv, rwkv + 1024)), by_output(w_in, c(rwkv + 1024, rwkv + 2048))),
        by_input(w["w_o"][0]),
        turns(by_output(w["ffn2_w_gate"][0], c(None)), by_output(w["ffn2_w_up"][0], c(None))),
        by_input(w["ffn2_w_down"][0]),
        turns(by_output(even, c(0, 1024)), by_output(even, c(1024, 2048))),
        by_input(w["even_w_out_2"][0])[:8],
        turns(by_output(even, c(2048, 3072)), by_output(even, c(3584, 4608))),
        by_output(even, c(3072, 3328)),
        v,
        by_input(w["even_w_out_2"][0])[8:],
        np.stack([by_output(odd, c(k * 2048, (k + 1) * 2048)).reshape(8, 2, 128, 8, 128) for k in range(2)], 1),
        by_input(w["odd_w_out_2"][0]),
    ]
    return np.ascontiguousarray(np.concatenate([p.reshape(-1, 128, 1024) for p in parts]))


def constants():
    import numpy as np

    f = np.float32
    bones = np.kron(np.eye(2), np.ones((64, 64)))
    perm = np.zeros((128, 128))
    for half in (0, 64):
        for i in range(32):
            perm[half + i + 32, half + i] = -1.0
            perm[half + i, half + i + 32] = 1.0
    mats = np.stack([np.ones((128, 128)), bones, np.eye(128), perm], 1).astype(f)
    r, q = np.arange(128)[:, None], np.arange(128)[None, :]
    levels = []
    for l in range(7):
        low = (r // (2 << l) == q // (2 << l)) & (r // (1 << l) > q // (1 << l))
        levels += [low, low.T]
    tri = [r < q, r <= q, r < q, r <= q]
    masks = np.stack(levels + tri, 1).reshape(128, -1).astype(np.int32)
    inv = (f(10000.0) ** (-np.arange(0, 64, 2, dtype=f) / f(64))).astype(f)
    t = np.arange(512)
    ang = np.stack([(t // 64).astype(f)[:, None] * inv, (t % 64).astype(f)[:, None] * inv])
    full = np.concatenate([ang[0].T, ang[0].T, ang[1].T, ang[1].T])
    rope = np.stack([np.cos(full.astype(np.float64)), np.sin(full.astype(np.float64))], 1).astype(f)
    ch = 2 * np.pi * np.outer(np.arange(256), np.arange(256)) / 256
    sq = 2 * np.pi * np.outer(np.arange(512), np.arange(512)) / 512
    dft_c = np.concatenate([np.cos(ch), -np.sin(ch)], 1) / 16.0
    dft_s = np.concatenate([np.cos(sq), np.sin(sq)], 0) / np.sqrt(512.0)
    dft_c = dft_c.reshape(2, 128, 512).transpose(1, 0, 2).astype(f)
    dft_s = dft_s.reshape(8, 128, 512).transpose(1, 0, 2).astype(f)
    return mats, masks, rope, dft_c, dft_s


def kernel(**inputs):
    import numpy as np
    import concourse.bacc as bacc
    from concourse.bass_utils import run_bass_kernel_spmd

    w = {k: np.asarray(v) for k, v in inputs.items()}
    par = np.zeros((NCOLS, 128), np.float32)
    for name, at in COLS.items():
        if name in w:
            v = w[name].reshape(-1, 128)
            par[at:at + v.shape[0]] = v
    par[COLS["eps_rms"]], par[COLS["eps_gn"]] = 1e-6, 64e-5
    mats, masks, rope, dft_c, dft_s = constants()
    gates = np.stack([w["gate_a_w_2"][0, 0], w["gate_x_w_2"][0, 0], w["gate_a_w_2"][0, 1], w["gate_x_w_2"][0, 1]])
    gates = gates.transpose(1, 2, 0, 3)
    gates = np.concatenate([gates, gates[:2]])
    fw = w["fourier_w_2"][0].reshape(4, 2, 128, 2, 128).transpose(2, 0, 1, 3, 4).reshape(128, 16, 128)
    arrays = {
        "xT": w["x"][0].T.reshape(8, 128, 512).transpose(1, 0, 2),
        "wstream": weight_stream(w),
        "params": par.T,
        "mats": mats,
        "masks": masks,
        "lora": np.concatenate([w["w_decay_up"][0], w["w_iclr_up"][0]], 0),
        "gup": w["w_gate_up"][0],
        "rope": rope,
        "dft_c": dft_c,
        "dft_s": dft_s,
        "fw": fw,
        "rgates": gates,
    }
    from concourse import mybir as mb
    nc = bacc.Bacc("TRN2", target_bir_lowering=False, num_devices=1)
    aps, feed = [], {}
    for name, a in arrays.items():
        feed[name] = np.ascontiguousarray(a)
        aps.append(nc.dram_tensor(name, a.shape, mb.dt.from_np(a.dtype), kind="ExternalInput").ap())
    aps.append(nc.dram_tensor("outT", (128, 8, 512), mb.dt.float32, kind="ExternalOutput").ap())
    program(nc, *aps)
    got = run_bass_kernel_spmd(nc, [feed], core_ids=[0]).results[0]["outT"]
    return np.ascontiguousarray(got.transpose(1, 0, 2).reshape(1024, 512).T).reshape(1, 512, 1024)
```

```python
from contextlib import ExitStack

import concourse.bass as bass
from concourse import mybir

ACT = mybir.ActivationFunctionType
ALU = mybir.AluOpType
AX_X = mybir.AxisListType.X
F32 = mybir.dt.float32
FR = mybir.dt.float32r
I32 = mybir.dt.int32
I8 = mybir.dt.int8

P = 128
T = 512
D = 1024
KD = D // P
KF = 2816 // P
BLK = 8
HEADS, HS = 8, 64
NJ = HEADS * HS // P
CH = 128
NCH = T // CH
EPS_RMS, EPS_GN = 1e-6, 64e-5
LEVELS = 7
QT = T // P
NRB = 16
INV_SQRT_E = 0.6065306597126334

COLS = {}
_at = 0
for _name, _n in (
    ("ffn1_norm", 8), ("mix_norm", 8), ("ffn2_norm", 8), ("final_norm", 8), ("even_norm_2", 8),
    ("odd_norm_2", 8), ("final_norm_2", 8), ("conv_w", 12), ("mu_b", 14), ("w0", 4), ("a0", 4),
    ("k_k", 4), ("k_a", 4), ("r_k", 4), ("ln_x_w", 4), ("ln_x_b", 4), ("q_gain_2", 1), ("k_gain_2", 1),
    ("conv_w_2", 64), ("conv_b_2", 16), ("gate_a_b_2", 32), ("gate_x_b_2", 32), ("rglru_lambda_2", 32),
    ("eps_rms", 1), ("eps_gn", 1),
):
    COLS[_name] = _at
    _at += _n
NCOLS = _at

N_UP, N_DOWN = 2 * KF, KF
N_MIX, N_CONV, N_GATES, N_MERGE, N_WO = 14, 12, 16, 8, 8
K0, R0, V0 = 2, 6, 10
V_BANKS = (5, 6, 0, 1)
BONUS, ROOTS = (4, 5, 6, 3), (2, 3, 6, 7)
GATES = 4
N_PAIR, N_QK, N_HALF, N_RNN = 16, 10, 8, 32
NBLOCKS = 2 * (N_UP + N_DOWN) + N_MIX + N_CONV + N_GATES + N_MERGE + N_WO + N_PAIR + N_QK + 2 + 8 + 2 * N_HALF + N_RNN + 16


def col(par, name, i=0, n=1):
    return par[:, bass.ds(COLS[name] + i, n)]


def tile(buf, i):
    return buf[:, bass.ds(i, 1), :].rearrange("p a t -> p (a t)")


class Chain:

    def __init__(self, eng, sem):
        self.eng, self.sem, self.base, self.k, self.at = eng, sem, 0, 0, None

    def link(self, ins):
        ins.then_inc(self.sem, 1)
        self.k += 1
        self.eng.wait_ge(self.sem, self.base + self.k if self.at is None else self.at + (self.base + self.k))

    def enter(self, i, per):
        self.base, self.k, self.per, self.at = self.base + self.k, 0, per, i * per

    def leave(self, trips):
        assert self.k == self.per, (self.k, self.per)
        self.base, self.k, self.at = self.base + trips * self.per, 0, None


def program(nc, gate_store, xT, wstream, params, mats, masks, lora, gup, rope, dft_c, dft_s, fw, fw_mid, rgates, outT):
    with ExitStack() as ctx:
        def sb(name, shape, dt=F32, on=ctx):
            return on.enter_context(nc.sbuf_tensor(name, shape, dt))

        def sem(name):
            return ctx.enter_context(nc.semaphore(name))

        ps = ctx.enter_context(nc.psum_tensor("ps", [P, 8, T], F32))

        x = sb("x", [P, KD, T])
        w_raw = sb("w_raw", [P, 2, BLK * P])
        w_hi = sb("w_hi", [P, 2, BLK * P], FR)
        w_lo = sb("w_lo", [P, 2, BLK * P], FR)
        par = sb("par", [P, NCOLS])
        mat = sb("mat", [P, 5, P])
        ones, bones, ident, perm, spread = (mat[:, k, :] for k in range(5))
        lev8 = sb("lev8", [P, LEVELS, 2, P], I8)
        tri8 = sb("tri8", [P, 4, P], I8)
        sq = sb("sq", [P, 2, T])
        root = sb("root", [P, 1, T])
        rinv = sb("rinv", [P, 1, T])
        tmp = sb("tmp", [P, 2, T])
        gain2 = sb("gain2", [P, KD])
        eps2 = sb("eps2", [P, 1])
        lam = sb("lam", [P, 6, 32])
        h_hi = sb("h_hi", [P, KD, T], FR)
        h_lo = sb("h_lo", [P, KD, T], FR)

        with ExitStack() as a:
            hid_hi = sb("hid_hi", [P, KF, T], FR, a)
            hid_lo = sb("hid_lo", [P, KF, T], FR, a)
            gate_s = sb("gate_s", [P, 2, T], F32, a)
            hid_t = sb("hid_t", [P, 2, T], F32, a)
            m32 = sb("m32", [P, (LEVELS * 2 + 4) * P], I32, a)
        with ExitStack() as a:
            scores = sb("scores", [P, HEADS, 4, P], F32, a)
            xx = sb("xx", [P, HEADS, 2, P], F32, a)
            t1 = sb("t1", [P, HEADS, P], F32, a)
            ar = sb("ar", [P, NJ, 2, CH], F32, a)
            bc = sb("bc", [P, NJ, CH], F32, a)
            kc_ = sb("kc_", [P, NJ, CH], F32, a)
            tok = sb("tok", [P, 3, T], F32, a)
            st = sb("st", [P, NJ, HS], F32, a)
            st0 = sb("st0", [P, NJ, HS], F32, a)
            pe_ = sb("pe_", [P, NJ, CH + 1], F32, a)
            pn = sb("pn", [P, NJ, CH + 1], F32, a)
            rmid = sb("rmid", [P, NJ, 1], F32, a)
            pend = sb("pend", [P, NJ, 1], F32, a)
            ya = sb("ya", [P, NJ, T], F32, a)
            mix = sb("mix", [P, 14, T], F32, a)
            wd = sb("wd", [P, NJ, T], F32, a)
            kk = sb("kk", [P, NJ, T], F32, a)
            bb = sb("bb", [P, NJ, T], F32, a)
            gg = sb("gg", [P, NJ, T], F32, a)
        with ExitStack() as a:
            padc = sb("padc", [P, 2, T + 2], F32, a)
            csb = sb("csb", [P, 2, T], F32, a)
            padm = sb("padm", [P, 2, T + 1], F32, a)
            dif = sb("dif", [P, 2, T], F32, a)
            kroot = sb("kroot", [P, NJ, T], F32, a)
        lora_s, gup_s = tok[:, 0, :], tok[:, 1, :]
        with ExitStack() as a:
            ya_hi = sb("ya_hi", [P, NJ, T], FR, a)
            ya_lo = sb("ya_lo", [P, NJ, T], FR, a)
            yb_hi = sb("yb_hi", [P, NJ, T], FR, a)
            yb_lo = sb("yb_lo", [P, NJ, T], FR, a)
            sga = sb("sga", [P, 2, 2, T], F32, a)
            gap = sb("gap", [P, 9, T], F32, a)
            mg_hi = sb("mg_hi", [P, KD, T], FR, a)
            mg_lo = sb("mg_lo", [P, KD, T], FR, a)
            mt = sb("mt", [P, 2, 2, T], F32, a)
        with ExitStack() as a:
            z_hi = sb("z_hi", [P, KD, T], FR, a)
            z_lo = sb("z_lo", [P, KD, T], FR, a)
            left = sb("left", [P, KD + 2, T], F32, a)
            right = sb("right", [P, KD, T], F32, a)
            with ExitStack() as b:
                dftc = sb("dftc", [P, 2, 257], F32, b)
                dfts = sb("dfts", [P, 2 * QT, T], F32, b)
                fws = sb("fws", [P, 16, P], F32, b)
                fw128 = sb("fw128", [P, KD, P], F32, b)
                chan = sb("chan", [P, QT, 256], F32, b)
                mid = sb("mid", [P, QT, 4], F32, b)
                ymid = sb("ymid", [P, T], F32, b)
                fmix = sb("fmix", [P, 4, T + 1], F32, b)
            with ExitStack() as b:
                vt = sb("vt", [P, QT, 256], F32, b)
                rope_s = sb("rope_s", [P, 2, T], F32, b)
                prob = sb("prob", [P, 2, QT, T], F32, b)
                probT = sb("probT", [P, QT, T], F32, b)
                qr = sb("qr", [P, 2, T], F32, b)
                qn = sb("qn", [P, 2, T], F32, b)
                mx = sb("mx", [P, 36], F32, b)
        with ExitStack() as a:
            y_hi = sb("y_hi", [P, NRB, T], FR, a)
            y_lo = sb("y_lo", [P, NRB, T], FR, a)
            rg_w = sb("rg_w", [P, 2, 4, P], F32, a)
            xp = sb("xp", [P, 2, T + 3], F32, a)
            xc = sb("xc", [P, 2, T], F32, a)
            sgate = sb("sgate", [P, 2, T], F32, a)
            ri = sb("ri", [P, 2, 4, T], F32, a)
            aa = sb("aa", [P, 2, 2, T], F32, a)
            th = sb("th", [P, 2, 2, T], F32, a)

        s_x = [sem(f"x_loaded_{q}") for q in range(4)]
        s_mat = sem("matrices_loaded")
        s_masks = sem("masks_loaded")
        s_par = sem("params_loaded")
        landed = [sem(f"weights_landed_{s}") for s in range(2)]
        w_hi_done = sem("w_hi_done")
        w_split = sem("w_split")
        w_done = sem("w_done")
        v_chain = sem("vector_chain")
        a_chain = sem("scalar_chain")
        s_pass = sem("vector_passed")
        s_act_pass = sem("scalar_passed")
        s_pool_pass = sem("pool_passed")
        nrm = {q: sem(f"norm_{q}") for q in ("x", "sq", "acc", "ss", "root", "hi", "h")}

        def x_at(k):
            return KD * (k - 1 if k < 5 else k)

        def h_at(k):
            return KD * (k if k < 3 else k - 1)

        ffn = [{q: sem(f"ffn{k}_{q}") for q in ("g", "u", "silu", "t", "hi", "hid")} for k in range(2)]
        mx_s = {q: sem(f"mixer_{q}") for q in (
            "small_loaded", "ya", "raw", "mix", "lora_in", "lora_mm", "lora_ev", "kk_sq", "kk_w", "gd", "gsig",
            "spilled_0", "spilled_1", "refilled_0", "refilled_1")}
        rw = {q: sem(f"rwkv_{q}") for q in (
            "ops", "vc", "reset", "tr", "tok", "mat", "sc", "t1mm", "t1", "xmm", "xx", "rhsmm", "rhs", "umm", "u",
            "ysmm", "y", "s")}
        po = {q: sem(f"post_{q}") for q in (
            "mean", "yc", "sq", "var", "root", "rcp", "bc", "rk", "bonus", "rkv", "t", "hi", "done", "yahi", "ya", "mg_t", "mg_hi", "mg")}
        ev = {q: sem(f"even_{q}") for q in ("loaded", "l0", "g0", "r0", "col", "v", "chmm", "chan", "sqmm",
                                             "fmix", "fwmm", "mid", "midmm", "ymid", "t", "hi", "z")}
        at = {q: sem(f"attn_{q}") for q in ("rope", "raw", "sq", "ssmm", "root", "qn", "rot", "qk", "qr", "ag", "silu", "smm", "max", "exp", "prob",
                                             "tr", "pt", "pv", "t", "hi", "z")}
        rg = {q: sem(f"rglru_{q}") for q in ("w0", "w1", "x", "g", "sg", "lexp", "xc", "gmm", "ri", "nla", "a", "a2", "th",
                                              "w", "root", "y", "t", "hi", "z")}
        s_bank = sem("residual_bank_done")
        s_out_t = sem("out_tile")
        s_out = sem("out_stored")

        block = ctx.enter_context(nc.Block())

        first = {}
        n = 0
        for name, size in (("up0", N_UP), ("down0", N_DOWN), ("mix", N_MIX), ("conv", N_CONV), ("gates", N_GATES), ("merge", N_MERGE),
                           ("wo", N_WO), ("up1", N_UP), ("down1", N_DOWN), ("pair0", N_PAIR), ("eo0", N_HALF),
                           ("qk", N_QK), ("v", 2), ("ag", 8), ("eo1", N_HALF), ("rnn", N_RNN), ("ro", 16)):
            first[name] = n
            n += size
        assert n == NBLOCKS and NBLOCKS % 2 == 0

        @block.sync
        def _(sp):
            sp.dma_start(par[:], params).then_inc(s_par, 16)
            for q in range(4):
                sp.dma_start(x[:, 2 * q:2 * q + 2, :], xT[:, 2 * q:2 * q + 2, :]).then_inc(s_x[q], 16)
                if q == 0:
                    sp.dma_start(w_raw[:, 0, :], wstream[0]).then_inc(landed[0], 16)
            sp.dma_start(w_raw[:, 1, :], wstream[1]).then_inc(landed[1], 16)
            sp.dma_start(mat[:], mats).then_inc(s_mat, 16)
            sp.dma_start(m32[:], masks).then_inc(s_masks, 16)
            with sp.Fori(0, NBLOCKS // 2 - 1) as i:
                for s in range(2):
                    sp.wait_ge(w_split, 2 * i + (s + 1))
                    sp.dma_start(w_raw[:, s, :], wstream[bass.ds(2 * i + (2 + s), 1)].rearrange("a p q -> p (a q)")
                                 ).then_inc(landed[s], 16)
            for m in range(KD):
                sp.wait_ge(s_out_t, m + 1)
                sp.dma_start(outT[:, m, :], x[:, m, :]).then_inc(s_out, 16)
            sp.wait_ge(s_out, 16 * KD)

        @block.gpsimd
        def _(pool):
            def split(s):
                nc.gpsimd.tensor_scalar(w_hi[:, s, :], w_raw[:, s, :], 1.0, 0.0, ALU.mult, ALU.add).then_inc(w_hi_done, 1)

            def rest(s):
                nc.gpsimd.tensor_tensor(w_lo[:, s, :], w_raw[:, s, :], w_hi[:, s, :].bitcast(F32), ALU.subtract
                                        ).then_inc(w_split, 1)

            for s in range(2):
                pool.wait_ge(landed[s], 16)
                split(s)
                pool.wait_ge(w_hi_done, s + 1)
                rest(s)
            with pool.Fori(0, NBLOCKS // 2 - 1) as i:
                for s in range(2):
                    pool.wait_ge(landed[s], 16 * i + 32)
                    pool.wait_ge(w_done, 2 * i + (s + 1))
                    pool.sem_inc(s_pool_pass, 1)
                    split(s)
                    pool.wait_ge(w_hi_done, 2 * i + (s + 3))
                    rest(s)

        @block.tensor
        def _(pe):
            mm = nc.tensor.matmul

            def mm3(out, s, k, hi, lo, start, stop, n=P):
                w = slice(k * n, (k + 1) * n)
                mm(out, w_hi[:, s, w], hi, start=start, stop=False)
                mm(out, w_hi[:, s, w], lo, start=False, stop=False)
                return mm(out, w_lo[:, s, w], hi, start=False, stop=stop)

            def dense(n, s, bank, hi, lo):
                pe.wait_ge(w_split, n + 1)
                for k in range(BLK):
                    last = mm3(ps[:, bank, :], s, k, hi[:, k, :], lo[:, k, :], k == 0, k == BLK - 1)
                last.then_inc(w_done, 1)

            def sum_squares(k):
                pe.wait_ge(nrm["acc"], (KD - 1) * (k + 1))
                mm(ps[:, 7, :], ones, root[:, 0, :], start=True, stop=True).then_inc(nrm["ss"], 1)

            def dense_third(n, sums):
                pe.wait_ge(w_split, n + 1)
                for k in range(BLK):
                    if k == BLK // 2:
                        sums()
                    last = mm3(ps[:, 2, :], 0, k, h_hi[:, k, :], h_lo[:, k, :], k == 0, k == BLK - 1)
                last.then_inc(w_done, 1)

            def dense_first(k, n):
                def high(s, m):
                    w = slice(m * P, (m + 1) * P)
                    mm(ps[:, s, :], w_hi[:, s, w], h_hi[:, m, :], start=(m == 0), stop=False)
                    mm(ps[:, s, :], w_lo[:, s, w], h_hi[:, m, :], start=False, stop=False)

                def low(s, m):
                    return mm(ps[:, s, :], w_hi[:, s, m * P:(m + 1) * P], h_lo[:, m, :], start=False, stop=(m == KD - 1))

                pe.wait_ge(w_split, n + 1)
                for m in range(KD):
                    pe.wait_ge(nrm["hi"], h_at(k) + m + 1)
                    high(0, m)
                pe.wait_ge(w_split, n + 2)
                for m in range(KD):
                    pe.wait_ge(nrm["h"], h_at(k) + m + 1)
                    last = low(0, m)
                    if m == KD - 1:
                        last.then_inc(w_done, 1)
                    high(1, m)
                for m in range(KD):
                    last = low(1, m)
                last.then_inc(w_done, 1)

            def residual(name, nk, hi, lo, ready, base=0, free=(), between=None):
                def step(n, s, k, start, stop):
                    pe.wait_ge(ready, k + (base + 1))
                    pe.wait_ge(w_split, n + 1)
                    for m in range(KD):
                        last = mm3(ps[:, m, :], s, m, tile(hi, k), tile(lo, k), start, stop)
                        if stop and m < KD - 1:
                            last.then_inc(s_bank, 1)
                    last.then_inc(w_done, 1)
                f = first[name]
                if between is None:
                    for k in range(2):
                        step(f + k, k, k, k == 0, False)
                else:
                    for k in range(2):
                        pe.wait_ge(ready, k + (base + 1))
                        pe.wait_ge(w_split, f + k + 1)
                        for m in free:
                            mm3(ps[:, m, :], k, m, tile(hi, k), tile(lo, k), k == 0, False)
                        between(k)
                    for k in range(2):
                        for m in range(KD):
                            if m not in free:
                                last = mm3(ps[:, m, :], k, m, tile(hi, k), tile(lo, k), k == 0, False)
                        last.then_inc(w_done, 1)
                with pe.Fori(0, nk // 2 - 2) as i:
                    for s in range(2):
                        step(2 * i + (f + 2 + s), s, 2 * i + (2 + s), False, False)
                for k in range(nk - 2, nk):
                    step(f + k, k % 2, k, False, k == nk - 1)

            def ffn_up(k, name):
                q = ffn[k]
                f = first[name]
                dense_first(2 * k, f)
                dense_third(f + 2, lambda: sum_squares(2 * k))
                dense(f + 3, 1, 3, h_hi, h_lo)
                with pe.Fori(0, KF // 2 - 1) as i:
                    for s in range(4):
                        pe.wait_ge(q["u"] if s % 2 else q["g"], 2 * i + (s // 2 + 1))
                        dense(4 * i + (f + 4 + s), s % 2, s, h_hi, h_lo)

            pe.wait_ge(s_mat, 16)
            ffn_up(0, "up0")
            pe.wait_ge(ffn[0]["u"], KF)
            residual("down0", KF, hid_hi, hid_lo, ffn[0]["hid"])

            f = first["mix"]
            dense_first(1, f)
            dense_third(f + 2, lambda: sum_squares(1))
            dense(f + 3, 1, 3, h_hi, h_lo)
            for s in range(2):
                pe.wait_ge(mx_s["raw"], s + 1)
                dense(f + 4 + s, s, s, h_hi, h_lo)
            with pe.Fori(0, N_MIX // 2 - 3) as i:
                for s in range(2):
                    pe.wait_ge(mx_s["raw"], 2 * i + (s + 5))
                    dense(2 * i + (f + 6 + s), s, s, h_hi, h_lo)
            pe.wait_ge(mx_s["small_loaded"], 32)
            pe.wait_ge(mx_s["lora_in"], 3)
            pe.wait_ge(nrm["root"], 2)
            for n in range(4 * NJ):
                kind, j = n // NJ, n % NJ
                w = slice(j * P, (j + 1) * P)
                if kind == 2:
                    pe.wait_ge(mx_s["kk_sq"], j + 1)
                if n >= 6:
                    pe.wait_ge(mx_s["lora_ev"], n - 5)
                a, b = ((lora_s[0:64, w], sq[0:64, 0, :]), (lora_s[64:128, w], tmp[64:128, 0, :]),
                        (bones, kroot[:, j, :]), (gup_s[:, w], sq[:, 1, :]))[kind]
                mm(ps[:, 2 + n % 6, :], a, b, start=True, stop=True).then_inc(mx_s["lora_mm"], 1)
            f = first["conv"]
            pe.wait_ge(mx_s["raw"], N_MIX)
            for n in range(N_CONV):
                if n == 2:
                    pe.wait_ge(mx_s["lora_ev"], 4 * NJ)
                if n >= 6 and n % 3 == 0:
                    pe.wait_ge(mx_s["ya"], n // 3 - 1)
                dense(f + n, n % 2, n % 6, h_hi, h_lo)

            f = first["gates"]

            def dense_part(n, s, bank, half):
                if half == 0:
                    pe.wait_ge(w_split, n + 1)
                for k in range(4 * half, 4 * half + 4):
                    last = mm3(ps[:, bank, :], s, k, h_hi[:, k, :], h_lo[:, k, :], k == 0, k == BLK - 1)
                if half == 1:
                    last.then_inc(w_done, 1)

            def chunk(c):
                pe.wait_ge(rw["ops"], c + 1)
                pe.wait_ge(rw["vc"], c + 1)
                for q, src in enumerate((bc, kc_, root)):
                    for j in range(NJ):
                        w = slice(j * P, (j + 1) * P)
                        a = src[:, j, :] if q < 2 else root[:, 0, w]
                        last = nc.tensor.transpose(ps[:, q, w], a, ident)
                    last.then_inc(rw["tr"], 1)
                pe.wait_ge(mx_s["ya"], NJ)
                for h in range(HEADS):
                    j, p0 = h // 2, HS * (h % 2)
                    pp = slice(p0, p0 + HS)
                    bank = 4 + h % 4
                    if h >= 4:
                        pe.wait_ge(rw["sc"], HEADS * c + (h - 3))
                    mm(ps[:, bank, 0:256], bc[pp, j, :], ar[pp, j, :, :].rearrange("p a t -> p (a t)"), start=True, stop=True)
                    mm(ps[:, bank, 256:512], kc_[pp, j, :], ar[pp, j, :, :].rearrange("p a t -> p (a t)"),
                       start=True, stop=True).then_inc(rw["mat"], 1)
                if type(c) is not int or c >= 1:
                    pe.wait_ge(mx_s["gd"], GATES * c)
                dense(GATES * c + f, 0, 3, h_hi, h_lo)
                pe.wait_ge(rw["reset"], c + 1)
                pe.wait_ge(rw["tok"], 3 * c + 3)
                pe.wait_ge(rw["sc"], HEADS * c + HEADS)
                for l in range(LEVELS):
                    for g in range(2):
                        if l >= 1:
                            pe.wait_ge(rw["xx"], 4 * LEVELS * c + (4 * (l - 1) + 2 * g + 2))
                        for h in range(4 * g, 4 * g + 4):
                            last = mm(ps[:, g, (h % 4) * P:(h % 4 + 1) * P], scores[:, h, 0, :],
                                      xx[:, h, 0, :] if l else ident, start=True, stop=True)
                        last.then_inc(rw["t1mm"], 1)
                    if l == 0:
                        continue
                    for g in range(2):
                        pe.wait_ge(rw["t1"], 2 * (LEVELS - 1) * c + (2 * l + g - 1))
                        for h in range(4 * g, 4 * g + 4):
                            bank, o = 4 + h // 2, 256 * (h % 2)
                            if l < LEVELS - 1:
                                mm(ps[:, bank, o:o + P], xx[:, h, 1, :], t1[:, h, :], start=True, stop=True)
                            last = mm(ps[:, bank, o + P:o + 2 * P], t1[:, h, :], xx[:, h, 1, :], start=True, stop=True)
                            if h % 2 == 1:
                                last.then_inc(rw["xmm"], 1)
                pe.wait_ge(mx_s["gd"], GATES * c + 1)
                for h in range(HEADS):
                    j, p0 = h // 2, HS * (h % 2)
                    pp = slice(p0, p0 + HS)
                    o = slice(j * HS, (j + 1) * HS)
                    out = ps[:, 2 + h % 2, o]
                    mm(out, ar[pp, j, 0, :], st0[pp, j, :], start=True, stop=False)
                    last = mm(out, scores[:, h, 2, :], tok[:, 2, h * HS:(h + 1) * HS], start=False, stop=True)
                last.then_inc(rw["rhsmm"], 1)
                dense_part(GATES * c + (f + 1), 1, 1, 0)
                pe.wait_ge(rw["xx"], 4 * LEVELS * c + 4 * LEVELS)
                pe.wait_ge(rw["rhs"], c + 1)
                for h in range(HEADS):
                    o = slice(h * HS, (h + 1) * HS)
                    last = mm(ps[:, 0, o], xx[:, h, 1, :], sq[:, 0, o], start=True, stop=True)
                last.then_inc(rw["umm"], 1)
                dense_part(GATES * c + (f + 1), 1, 1, 1)
                pe.wait_ge(rw["u"], c + 1)
                for h in range(HEADS):
                    j, p0 = h // 2, HS * (h % 2)
                    pp = slice(p0, p0 + HS)
                    o = slice(h * HS, (h + 1) * HS)
                    out = ps[pp, 4 + h % 2, j * CH:(j + 1) * CH]
                    mm(out, sq[:, 1, o], scores[:, h, 1, :], start=True, stop=False)
                    mm(out, tok[:, 2, o], scores[:, h, 3, :], start=False, stop=False)
                    mm(out, st0[pp, j, :], ar[pp, j, 1, :], start=False, stop=True)
                for h in range(HEADS):
                    j, p0 = h // 2, HS * (h % 2)
                    pp = slice(p0, p0 + HS)
                    o = slice(h * HS, (h + 1) * HS)
                    out = ps[pp, 6, j * HS:(j + 1) * HS]
                    mm(out, tok[:, 0, o], sq[:, 1, o], start=True, stop=False)
                    last = mm(out, tok[:, 1, o], tok[:, 2, o], start=False, stop=True)
                last.then_inc(rw["ysmm"], 1)
                dense(GATES * c + (f + 2), 0, 7, h_hi, h_lo)
                if type(c) is int:
                    pe.wait_ge(rw["y"], 2 * NCH)
                    for j in range(NJ):
                        mm(ps[:, j, :], bones, wd[:, j, :], start=True, stop=True).then_inc(po["mean"], 1)
                    pe.wait_ge(rw["s"], NCH + 1)
                    for j in range(NJ):
                        pe.wait_ge(po["rk"], j + 1)
                        if j == NJ - 1:
                            pe.wait_ge(po["yc"], NJ)
                        mm(ps[:, BONUS[j], :], bones, mix[:, K0 + j, :], start=True, stop=True).then_inc(po["bonus"], 1)
                    for j in range(NJ):
                        pe.wait_ge(po["sq"], j + 1)
                        last = mm(ps[32 * j:32 * j + 32, 0, :], bones[:, 48:80], kk[:, j, :], start=True, stop=True)
                    last.then_inc(po["var"], 1)
                    pe.wait_ge(mx_s["gd"], GATES * c + 3)
                dense(GATES * c + (f + 3), 1, 7 if type(c) is int else 3, h_hi, h_lo)
                pe.wait_ge(mx_s["gd"], GATES * c + 3)

            pe.wait_ge(mx_s["ya"], NJ - 1)
            with pe.Fori(0, NCH - 1) as c:
                chunk(c)
            chunk(NCH - 1)

            f = first["merge"]
            def merge_a(n, s):
                pe.wait_ge(w_split, n + 1)
                for k in range(NJ):
                    mm3(ps[:, 4 * s, :], s, k, ya_hi[:, k, :], ya_lo[:, k, :], k == 0, k == NJ - 1)

            def merge_b(s, ready=None):
                for k in range(NJ):
                    if ready is not None:
                        pe.wait_ge(ready, k + 1)
                    last = mm3(ps[:, 4 * s + 1, :], s, NJ + k, yb_hi[:, k, :], yb_lo[:, k, :], k == 0, k == NJ - 1)
                last.then_inc(w_done, 1)

            def merge(n, s):
                merge_a(n, s)
                merge_b(s)

            pe.wait_ge(po["root"], 1)
            pe.wait_ge(po["ya"], NJ)
            merge_a(f, 0)
            pe.wait_ge(po["rkv"], NJ)
            pe.wait_ge(mx_s["gd"], GATES * NCH)
            pe.wait_ge(po["rcp"], 1)
            for j in range(NJ):
                q = slice(32 * j, 32 * j + 32)
                mm(ps[:, ROOTS[j], :], spread[q, :], bb[q, 0, :], start=True, stop=True).then_inc(po["bc"], 1)
            merge_a(f + 1, 1)
            for s in range(2):
                merge_b(s, po["done"])
            with pe.Fori(0, 3) as i:
                for s in range(2):
                    pe.wait_ge(po["mg_t"], 2 * i + (s + 1))
                    merge(2 * i + (f + 2 + s), s)
            pe.wait_ge(po["mg_t"], KD)
            residual("wo", KD, mg_hi, mg_lo, po["mg"])

            ffn_up(1, "up1")
            pe.wait_ge(ffn[1]["u"], KF)
            residual("down1", KF, hid_hi, hid_lo, ffn[1]["hid"])

            def pairs(name, ls, gs):
                f = first[name]
                dense_first(4, f)
                dense(f + 2, 0, 2, h_hi, h_lo)
                sum_squares(3)
                pe.wait_ge(nrm["acc"], (KD - 1) * 5)
                mm(ps[:, 6, :], ones, tmp[:, 1, :], start=True, stop=True).then_inc(nrm["ss"], 1)
                dense(f + 3, 1, 3, h_hi, h_lo)
                with pe.Fori(0, 3) as i:
                    for s in range(4):
                        pe.wait_ge(gs if s % 2 else ls, 2 * i + (s // 2 + 1))
                        dense(4 * i + (f + 4 + s), s % 2, s, h_hi, h_lo)

            pairs("pair0", ev["l0"], ev["g0"])
            pe.wait_ge(ev["l0"], KD)
            pe.wait_ge(ev["r0"], KD)
            pe.wait_ge(ev["loaded"], 64)

            def channels(g):
                for t in range(QT):
                    if g >= 1:
                        pe.wait_ge(ev["chan"], QT * (g - 1) + t + 1)
                    for k in range(2):
                        last = mm(ps[:, t, 0:257], left[:, 2 * g + k, t * P:(t + 1) * P], dftc[:, k, :],
                                  start=(k == 0), stop=(k == 1))
                    last.then_inc(ev["chmm"], 1)

            def tokens(g):
                pe.wait_ge(ev["chan"], QT * (g + 1))
                if g >= 1:
                    pe.wait_ge(ev["fmix"], g)
                for part in range(2):
                    for t in range(QT):
                        last = mm(ps[:, 4, :], chan[:, t, P * part:P * part + P], dfts[:, part * QT + t, :],
                                  start=(part == 0 and t == 0), stop=(part == 1 and t == QT - 1))
                last.then_inc(ev["sqmm"], 1)

            def mixed(g):
                pe.wait_ge(ev["fmix"], g + 1)
                for e in range(2):
                    if g >= 1:
                        pe.wait_ge(ev["t"], 2 * g - 1 + e)
                    mm(ps[:, 6 + e, :], fws[:, (2 * g) * 2 + e, :], fmix[:, g, 0:T], start=True, stop=False)
                    mm(ps[:, 6 + e, :], fws[:, (2 * g + 1) * 2 + e, :], fmix[:, g, T:0:-1], start=False, stop=False)
                    mm(ps[:, 6 + e, :], fw128[0:4, 2 * g + e, :], ymid[0:4, :], start=False, stop=True
                       ).then_inc(ev["fwmm"], 1)

            channels(0)
            tokens(0)
            for g in range(1, 4):
                channels(g)
                tokens(g)
                if g == 3:
                    pe.wait_ge(ev["mid"], 4 * QT)
                    for t in range(QT):
                        last = mm(ps[0:4, 5, :], mid[:, t, :], dfts[:, t, :], start=(t == 0), stop=(t == QT - 1))
                    last.then_inc(ev["midmm"], 1)
            pe.wait_ge(ev["ymid"], 1)
            for g in range(4):
                mixed(g)
            pe.wait_ge(ev["t"], KD)
            residual("eo0", KD, z_hi, z_lo, ev["z"])

            pe.wait_ge(nrm["x"], x_at(5))
            f = first["qk"]

            def project(n, s):
                if type(n) is not int or n >= 2:
                    pe.wait_ge(at["raw"], n - 1)
                dense(n + f, s, s, h_hi, h_lo)

            def sum_head(u):
                pe.wait_ge(at["sq"], u + 1)
                if type(u) is not int or u >= 1:
                    pe.wait_ge(at["root"], u)
                mm(ps[:, 2, :], ones, sq[:, 0, :], start=True, stop=True).then_inc(at["ssmm"], 1)

            def swap_halves(u, s):
                pe.wait_ge(at["qn"], u + 1)
                if type(u) is not int or u >= 1:
                    pe.wait_ge(at["qk"], u)
                mm(ps[:, 3, :], perm, qn[:, s, :], start=True, stop=True).then_inc(at["rot"], 1)

            project(0, 0)
            project(1, 1)
            sum_head(0)
            with pe.Fori(0, 4) as i:
                for s in range(2):
                    project(2 * i + (2 + s), s)
                    sum_head(2 * i + (1 + s))
                    swap_halves(2 * i + s, s)
            for t in range(QT):
                last = nc.tensor.transpose(ps[:, 4, t * P:(t + 1) * P], rinv[:, 0, t * P:(t + 1) * P], ident)
            last.then_inc(ev["col"], 1)
            f = first["v"]
            pe.wait_ge(at["raw"], 10)
            for b in range(2):
                pe.wait_ge(w_split, f + 1 + b)
                for t, bank in enumerate(V_BANKS):
                    tt = slice(t * P, (t + 1) * P)
                    for k in range(4):
                        w = slice(k * 256, (k + 1) * 256)
                        kk_ = 4 * b + k
                        mm(ps[:, bank, 0:256], h_hi[:, kk_, tt], w_hi[:, b, w], start=(kk_ == 0), stop=False)
                        mm(ps[:, bank, 0:256], h_lo[:, kk_, tt], w_hi[:, b, w], start=False, stop=False)
                        last = mm(ps[:, bank, 0:256], h_hi[:, kk_, tt], w_lo[:, b, w], start=False, stop=(kk_ == KD - 1))
                last.then_inc(w_done, 1)
                if b == 0:
                    sum_head(9)
                    swap_halves(8, 0)

            def score(v, g):
                pe.wait_ge(at["qr"], v + 1)
                if type(v) is not int or v >= 1:
                    pe.wait_ge(at["exp"], QT * v)
                for t in range(QT):
                    mm(ps[:, 4 + t, :], qr[:, g, t * P:(t + 1) * P], left[:, g, :], start=True, stop=True).then_inc(at["smm"], 1)

            def head_gate(v, s, bank=3):
                if type(v) is not int or v >= 1:
                    pe.wait_ge(at["ag"], v)
                dense(v + first["ag"], s, bank, h_hi, h_lo)

            def turn(v, g):
                for t in range(QT):
                    pe.wait_ge(at["prob"], QT * v + (t + 1))
                    if type(v) is not int or QT * v + t >= 2:
                        pe.wait_ge(at["pt"], QT * v + (t - 1))
                    for k in range(QT):
                        last = nc.tensor.transpose(ps[:, t % 2, k * P:(k + 1) * P], prob[:, g, t, k * P:(k + 1) * P], ident)
                    last.then_inc(at["tr"], 1)

            def weigh(v, g):
                pe.wait_ge(at["pt"], QT * v + QT)
                if type(v) is not int or v >= 1:
                    pe.wait_ge(at["t"], v)
                for t in range(QT):
                    last = mm(ps[:, 2, :], vt[:, t, g * P:(g + 1) * P], probT[:, t, :], start=(t == 0), stop=(t == QT - 1))
                last.then_inc(at["pv"], 1)

            def head(v, g):
                score(v, g)
                head_gate(v, g)
                turn(v - 1, 1 - g)
                weigh(v - 1, 1 - g)

            head_gate(0, 0, 7)
            swap_halves(9, 1)
            pe.wait_ge(ev["v"], QT)
            pe.wait_ge(at["ag"], 1)
            score(0, 0)
            pe.wait_ge(at["qk"], 10)
            head(1, 1)
            with pe.Fori(0, 3) as i:
                for g in range(2):
                    head(2 * i + (2 + g), g)
            pe.wait_ge(at["ag"], HEADS)
            pe.wait_ge(at["exp"], QT * HEADS)

            def last_head(k):
                if k == 0:
                    turn(7, 1)
                else:
                    weigh(7, 1)
                    pe.wait_ge(at["t"], HEADS)

            residual("eo1", KD, z_hi, z_lo, at["z"], free=(3, 4, 5, 6, 7), between=last_head)

            f = first["rnn"]

            def gates(b, s):
                pe.wait_ge(rg[f"w{s}"], 8 * b + (16 - 8 * s))
                pe.wait_ge(rg["xc"], b + 1)
                if type(b) is not int or b >= 1:
                    pe.wait_ge(rg["ri"], 4 * b)
                for k in range(4):
                    last = mm(ps[:, 4 + k, :], rg_w[:, s, k, :], xc[:, s, :], start=True, stop=True)
                last.then_inc(rg["gmm"], 1)

            dense_first(5, f)
            dense_third(f + 2, lambda: sum_squares(5))
            dense(f + 3, 1, 3, h_hi, h_lo)
            pe.wait_ge(nrm["root"], 6)
            gates(0, 0)
            pe.wait_ge(rg["x"], 1)
            dense(f + 4, 0, 0, h_hi, h_lo)
            gates(1, 1)
            pe.wait_ge(rg["x"], 2)
            dense(f + 5, 1, 1, h_hi, h_lo)
            for s in range(2):
                pe.wait_ge(rg["g"], s + 1)
                dense(f + 6 + s, s, 2 + s, h_hi, h_lo)
            with pe.Fori(0, NRB // 2 - 2) as i:
                for s in range(2):
                    gates(2 * i + (2 + s), s)
                    pe.wait_ge(rg["x"], 2 * i + (3 + s))
                    dense(4 * i + (f + 8 + s), s, s, h_hi, h_lo)
                for s in range(2):
                    pe.wait_ge(rg["g"], 2 * i + (3 + s))
                    dense(4 * i + (f + 10 + s), s, 2 + s, h_hi, h_lo)
            gates(NRB - 2, 0)
            pe.wait_ge(rg["x"], NRB)

            def last_gates(k):
                if k == 0:
                    gates(NRB - 1, 1)
                else:
                    pe.wait_ge(rg["ri"], 4 * NRB)
                    pe.wait_ge(rg["g"], NRB)

            residual("ro", NRB, y_hi, y_lo, rg["z"], free=(0, 1), between=last_gates)
            sum_squares(6)

        @block.scalar
        def _(act):
            A = nc.scalar.activation
            own = Chain(act, a_chain)

            def norm(k, where, g=None):
                def x_stands(m):
                    if k > 0:
                        act.wait_ge(nrm["x"], x_at(k) + m + 1)
                    elif m % 2 == 0:
                        act.wait_ge(s_x[m // 2], 16)
                        act.wait_ge(s_par, 16)
                if where == "h":
                    for m in range(KD):
                        x_stands(m)
                        A(h_hi[:, m, :], x[:, m, :], ACT.Copy, scale=col(par, g, m)).then_inc(nrm["hi"], 1)
                for m in range(KD):
                    if where != "h":
                        x_stands(m)
                    if m >= 2:
                        act.wait_ge(nrm["acc"], (KD - 1) * k + max(1, m - 2))
                    A(sq[:, m % 2, :], x[:, m, :], ACT.Square).then_inc(nrm["sq"], 1)
                act.wait_ge(nrm["ss"], k + 1)
                A(root[:, 0, :], ps[:, 7, :], ACT.Sqrt, bias=col(par, "eps_rms"), scale=1.0 / D).then_inc(nrm["root"], 1)

            def two_norms():
                for m in range(KD):
                    act.wait_ge(nrm["x"], x_at(3) + m + 1)
                    A(h_hi[:, m, :], x[:, m, :], ACT.Copy, scale=gain2[:, m:m + 1]).then_inc(nrm["hi"], 1)
                for k in (3, 4):
                    for m in range(KD):
                        if k == 4 or m >= 2:
                            act.wait_ge(nrm["acc"], (KD - 1) * k + (max(1, m - 2) if m >= 2 else m - 1))
                        A(sq[:, m % 2, :], x[:, m, :], ACT.Square, scale=1.0 if k == 3 else col(par, "final_norm", m)
                          ).then_inc(nrm["sq"], 1)
                act.wait_ge(nrm["ss"], 4)
                A(tmp[:, 0, :], ps[:, 7, :], ACT.Sqrt, bias=col(par, "eps_rms"), scale=1.0 / D).then_inc(nrm["root"], 1)
                act.wait_ge(nrm["ss"], 5)
                A(root[:, 0, :], ps[:, 6, :], ACT.Sqrt, bias=eps2[:], scale=1.0 / D).then_inc(nrm["root"], 1)

            def ffn_up(k, name):
                q = ffn[k]
                with act.Fori(0, KF // 2) as i:
                    for s in range(2):
                        act.wait_ge(q["g"], 2 * i + (s + 1))
                        A(gate_s[:, s, :], gate_s[:, s, :], ACT.Silu).then_inc(q["silu"], 1)
                        act.wait_ge(q["t"], 2 * i + (s + 1))
                        act.sem_inc(s_act_pass, 1)
                        nc.scalar.copy(tile(hid_hi, 2 * i + s), hid_t[:, s, :]).then_inc(q["hi"], 1)

            act.wait_ge(rg["lexp"], 1)
            A(lam[:, 1, :], lam[:, 0, :], ACT.Exp, scale=-1.0).then_inc(rg["lexp"], 1)
            norm(0, "h", "ffn1_norm")
            ffn_up(0, "up0")
            act.wait_ge(w_done, first["mix"])
            act.dma_start(lora_s, lora).then_inc(mx_s["small_loaded"], 16)
            act.dma_start(gup_s, gup).then_inc(mx_s["small_loaded"], 16)
            norm(1, "h", "mix_norm")

            act.wait_ge(mx_s["mix"], 2)
            A(sq[0:64, 0, :], mix[0:64, 0, :], ACT.Tanh).then_inc(mx_s["lora_in"], 1)
            nc.scalar.copy(tmp[64:128, 0, :], mix[64:128, 0, :]).then_inc(mx_s["lora_in"], 1)
            A(sq[:, 1, :], mix[:, 1, :], ACT.Sigmoid).then_inc(mx_s["lora_in"], 1)
            for n in range(4 * NJ):
                kind, j = n // NJ, n % NJ
                act.wait_ge(mx_s["lora_mm"], n + 1)
                bank = ps[:, 2 + n % 6, :]
                if kind == 0:
                    A(wd[:, j, :], bank, ACT.Sigmoid, bias=col(par, "w0", j)).then_inc(mx_s["lora_ev"], 1)
                elif kind == 1:
                    A(bb[:, j, :], bank, ACT.Sigmoid, bias=col(par, "a0", j)).then_inc(mx_s["lora_ev"], 1)
                elif kind == 2:
                    A(kroot[:, j, :], bank, ACT.Sqrt).then_inc(mx_s["lora_ev"], 1)
                else:
                    nc.scalar.copy(gg[:, j, :], bank).then_inc(mx_s["lora_ev"], 1)
            act.wait_ge(mx_s["lora_ev"], NJ)
            for j in range(NJ):
                A(wd[:, j, :], wd[:, j, :], ACT.Exp, scale=-INV_SQRT_E).then_inc(mx_s["kk_w"], 1)

            def chunk_inputs(c):
                if type(c) is not int or c >= 1:
                    act.wait_ge(rw["umm"], c)
                else:
                    act.wait_ge(mx_s["mix"], N_MIX)
                nc.scalar.copy(root[:, 0, :].rearrange("p (j t) -> p j t", j=NJ),
                               mix[:, V0:V0 + NJ, bass.ds(c * CH, CH)]).then_inc(rw["vc"], 1)
                if type(c) is int and c == 0:
                    act.wait_ge(mx_s["ya"], NJ)
                for h in range(HEADS):
                    for z in range(2):
                        last = nc.scalar.copy(xx[:, h, z, :], ident)
                last.then_inc(rw["reset"], 1)

            def gate_tile(c, n):
                act.wait_ge(mx_s["gd"], GATES * c + (n + 1))
                A(mix[:, n % 2, :], mix[:, n % 2, :], ACT.Sigmoid).then_inc(mx_s["gsig"], 1)
                act.wait_ge(mx_s["gsig"], GATES * c + (n + 1))
                act.dma_start(gate_store[bass.ds(GATES * c + n, 1)].rearrange("a p t -> p (a t)"), mix[:, n % 2, :]
                              ).then_inc(mx_s[f"spilled_{n % 2}"], 16)

            def chunk(c, follows=True):
                for q in range(3):
                    act.wait_ge(rw["tr"], 3 * c + (q + 1))
                    nc.scalar.copy(tok[:, q, :], ps[:, q, :]).then_inc(rw["tok"], 1)
                for l in range(1, LEVELS):
                    for g in range(2):
                        act.wait_ge(rw["t1mm"], 2 * LEVELS * c + (2 * l + g + 1))
                        nc.scalar.copy(t1[:, 4 * g:4 * g + 4, :].rearrange("p h t -> p (h t)"), ps[:, g, :]).then_inc(rw["t1"], 1)
                    if l == 1:
                        gate_tile(c, 0)
                act.wait_ge(rw["rhsmm"], c + 1)
                rhs = sq[:, 0, :].rearrange("p (j e v) -> p e j v", j=NJ, e=2)
                for e in range(2):
                    last = nc.scalar.copy(rhs[:, e], ps[:, 2 + e, 0:256].rearrange("p (j v) -> p j v", j=NJ))
                last.then_inc(rw["rhs"], 1)
                act.wait_ge(rw["umm"], c + 1)
                nc.scalar.copy(sq[:, 1, :], ps[:, 0, :]).then_inc(rw["u"], 1)
                gate_tile(c, 1)
                if follows:
                    chunk_inputs(c + 1)
                gate_tile(c, 2)
                if not follows:
                    for j in range(NJ):
                        act.wait_ge(po["yc"], j + 1)
                        A(kk[:, j, :], wd[:, j, :], ACT.Square).then_inc(po["sq"], 1)
                    act.wait_ge(rw["s"], NCH + 1)
                    for s in range(2):
                        act.wait_ge(mx_s[f"spilled_{s}"], 32)
                        act.dma_start(sga[:, s], gate_store[2 * s:2 * s + 2].rearrange("a p t -> p a t")
                                      ).then_inc(mx_s[f"refilled_{s}"], 16)
                    for j in range(NJ):
                        nc.scalar.copy(ya_hi[:, j, :], ya[:, j, :]).then_inc(po["yahi"], 1)
                    act.wait_ge(po["var"], 1)
                    A(bb[:, 0, :], ps[:, 0, :], ACT.Sqrt, bias=col(par, "eps_gn"), scale=1.0 / HS).then_inc(po["root"], 1)
                gate_tile(c, 3)

            chunk_inputs(0)
            with act.Fori(0, NCH - 1) as c:
                chunk(c)
            chunk(NCH - 1, follows=False)

            for s in range(2):
                act.wait_ge(mx_s[f"spilled_{s}"], 16 * N_GATES // 2)
            for j in range(NJ):
                act.wait_ge(po["t"], j + 1)
                nc.scalar.copy(yb_hi[:, j, :], wd[:, j, :]).then_inc(po["hi"], 1)

            def merge(m, s, more):
                act.wait_ge(po["mg_t"], m + 1)
                act.sem_inc(s_act_pass, 1)
                nc.scalar.copy(tile(mg_hi, m), mt[:, s, 1, :]).then_inc(po["mg_hi"], 1)
                if more:
                    act.dma_start(sga[:, s], gate_store[bass.ds(2 * m + 4, 2)].rearrange("a p t -> p a t")
                                  ).then_inc(mx_s[f"refilled_{s}"], 16)

            with act.Fori(0, KD // 2 - 1) as i:
                for s in range(2):
                    merge(2 * i + s, s, True)
            for s in range(2):
                merge(KD - 2 + s, s, False)

            norm(2, "h", "ffn2_norm")
            ffn_up(1, "up1")
            act.wait_ge(w_done, first["pair0"])
            act.dma_start(dftc[:], dft_c).then_inc(ev["loaded"], 16)
            act.dma_start(dfts[:], dft_s).then_inc(ev["loaded"], 16)
            act.dma_start(fws[:], fw).then_inc(ev["loaded"], 16)
            act.dma_start(fw128[0:4], fw_mid).then_inc(ev["loaded"], 16)
            two_norms()

            def pairs(gs, rs):
                with act.Fori(0, 4) as i:
                    for s in range(2):
                        act.wait_ge(gs, 2 * i + (s + 1))
                        act.sem_inc(s_act_pass, 1)
                        A(tile(right, 2 * i + s), tile(right, 2 * i + s), ACT.Silu).then_inc(rs, 1)

            pairs(ev["g0"], ev["r0"])
            for g in range(4):
                for t in range(QT):
                    act.wait_ge(ev["chmm"], QT * g + t + 1)
                    if g >= 1:
                        act.wait_ge(ev["sqmm"], g)
                    nc.scalar.copy(mid[:, t, g:g + 1], ps[:, t, 256:257]).then_inc(ev["mid"], 1)
                    nc.scalar.copy(chan[:, t, :], ps[:, t, 0:256]).then_inc(ev["chan"], 1)
            for g in range(4):
                for e in range(2):
                    act.wait_ge(ev["t"], 2 * g + e + 1)
                    nc.scalar.copy(z_hi[:, 2 * g + e, :], tmp[:, e, :]).then_inc(ev["hi"], 1)
            act.wait_ge(w_done, first["qk"])
            act.dma_start(rope_s[:], rope).then_inc(at["rope"], 16)
            def square_head(u):
                if type(u) is not int or u >= 1:
                    act.wait_ge(at["ssmm"], u)
                act.wait_ge(at["raw"], u + 1)
                act.sem_inc(s_act_pass, 1)
                A(sq[:, 0, :], tile(left, u), ACT.Square).then_inc(at["sq"], 1)

            def root_head(u):
                act.wait_ge(at["ssmm"], u + 1)
                if type(u) is not int or u >= 1:
                    act.wait_ge(at["qn"], u)
                A(root[:, 0, :], ps[:, 2, :], ACT.Sqrt, bias=col(par, "eps_rms"), scale=1.0 / P).then_inc(at["root"], 1)

            square_head(0)
            with act.Fori(0, 9) as i:
                root_head(i)
                square_head(i + 1)
            root_head(9)

            def copy_turned(v):
                if type(v) is not int or v >= 1:
                    act.wait_ge(at["pv"], v)
                for t in range(QT):
                    act.wait_ge(at["tr"], QT * v + (t + 1))
                    nc.scalar.copy(probT[:, :, t * P:(t + 1) * P], ps[:, t % 2, :].rearrange("p (k t) -> p k t", k=QT)
                                   ).then_inc(at["pt"], 1)

            def z_part(v):
                act.wait_ge(at["t"], v + 1)
                act.sem_inc(s_act_pass, 1)
                nc.scalar.copy(tile(z_hi, v), tmp[:, 1, :]).then_inc(at["hi"], 1)

            def exps(v, g):
                if type(v) is not int or v >= 2:
                    act.wait_ge(at["tr"], QT * v - QT)
                for t in range(QT):
                    act.wait_ge(at["max"], QT * v + (t + 1))
                    A(prob[:, g, t, :], ps[:, 4 + t, :], ACT.Exp, bias=mx[:, 16 * g + t:16 * g + t + 1], scale=P ** -0.5,
                      accum_out=mx[:, 16 * g + 4 + t:16 * g + 5 + t]).then_inc(at["exp"], 1)

            def silu(v, g):
                act.wait_ge(at["ag"], v + 1)
                A(right[:, g, :], right[:, g, :], ACT.Silu).then_inc(at["silu"], 1)

            def head(v, g):
                exps(v, g)
                copy_turned(v - 1)
                z_part(v - 1)
                silu(v, g)

            exps(0, 0)
            silu(0, 0)
            head(1, 1)
            with act.Fori(0, 3) as i:
                for g in range(2):
                    head(2 * i + (2 + g), g)
            copy_turned(7)
            z_part(7)

            norm(5, "h", "odd_norm_2")

            f = first["rnn"]
            for s in range(2):
                act.dma_start(rg_w[:, s], rgates[s]).then_inc(rg[f"w{s}"], 16)
            def block_gates(b, s, acquire):
                act.wait_ge(rg["gmm"], b + 1)
                if acquire:
                    act.wait_ge(rg["y"], b - 1)
                for k in range(4):
                    name, d = ("gate_a_b_2", "gate_x_b_2")[k % 2], k // 2
                    A(ri[:, s, k, :], ps[:, 4 + k, :], ACT.Sigmoid, bias=col(par, name, b + 16 * d)).then_inc(rg["ri"], 1)
                act.dma_start(rg_w[:, s], rgates[bass.ds(b + 2, 1)].rearrange("a p k q -> p (a k) q")
                              ).then_inc(rg[f"w{s}"], 16)

            def pair_maps(b):
                for s in range(2):
                    act.wait_ge(rg["nla"], 2 * b + 2 * (s + 1))
                    for d in range(2):
                        A(aa[:, s, d, :], ri[:, s, 2 * d, :], ACT.Exp, scale=-1.0).then_inc(rg["a"], 1)
                    for d in range(2):
                        A(th[:, s, d, :], ri[:, s, 2 * d, :], ACT.Tanh).then_inc(rg["th"], 1)
                act.wait_ge(rg["th"], 2 * b + 4)
                for s in range(2):
                    for d in range(2):
                        A(ri[:, s, 2 * d, :], aa[:, s, d, :], ACT.Square).then_inc(rg["a2"], 1)
                for s in range(2):
                    for d in range(2):
                        act.wait_ge(rg["w"], 2 * b + (2 * s + d + 1))
                        A(th[:, s, d, :], th[:, s, d, :], ACT.Sqrt).then_inc(rg["root"], 1)
                for s in range(2):
                    act.wait_ge(rg["g"], b + (s + 1))
                    A(sgate[:, s, :], sgate[:, s, :], ACT.Silu).then_inc(rg["sg"], 1)

            def pair_values(b):
                for s in range(2):
                    act.wait_ge(rg["t"], b + (s + 1))
                    act.sem_inc(s_act_pass, 1)
                    nc.scalar.copy(tile(y_hi, b + s), th[:, s, 1, :]).then_inc(rg["hi"], 1)

            for s in range(2):
                block_gates(s, s, False)
            pair_maps(0)
            with act.Fori(0, NRB // 2 - 1) as i:
                block_gates(2 * i + 2, 0, True)
                pair_values(2 * i)
                block_gates(2 * i + 3, 1, True)
                pair_maps(2 * i + 2)
            pair_values(NRB - 2)
            norm(6, "out")
            for s in range(2):
                act.wait_ge(rg[f"w{s}"], 16 * (NRB // 2 + 1))

        @block.vector
        def _(dve):
            V = nc.vector
            own = Chain(dve, v_chain)

            def norm(k, where, g):
                if where == "h":
                    for m in range(KD):
                        dve.wait_ge(nrm["hi"], h_at(k) + m + 1)
                        rest_of_h(m, g)
                sum_up(k)
                if where == "out":
                    for m in range(KD):
                        V.scalar_tensor_tensor(out=x[:, m, :], in0=x[:, m, :], scalar=col(par, g, m),
                                               in1=rinv[:, 0, :], op0=ALU.mult, op1=ALU.mult).then_inc(s_out_t, 1)

            def rest_of_h(m, g):
                V.scalar_tensor_tensor(out=h_lo[:, m, :], in0=x[:, m, :],
                                       scalar=gain2[:, m:m + 1] if g == "gain2" else col(par, g, m),
                                       in1=h_hi[:, m, :].bitcast(F32), op0=ALU.mult, op1=ALU.subtract
                                       ).then_inc(nrm["h"], 1)

            def sum_up(k):
                sum_tiles(k)
                dve.wait_ge(nrm["root"], k + 1)
                own.link(V.reciprocal(rinv[:, 0, :], root[:, 0, :]))

            def sum_tiles(k):
                for m in range(1, KD):
                    dve.wait_ge(nrm["sq"], KD * k + m + 1)
                    if m >= 2:
                        dve.wait_ge(nrm["acc"], (KD - 1) * k + m - 1)
                    V.tensor_tensor(root[:, 0, :], sq[:, 0, :] if m == 1 else root[:, 0, :], sq[:, m % 2, :], ALU.add
                                    ).then_inc(nrm["acc"], 1)

            def sum_both():
                sum_tiles(3)
                dve.wait_ge(nrm["acc"], (KD - 1) * 4)
                dve.wait_ge(nrm["sq"], KD * 4 + 1)
                own.link(V.scalar_tensor_tensor(out=tmp[:, 1, :], in0=root[:, 0, :], scalar=EPS_RMS, in1=sq[:, 0, :],
                                                op0=ALU.mult, op1=ALU.add))
                for m in range(1, KD):
                    dve.wait_ge(nrm["sq"], KD * 4 + m + 1)
                    dve.wait_ge(nrm["acc"], (KD - 1) * 4 + m - 1)
                    V.tensor_tensor(tmp[:, 1, :], tmp[:, 1, :], sq[:, m % 2, :], ALU.add).then_inc(nrm["acc"], 1)
                dve.wait_ge(nrm["root"], 5)
                own.link(V.reciprocal(rinv[:, 0, :], root[:, 0, :]))

            def finish_norm_3():
                dve.wait_ge(nrm["root"], 4)
                own.link(V.reciprocal(tmp[:, 0, :], tmp[:, 0, :]))
                for m in range(KD):
                    V.scalar_tensor_tensor(out=x[:, m, :], in0=x[:, m, :], scalar=col(par, "final_norm", m),
                                           in1=tmp[:, 0, :], op0=ALU.mult, op1=ALU.mult).then_inc(nrm["x"], 1)
                dve.wait_ge(nrm["x"], x_at(4) + KD)

            def divided(out, bank):
                return V.tensor_tensor(out, ps[:, bank, :], rinv[:, 0, :], ALU.mult)

            def ffn_up(k, name):
                q, f = ffn[k], first[name]
                with dve.Fori(0, KF // 2) as i:
                    own.enter(i, 0)
                    for s in range(2):
                        m = 2 * i + s
                        dve.wait_ge(w_done, 4 * i + (f + 2 * s + 1))
                        divided(gate_s[:, s, :], 2 * s).then_inc(q["g"], 1)
                        dve.wait_ge(w_done, 4 * i + (f + 2 * s + 2))
                        divided(hid_t[:, s, :], 2 * s + 1).then_inc(q["u"], 1)
                        dve.wait_ge(q["u"], m + 1)
                        dve.wait_ge(q["silu"], m + 1)
                        V.tensor_tensor(hid_t[:, s, :], gate_s[:, s, :], hid_t[:, s, :], ALU.mult).then_inc(q["t"], 1)
                        dve.wait_ge(q["hi"], m + 1)
                        V.tensor_tensor(tile(hid_lo, m), hid_t[:, s, :], tile(hid_hi, m).bitcast(F32), ALU.subtract
                                        ).then_inc(q["hid"], 1)
                        dve.wait_ge(q["hid"], m + 1)
                    own.leave(0)

            BANKS = {1: 0, 2: 1, 3: 2, 5: 3, 6: 4, 7: 5}

            def add_to_x(k, until, scale, g=None):
                for m in range(KD):
                    if m < KD - 1:
                        dve.wait_ge(s_bank, (KD - 1) * BANKS[k] + m + 1)
                    else:
                        dve.wait_ge(w_done, until)
                    V.scalar_tensor_tensor(out=x[:, m, :], in0=ps[:, m, :], scalar=scale, in1=x[:, m, :],
                                           op0=ALU.mult, op1=ALU.add).then_inc(nrm["x"], 1)
                if g is not None:
                    for m in range(KD):
                        n = {3: 4, 6: 5}.get(k, k)
                        dve.wait_ge(nrm["hi"], h_at(n) + m + 1)
                        rest_of_h(m, g)

            dve.wait_ge(s_par, 16)
            lm = par[:, COLS["rglru_lambda_2"]:COLS["rglru_lambda_2"] + 32]
            own.link(V.tensor_scalar(lam[:, 0, :], lm, -1.0, None, ALU.mult))
            own.link(V.tensor_tensor(lam[:, 0, :], lam[:, 0, :], lm, ALU.max))
            dve.sem_inc(rg["lexp"], 1)
            dve.wait_ge(rg["lexp"], 2)
            own.link(V.tensor_scalar(lam[:, 2, :], lam[:, 1, :], 2.0, None, ALU.add))
            own.link(V.reciprocal(lam[:, 2, :], lam[:, 2, :]))
            own.link(V.tensor_tensor(lam[:, 2, :], lam[:, 2, :], lam[:, 1, :], ALU.mult))
            own.link(V.tensor_tensor(lam[:, 3, :], lam[:, 2, :], lam[:, 2, :], ALU.mult))
            own.link(V.tensor_scalar(lam[:, 4, :], lam[:, 3, :], 1.0 / 17, 1.0 / 15, ALU.mult, ALU.add))
            for k in (13, 11, 9, 7, 5, 3, 1):
                own.link(V.tensor_tensor(lam[:, 4, :], lam[:, 4, :], lam[:, 3, :], ALU.mult))
                own.link(V.tensor_scalar(lam[:, 4, :], lam[:, 4, :], 1.0 / k, None, ALU.add))
            own.link(V.tensor_tensor(lam[:, 4, :], lam[:, 4, :], lam[:, 2, :], ALU.mult))
            own.link(V.tensor_scalar(lam[:, 5, :], lm, -1.0, 0.0, ALU.mult, ALU.max))
            own.link(V.scalar_tensor_tensor(out=lam[:, 5, :], in0=lam[:, 4, :], scalar=2.0, in1=lam[:, 5, :],
                                            op0=ALU.mult, op1=ALU.add))
            own.link(V.tensor_scalar(lam[:, 5, :], lam[:, 5, :], 8.0, None, ALU.mult))
            for q in range(4):
                dve.wait_ge(s_x[q], 16)
            norm(0, "h", "ffn1_norm")
            V.tensor_tensor(gain2[:], col(par, "final_norm", 0, KD), col(par, "even_norm_2", 0, KD), ALU.mult)
            own.link(V.tensor_tensor(eps2[:], col(par, "eps_rms"), col(par, "eps_rms"), ALU.mult))
            dve.wait_ge(s_masks, 16)
            V.tensor_copy(lev8[:].rearrange("p a b c -> p (a b c)"), m32[:, 0:LEVELS * 2 * P])
            own.link(V.tensor_copy(tri8[:].rearrange("p a b -> p (a b)"), m32[:, LEVELS * 2 * P:]))
            ffn_up(0, "up0")
            add_to_x(1, first["mix"], 0.5, "mix_norm")
            sum_up(1)

            own.link(V.memset(padc[:, :, 0:2], 0.0))
            own.link(V.memset(padm[:, :, 0:1], 0.0))
            f = first["mix"]
            def shifted(m, s, bank):
                dve.wait_ge(w_done, m + (f + 1))
                divided(padm[:, s, 1:T + 1], bank).then_inc(mx_s["raw"], 1)
                dve.wait_ge(mx_s["raw"], m + 1)
                own.link(V.tensor_tensor(dif[:, s, :], padm[:, s, 0:T], padm[:, s, 1:T + 1], ALU.subtract))
                own.link(V.scalar_tensor_tensor(out=tile(mix, m), in0=dif[:, s, :],
                                                scalar=col(par, "mu_b", m), in1=padm[:, s, 1:T + 1],
                                                op0=ALU.mult, op1=ALU.add))
                dve.sem_inc(mx_s["mix"], 1)

            def kk_squares(j):
                own.link(V.tensor_scalar(kk[:, j, :], mix[:, K0 + j, :], col(par, "k_k", j), None, ALU.mult))
                V.tensor_tensor(kroot[:, j, :], kk[:, j, :], kk[:, j, :], ALU.mult).then_inc(mx_s["kk_sq"], 1)

            for m in range(6):
                shifted(m, m % 2, m if m < 4 else m % 2)
                if m in (3, 5):
                    for j in range(m - 3, m - 1):
                        kk_squares(j)
            with dve.Fori(0, N_MIX // 2 - 3) as i:
                own.enter(i, 4)
                for s in range(2):
                    shifted(2 * i + (6 + s), s, s)
            own.leave(N_MIX // 2 - 3)
            for j in range(NJ):
                s = j % 2
                dve.wait_ge(mx_s["lora_ev"], NJ + j + 1)
                own.link(V.tensor_scalar(csb[:, s, :], bb[:, j, :], 1.0, col(par, "k_a", j), ALU.subtract, ALU.mult))
                own.link(V.scalar_tensor_tensor(out=mix[:, K0 + j, :], in0=csb[:, s, :], scalar=1.0,
                                                in1=mix[:, K0 + j, :], op0=ALU.add, op1=ALU.mult))
            for j in range(NJ):
                s = j % 2
                dve.wait_ge(mx_s["lora_ev"], 2 * NJ + j + 1)
                own.link(V.tensor_scalar(csb[:, s, :], kroot[:, j, :], 1e-12, None, ALU.max))
                own.link(V.reciprocal(csb[:, s, :], csb[:, s, :]))
                own.link(V.tensor_tensor(kk[:, j, :], kk[:, j, :], csb[:, s, :], ALU.mult))
                own.link(V.scalar_tensor_tensor(out=bb[:, j, :], in0=kk[:, j, :], scalar=-1.0, in1=bb[:, j, :],
                                                op0=ALU.mult, op1=ALU.mult))

            dve.wait_ge(mx_s["kk_w"], NJ)
            dve.wait_ge(mx_s["lora_mm"], 4 * NJ)
            own.link(V.memset(st[:], 0.0))
            own.link(V.memset(pe_[:], 1.0))
            dve.sem_inc(rw["s"], 1)

            def decays(c):
                tt = bass.ds(c * CH, CH)
                for j in range(NJ):
                    own.link(V.tensor_tensor_scan(pe_[:, j, 1:CH + 1], wd[:, j, tt], wd[:, j, tt], 1.0, ALU.mult, ALU.bypass))
                own.link(V.reciprocal(rmid[:], pe_[:, :, 64:65]))
                own.link(V.tensor_tensor(pn[:], pe_[:], rmid[:].broadcast_to([P, NJ, CH + 1]), ALU.mult))
                pinv = tmp[:, 0, :].rearrange("p (j t) -> p j t", j=NJ)
                own.link(V.reciprocal(pinv, pn[:, :, 1:CH + 1]))
                own.link(V.tensor_tensor(bc[:], bb[:, :, tt], pinv, ALU.mult))
                own.link(V.tensor_tensor(kc_[:], mix[:, K0:K0 + NJ, tt], pinv, ALU.mult))

            def operands(c):
                tt = bass.ds(c * CH, CH)
                own.link(V.tensor_tensor(st0[:], st[:], pe_[:, :, 64:65].broadcast_to([P, NJ, HS]), ALU.mult))
                own.link(V.tensor_tensor(ar[:, :, 0, :], kk[:, :, tt], pn[:, :, 0:CH], ALU.mult))
                V.tensor_tensor(ar[:, :, 1, :], mix[:, R0:R0 + NJ, tt], pn[:, :, 1:CH + 1], ALU.mult).then_inc(rw["ops"], 1)

            def gate_tile(c, n, bank):
                if type(c) is not int or c >= 1 or n >= 2:
                    dve.wait_ge(mx_s[f"spilled_{n % 2}"], 32 * c + 16 * (n // 2))
                dve.wait_ge(w_done, GATES * c + (first["gates"] + n + 1))
                divided(mix[:, n % 2, :], bank).then_inc(mx_s["gd"], 1)

            def chunk(c, follows=True):
                tt = bass.ds(c * CH, CH)
                for h in range(HEADS):
                    dve.wait_ge(rw["mat"], HEADS * c + (h + 1))
                    dve.sem_inc(s_pass, 1)
                    V.copy_predicated(scores[:, h].rearrange("p a t -> p (a t)"), tri8[:].rearrange("p a t -> p (a t)"),
                                      ps[:, 4 + h % 4, :]).then_inc(rw["sc"], 1)
                gate_tile(c, 0, 3)
                dve.wait_ge(rw["sc"], HEADS * c + HEADS)
                dve.wait_ge(rw["reset"], c + 1)
                dve.sem_inc(s_pass, 1)
                for g in range(2):
                    hh_ = slice(4 * g, 4 * g + 4)
                    V.copy_predicated(xx[:, hh_, 1, :], lev8[:, 0, 1:2, :].broadcast_to([P, 4, P]), scores[:, hh_, 0, :])
                    dve.wait_ge(rw["t1mm"], 2 * LEVELS * c + (g + 1))
                    dve.sem_inc(s_pass, 1)
                    V.copy_predicated(xx[:, hh_, 0, :], lev8[:, 0, 0:1, :].broadcast_to([P, 4, P]),
                                      ps[:, g, :].rearrange("p (h t) -> p h t", h=4)).then_inc(rw["xx"], 2)
                for l in range(1, LEVELS):
                    for hp in range(4):
                        dve.wait_ge(rw["xmm"], 4 * (LEVELS - 1) * c + (4 * l + hp - 3))
                        dve.sem_inc(s_pass, 1)
                        z = slice(0 if l < LEVELS - 1 else 1, 2)
                        n = z.stop - z.start
                        m = lev8[:, l, z].rearrange("p a t -> p (a t)").rearrange("p (b t) -> p b t", b=1)
                        V.copy_predicated(xx[:, 2 * hp:2 * hp + 2, z].rearrange("p h a t -> p h (a t)"),
                                          m.broadcast_to([P, 2, n * P]),
                                          ps[:, 4 + hp, :].rearrange("p (h t) -> p h t", h=2)[:, :, z.start * P:256]
                                          ).then_inc(rw["xx"], 1)
                gate_tile(c, 1, 1)
                own.link(V.tensor_scalar(pend[:], pn[:, :, CH:CH + 1], 1.0, None, ALU.mult))
                if follows:
                    decays(c + 1)
                dve.wait_ge(rw["ysmm"], c + 1)
                for e in range(2):
                    pp = slice(64 * e, 64 * e + 64)
                    V.tensor_scalar(wd[pp, :, tt], ps[pp, 4 + e, :].rearrange("p (j t) -> p j t", j=NJ), 1.0, None, ALU.mult
                                    ).then_inc(rw["y"], 1)
                own.link(V.tensor_tensor(st0[:], st0[:], ps[:, 6, 0:256].rearrange("p (j v) -> p j v", j=NJ), ALU.add))
                V.tensor_tensor(st[:], st0[:], pend[:].broadcast_to([P, NJ, HS]), ALU.mult).then_inc(rw["s"], 1)
                if follows:
                    dve.wait_ge(rw["s"], c + 2)
                    operands(c + 1)
                else:
                    for j in range(NJ):
                        V.scalar_tensor_tensor(out=mix[:, K0 + j, :], in0=mix[:, R0 + j, :], scalar=col(par, "r_k", j),
                                               in1=mix[:, K0 + j, :], op0=ALU.mult, op1=ALU.mult).then_inc(po["rk"], 1)
                gate_tile(c, 2, 7)
                if not follows:
                    for j in range(NJ):
                        dve.wait_ge(po["mean"], j + 1)
                        V.scalar_tensor_tensor(out=wd[:, j, :], in0=ps[:, j, :], scalar=-1.0 / HS, in1=wd[:, j, :],
                                               op0=ALU.mult, op1=ALU.add).then_inc(po["yc"], 1)
                    for j in range(NJ):
                        dve.wait_ge(po["sq"], j + 1)
                        own.link(V.scalar_tensor_tensor(out=wd[:, j, :], in0=wd[:, j, :], scalar=col(par, "ln_x_w", j),
                                                        in1=gg[:, j, :], op0=ALU.mult, op1=ALU.mult))
                    for j in range(NJ):
                        dve.wait_ge(po["bonus"], j + 1)
                        V.tensor_tensor(mix[:, V0 + j, :], ps[:, BONUS[j], :], mix[:, V0 + j, :], ALU.mult
                                        ).then_inc(po["rkv"], 1)
                    dve.wait_ge(po["root"], 1)
                    V.reciprocal(bb[:, 0, :], bb[:, 0, :]).then_inc(po["rcp"], 1)
                    for j in range(NJ):
                        dve.wait_ge(po["yahi"], j + 1)
                        V.tensor_tensor(ya_lo[:, j, :], ya[:, j, :], ya_hi[:, j, :].bitcast(F32), ALU.subtract
                                        ).then_inc(po["ya"], 1)
                gate_tile(c, 3, 3 if follows else 7)

            decays(0)
            operands(0)
            f = first["conv"]
            for j in range(NJ):
                s = j % 2
                dve.wait_ge(w_done, f + 3 * j + 1)
                own.link(divided(csb[:, s, :], 3 * s))
                dve.wait_ge(w_done, f + 3 * j + 2)
                own.link(divided(dif[:, s, :], 3 * s + 1))
                own.link(V.tensor_tensor(padc[:, s, 2:T + 2], csb[:, s, :], dif[:, s, :], ALU.mult))
                own.link(V.tensor_scalar(dif[:, s, :], padc[:, s, 0:T], col(par, "conv_w", j), None, ALU.mult))
                for tap in (1, 2):
                    own.link(V.scalar_tensor_tensor(out=dif[:, s, :], in0=padc[:, s, tap:T + tap],
                                                    scalar=col(par, "conv_w", 4 * tap + j), in1=dif[:, s, :],
                                                    op0=ALU.mult, op1=ALU.add))
                dve.wait_ge(w_done, f + 3 * j + 3)
                own.link(divided(csb[:, s, :], 3 * s + 2))
                own.link(V.tensor_tensor(ya[:, j, :], dif[:, s, :], csb[:, s, :], ALU.mult))
                dve.sem_inc(mx_s["ya"], 1)
            own.link(V.memset(scores[:], 0.0))
            with dve.Fori(0, NCH - 1) as c:
                own.enter(c, 1 + 4 + 5 + 1 + 2)
                chunk(c)
            own.leave(NCH - 1)
            chunk(NCH - 1, follows=False)

            dve.wait_ge(po["rkv"], NJ)
            for j in range(NJ):
                own.link(V.scalar_tensor_tensor(out=mix[:, V0 + j, :], in0=mix[:, V0 + j, :], scalar=col(par, "ln_x_b", j),
                                                in1=gg[:, j, :], op0=ALU.add, op1=ALU.mult))
            for j in range(NJ + 1):
                if j < NJ:
                    dve.wait_ge(po["bc"], j + 1)
                    own.link(V.tensor_tensor(wd[:, j, :], wd[:, j, :], ps[:, ROOTS[j], :], ALU.mult))
                    V.tensor_tensor(wd[:, j, :], wd[:, j, :], mix[:, V0 + j, :], ALU.add).then_inc(po["t"], 1)
                if j >= 1:
                    dve.wait_ge(po["hi"], j)
                    V.tensor_tensor(yb_lo[:, j - 1, :], wd[:, j - 1, :], yb_hi[:, j - 1, :].bitcast(F32), ALU.subtract
                                    ).then_inc(po["done"], 1)

            dve.wait_ge(po["done"], NJ)
            f = first["merge"]
            with dve.Fori(0, KD // 2) as i:
                own.enter(i, 4)
                for s in range(2):
                    dve.wait_ge(mx_s[f"refilled_{s}"], 16 * i + 16)
                    dve.wait_ge(w_done, 2 * i + (f + s + 1))
                    own.link(V.tensor_tensor(mt[:, s, 0, :], sga[:, s, 0, :], ps[:, 4 * s, :], ALU.mult))
                    own.link(V.tensor_tensor(mt[:, s, 1, :], sga[:, s, 1, :], ps[:, 4 * s + 1, :], ALU.mult))
                    V.tensor_tensor(mt[:, s, 1, :], mt[:, s, 0, :], mt[:, s, 1, :], ALU.add).then_inc(po["mg_t"], 1)
                    dve.wait_ge(po["mg_hi"], 2 * i + (s + 1))
                    V.tensor_tensor(tile(mg_lo, 2 * i + s), mt[:, s, 1, :], tile(mg_hi, 2 * i + s).bitcast(F32),
                                    ALU.subtract).then_inc(po["mg"], 1)
            own.leave(KD // 2)
            add_to_x(2, first["up1"], 1.0, "ffn2_norm")
            sum_up(2)
            ffn_up(1, "up1")
            add_to_x(3, first["pair0"], 0.5, "gain2")
            sum_both()

            def pairs(name, ls, gs):
                f = first[name]
                with dve.Fori(0, 4) as i:
                    for s in range(2):
                        dve.wait_ge(w_done, 4 * i + (f + 2 * s + 1))
                        divided(tile(left, 2 * i + s), 2 * s).then_inc(ls, 1)
                        dve.wait_ge(w_done, 4 * i + (f + 2 * s + 2))
                        divided(tile(right, 2 * i + s), 2 * s + 1).then_inc(gs, 1)

            pairs("pair0", ev["l0"], ev["g0"])
            finish_norm_3()
            for g in range(4):
                dve.wait_ge(ev["sqmm"], g + 1)
                V.tensor_copy(fmix[:, g, T:T + 1], ps[:, 4, 0:1])
                V.tensor_copy(fmix[:, g, 0:T], ps[:, 4, :]).then_inc(ev["fmix"], 1)
            dve.wait_ge(ev["midmm"], 1)
            V.tensor_copy(ymid[0:4, :], ps[0:4, 5, :]).then_inc(ev["ymid"], 1)
            for g in range(4):
                for e in range(2):
                    m = 2 * g + e
                    dve.wait_ge(ev["fwmm"], m + 1)
                    if m == 0:
                        dve.wait_ge(ev["r0"], KD)
                    if g >= 1:
                        dve.wait_ge(ev["z"], m - 1)
                    V.tensor_tensor(tmp[:, e, :], ps[:, 6 + e, :], right[:, m, :], ALU.mult).then_inc(ev["t"], 1)
                    dve.wait_ge(ev["hi"], m + 1)
                    V.tensor_tensor(z_lo[:, m, :], tmp[:, e, :], z_hi[:, m, :].bitcast(F32), ALU.subtract).then_inc(ev["z"], 1)
            add_to_x(5, first["qk"], 1.0)
            f = first["qk"]

            def raw_head(n, s):
                dve.wait_ge(w_done, n + (f + 1))
                divided(tile(left, n), s).then_inc(at["raw"], 1)

            def scale_head(u, s, gain):
                dve.wait_ge(at["root"], u + 1)
                own.link(V.reciprocal(sq[:, 1, :], root[:, 0, :]))
                V.scalar_tensor_tensor(out=qn[:, s, :], in0=tile(left, u), scalar=gain, in1=sq[:, 1, :],
                                       op0=ALU.mult, op1=ALU.mult).then_inc(at["qn"], 1)

            def rotate(u, s):
                dve.wait_ge(at["rot"], u + 1)
                own.link(V.tensor_tensor(tmp[:, 0, :], ps[:, 3, :], rope_s[:, 1, :], ALU.mult))
                own.link(V.tensor_tensor(qn[:, s, :], qn[:, s, :], rope_s[:, 0, :], ALU.mult))
                V.tensor_tensor(tile(left, u), qn[:, s, :], tmp[:, 0, :], ALU.add).then_inc(at["qk"], 1)
                dve.wait_ge(at["qk"], u + 1)

            k_gain, q_gain = col(par, "k_gain_2"), col(par, "q_gain_2")
            raw_head(0, 0)
            raw_head(1, 1)
            scale_head(0, 0, k_gain)
            dve.wait_ge(at["rope"], 16)
            raw_head(2, 0)
            scale_head(1, 1, k_gain)
            rotate(0, 0)
            raw_head(3, 1)
            scale_head(2, 0, q_gain)
            rotate(1, 1)
            with dve.Fori(0, 3) as i:
                own.enter(i, 2 * 3)
                for s in range(2):
                    raw_head(2 * i + (4 + s), s)
                    scale_head(2 * i + (3 + s), 1 - s, q_gain)
                    rotate(2 * i + (2 + s), s)
            own.leave(3)
            scale_head(9, 1, q_gain)
            rotate(8, 0)
            dve.wait_ge(ev["col"], 1)
            own.link(V.tensor_copy(mx[:, 32:36], ps[:, 4, ::P]))
            dve.wait_ge(w_done, first["v"] + 2)
            for t, bank in enumerate(V_BANKS):
                V.tensor_scalar(vt[:, t, :], ps[:, bank, 0:256], mx[:, 32 + t:33 + t], None, ALU.mult).then_inc(ev["v"], 1)

            def fix_head(v, g):
                if type(v) is not int or v >= 2:
                    dve.wait_ge(at["smm"], QT * v - QT)
                V.tensor_scalar(qr[:, g, :], tile(left, v + 2), 1.0, None, ALU.mult).then_inc(at["qr"], 1)

            def soften(v, g, follows=True):
                o = 16 * g
                for t in range(QT):
                    dve.wait_ge(at["smm"], QT * v + (t + 1))
                    own.link(V.tensor_reduce(mx[:, o + 8 + t:o + 9 + t], ps[:, 4 + t, :], AX_X, ALU.max))
                    V.tensor_scalar(mx[:, o + t:o + t + 1], mx[:, o + 8 + t:o + 9 + t], -(P ** -0.5), None, ALU.mult
                                    ).then_inc(at["max"], 1)
                if follows:
                    fix_head(v + 1, 1 - g)
                for t in range(QT):
                    dve.wait_ge(at["exp"], QT * v + (t + 1))
                    own.link(V.reciprocal(mx[:, o + 12 + t:o + 13 + t], mx[:, o + 4 + t:o + 5 + t]))
                    V.tensor_scalar(prob[:, g, t, :], prob[:, g, t, :], mx[:, o + 12 + t:o + 13 + t], None, ALU.mult
                                    ).then_inc(at["prob"], 1)

            def gate(v, g, bank=3):
                dve.wait_ge(w_done, v + (first["ag"] + 1))
                divided(right[:, g, :], bank).then_inc(at["ag"], 1)

            def z_part(v, g):
                dve.wait_ge(at["pv"], v + 1)
                dve.wait_ge(at["silu"], v + 1)
                V.tensor_tensor(tmp[:, 1, :], ps[:, 2, :], right[:, g, :], ALU.mult).then_inc(at["t"], 1)
                dve.wait_ge(at["hi"], v + 1)
                V.tensor_tensor(tile(z_lo, v), tmp[:, 1, :], tile(z_hi, v).bitcast(F32), ALU.subtract
                                ).then_inc(at["z"], 1)
                dve.wait_ge(at["z"], v + 1)

            def head(v, g, follows=True):
                soften(v, g, follows)
                gate(v, g)
                z_part(v - 1, 1 - g)

            fix_head(0, 0)
            gate(0, 0, 7)
            rotate(9, 1)
            soften(0, 0)
            head(1, 1)
            with dve.Fori(0, 2) as i:
                own.enter(i, 2 * 2 * QT)
                for g in range(2):
                    head(2 * i + (2 + g), g)
            own.leave(2)
            head(6, 0)
            head(7, 1, follows=False)
            z_part(7, 1)
            add_to_x(6, first["rnn"], 1.0, "odd_norm_2")
            sum_up(5)

            own.link(V.memset(xp[:], 0.0))
            f = first["rnn"]

            def values(n, b, s):
                dve.wait_ge(w_done, n + (s + 1))
                divided(xp[:, s, 2:T + 2], s).then_inc(rg["x"], 1)
                dve.wait_ge(rg["x"], b + 1)
                if type(b) is not int or b >= 2:
                    dve.wait_ge(rg["gmm"], b - 1)
                own.link(V.tensor_scalar(xc[:, s, :], xp[:, s, 0:T], col(par, "conv_w_2", b), col(par, "conv_b_2", b),
                                         ALU.mult, ALU.add))
                for tap in range(1, 4):
                    own.link(V.scalar_tensor_tensor(out=xc[:, s, :], in0=xp[:, s, tap:T + tap],
                                                    scalar=col(par, "conv_w_2", b + 16 * tap), in1=xc[:, s, :],
                                                    op0=ALU.mult, op1=ALU.add))
                dve.sem_inc(rg["xc"], 1)

            def gate(n, b, s):
                dve.wait_ge(w_done, n + (s + 3))
                divided(sgate[:, s, :], 2 + s).then_inc(rg["g"], 1)

            def rates(b, s):
                dve.wait_ge(rg["ri"], 4 * b + 4)
                for d in range(2):
                    V.tensor_scalar(ri[:, s, 2 * d, :], ri[:, s, 2 * d, :], lam[:, 5, bass.ds(b + 16 * d, 1)], None, ALU.mult
                                    ).then_inc(rg["nla"], 1)
                    own.link(V.tensor_tensor(ri[:, s, 2 * d + 1, :], ri[:, s, 2 * d + 1, :], xc[:, s, :], ALU.mult))

            def recurrences(b):
                for s in range(2):
                    for d in range(2):
                        dve.wait_ge(rg["a2"], 2 * b + (2 * s + d + 1))
                        own.link(V.scalar_tensor_tensor(out=th[:, s, d, :], in0=ri[:, s, 2 * d, :], scalar=1.0,
                                                        in1=th[:, s, d, :], op0=ALU.add, op1=ALU.mult))
                        dve.sem_inc(rg["w"], 1)
                for s in range(2):
                    for d in range(2):
                        dve.wait_ge(rg["root"], 2 * b + (2 * s + d + 1))
                        own.link(V.tensor_tensor(th[:, s, d, :], th[:, s, d, :], ri[:, s, 2 * d + 1, :], ALU.mult))
                    dve.sem_inc(rg["y"], 1)
                for s in range(2):
                    for d in range(2):
                        o = slice(None, None, -1) if d else slice(None)
                        own.link(V.tensor_tensor_scan(th[:, s, d, o], aa[:, s, d, o], th[:, s, d, o], 0.0,
                                                      ALU.mult, ALU.add))
                    own.link(V.tensor_tensor(th[:, s, 0, :], th[:, s, 0, :], th[:, s, 1, :], ALU.add))
                    dve.wait_ge(rg["sg"], b + (s + 1))
                    own.link(V.tensor_tensor(th[:, s, 1, :], th[:, s, 0, :], sgate[:, s, :], ALU.mult))
                    dve.sem_inc(rg["t"], 1)

            def rests(b):
                for s in range(2):
                    dve.wait_ge(rg["hi"], b + (s + 1))
                    V.tensor_tensor(tile(y_lo, b + s), th[:, s, 1, :], tile(y_hi, b + s).bitcast(F32), ALU.subtract
                                    ).then_inc(rg["z"], 1)

            for s in range(2):
                values(f, s, s)
            for s in range(2):
                gate(f, s, s)
            with dve.Fori(0, NRB // 2 - 1) as i:
                own.enter(i, 2 * (2 + 4) + 4 + 2 * (2 * 2 + 2))
                for s in range(2):
                    rates(2 * i + s, s)
                    values(4 * i + (f + 4), 2 * i + (2 + s), s)
                recurrences(2 * i)
                for s in range(2):
                    gate(4 * i + (f + 4), 2 * i + (2 + s), s)
                rests(2 * i)
            own.leave(NRB // 2 - 1)
            for s in range(2):
                rates(NRB - 2 + s, s)
            recurrences(NRB - 2)
            rests(NRB - 2)
            add_to_x(7, NBLOCKS, 1.0)
            norm(6, "out", "final_norm_2")


MIX_ORDER = [12, 13, 4, 5, 6, 7, 0, 1, 2, 3, 8, 9, 10, 11]


def weight_stream(w):
    import numpy as np

    def by_output(m, cols):
        k = m.shape[0] // 128
        return m[:, cols].reshape(k, 128, -1, 128).transpose(2, 1, 0, 3)

    def by_input(m):
        return m.reshape(m.shape[0] // 128, 128, 8, 128)

    def turns(*parts):
        return np.stack(parts, 1).reshape(-1, 128, 8, 128)

    head_order = [(n % 2) * 4 + n // 2 for n in range(8)]
    c = slice
    w_in = w["w_in"][0]
    conv, rwkv = 3 * 512, 3 * 512 + 1792
    even = w["even_w_in_2"][0]
    odd = w["odd_w_in_2"][0]
    oa, ob = by_output(w["w_out_a"][0], c(None)), by_output(w["w_out_b"][0], c(None))
    out_ab = np.concatenate([oa, ob], axis=2)
    v = even[:, 3328:3584].reshape(2, 4, 128, 256).transpose(0, 2, 1, 3).reshape(2, 128, 8, 128)
    parts = [
        turns(by_output(w["ffn1_w_gate"][0], c(None)), by_output(w["ffn1_w_up"][0], c(None))),
        by_input(w["ffn1_w_down"][0]),
        by_output(w_in, c(conv, rwkv))[MIX_ORDER],
        turns(by_output(w_in, c(512, 1024)), by_output(w_in, c(1024, 1536)), by_output(w_in, c(0, 512))),
        turns(by_output(w_in, c(rwkv, rwkv + 1024)), by_output(w_in, c(rwkv + 1024, rwkv + 2048))),
        out_ab,
        by_input(w["w_o"][0]),
        turns(by_output(w["ffn2_w_gate"][0], c(None)), by_output(w["ffn2_w_up"][0], c(None))),
        by_input(w["ffn2_w_down"][0]),
        turns(by_output(even, c(0, 1024)), by_output(even, c(1024, 2048))),
        by_input(w["even_w_out_2"][0])[:8],
        by_output(even, c(3072, 3328)),
        by_output(even, c(2048, 3072))[head_order],
        v,
        by_output(even, c(3584, 4608))[head_order],
        by_input(w["even_w_out_2"][0])[8:][head_order],
        np.stack([by_output(odd, c(k * 2048, (k + 1) * 2048)).reshape(8, 2, 128, 8, 128) for k in range(2)], 1),
        by_input(w["odd_w_out_2"][0]),
    ]
    return np.ascontiguousarray(np.concatenate([p.reshape(-1, 128, 1024) for p in parts]))


def constants():
    import numpy as np

    f = np.float32
    bones = np.kron(np.eye(2), np.ones((64, 64)))
    perm = np.zeros((128, 128))
    for half in (0, 64):
        for i in range(32):
            perm[half + i + 32, half + i] = -1.0
            perm[half + i, half + i + 32] = 1.0
    spread = np.zeros((4, 32, 128))
    spread[:, 0, :64] = 1.0
    spread[:, 16, 64:] = 1.0
    mats = np.stack([np.ones((128, 128)), bones, np.eye(128), perm, spread.reshape(128, 128)], 1).astype(f)
    r, q = np.arange(128)[:, None], np.arange(128)[None, :]
    levels = []
    for l in range(7):
        low = (r // (2 << l) == q // (2 << l)) & (r // (1 << l) > q // (1 << l))
        levels += [low, low.T]
    tri = [r < q, r <= q, r < q, r <= q]
    masks = np.stack(levels + tri, 1).reshape(128, -1).astype(np.int32)
    inv = (f(10000.0) ** (-np.arange(0, 64, 2, dtype=f) / f(64))).astype(f)
    t = np.arange(512)
    ang = np.stack([(t // 64).astype(f)[:, None] * inv, (t % 64).astype(f)[:, None] * inv])
    full = np.concatenate([ang[0].T, ang[0].T, ang[1].T, ang[1].T])
    rope = np.stack([np.cos(full.astype(np.float64)), np.sin(full.astype(np.float64))], 1).astype(f)
    ch = 2 * np.pi * np.outer(np.arange(256), np.arange(256)) / 256
    sq = 2 * np.pi * np.outer(np.arange(512), np.arange(512)) / 512
    dft_c = np.concatenate([np.cos(ch[:, :128]), -np.sin(ch[:, :128]), np.cos(ch[:, 128:129])], 1) / 16.0
    dft_s = np.concatenate([np.cos(sq), np.sin(sq)], 0) / np.sqrt(512.0)
    dft_c = dft_c.reshape(2, 128, 257).transpose(1, 0, 2).astype(f)
    dft_s = dft_s.reshape(8, 128, 512).transpose(1, 0, 2).astype(f)
    return mats, masks, rope, dft_c, dft_s


def kernel(**inputs):
    import numpy as np
    import concourse.bacc as bacc
    from concourse.bass_utils import run_bass_kernel_spmd

    w = {k: np.asarray(v) for k, v in inputs.items()}
    par = np.zeros((NCOLS, 128), np.float32)
    for name, at in COLS.items():
        if name in w:
            v = w[name].reshape(-1, 128)
            par[at:at + v.shape[0]] = v[MIX_ORDER] if name == "mu_b" else v
    par[COLS["eps_rms"]], par[COLS["eps_gn"]] = EPS_RMS, EPS_GN
    mats, masks, rope, dft_c, dft_s = constants()
    gates = np.stack([w["gate_a_w_2"][0, 0], w["gate_x_w_2"][0, 0], w["gate_a_w_2"][0, 1], w["gate_x_w_2"][0, 1]])
    gates = gates.transpose(1, 2, 0, 3)
    gates = np.concatenate([gates, gates[:2]])
    f4 = w["fourier_w_2"][0]
    mirror = np.zeros((4, 128, 256), np.float32)
    mirror[:, 1:] = f4[:, :128:-1]
    fw = np.stack([f4[:, :128], mirror], 1).reshape(4, 2, 128, 2, 128).transpose(2, 0, 1, 3, 4).reshape(128, 16, 128)
    fw_mid = np.zeros((4, 4, 256), np.float32)
    for g in range(4):
        fw_mid[g, g] = f4[g, 128]
    fw_mid = fw_mid.reshape(4, 8, 128)
    arrays = {
        "xT": w["x"][0].T.reshape(8, 128, 512).transpose(1, 0, 2),
        "wstream": weight_stream(w),
        "params": par.T,
        "mats": mats,
        "masks": masks,
        "lora": np.concatenate([w["w_decay_up"][0], w["w_iclr_up"][0]], 0),
        "gup": w["w_gate_up"][0],
        "rope": rope,
        "dft_c": dft_c,
        "dft_s": dft_s,
        "fw": fw,
        "fw_mid": fw_mid,
        "rgates": gates,
    }
    from concourse import mybir as mb
    nc = bacc.Bacc("TRN2", target_bir_lowering=False, num_devices=1)
    aps, feed = [], {}
    for name, a in arrays.items():
        feed[name] = np.ascontiguousarray(a)
        aps.append(nc.dram_tensor(name, a.shape, mb.dt.from_np(a.dtype), kind="ExternalInput").ap())
    aps.append(nc.dram_tensor("outT", (128, 8, 512), mb.dt.float32, kind="ExternalOutput").ap())
    gate_store = nc.dram_tensor("gate_store", (N_GATES, 128, 512), mb.dt.float32, kind="Internal").ap()
    program(nc, gate_store, *aps)
    got = run_bass_kernel_spmd(nc, [feed], core_ids=[0]).results[0]["outT"]
    return np.ascontiguousarray(got.transpose(1, 0, 2).reshape(1024, 512).T).reshape(1, 512, 1024)
```
